# Optimizing a Trainium2 kernel written in Bass

```python
import jax, jax.numpy as jnp
from jax import lax
import numpy as np
import math

D_MODEL = 1024
BATCH = 1
SEQ = 256
DEPTH = 2

MIX_WIDTH = D_MODEL
POOL_WIDTH = MIX_WIDTH // 2
POOL_WINDOWS = (2, 4, 8, 16)
N_POOL_GROUPS = len(POOL_WINDOWS)
POOL_GROUP = POOL_WIDTH // N_POOL_GROUPS
ATTN_WIDTH = MIX_WIDTH - POOL_WIDTH
HEAD_DIM = 64
N_HEADS = ATTN_WIDTH // HEAD_DIM
N_KV_HEADS = 2
GQA_GROUP = N_HEADS // N_KV_HEADS
WINDOW = 128
BLOCK = 128
Q_OFF = POOL_WIDTH
K_OFF = Q_OFF + N_HEADS * HEAD_DIM
V_OFF = K_OFF + N_KV_HEADS * HEAD_DIM
IN_WIDTH = V_OFF + N_KV_HEADS * HEAD_DIM

N_KEYS = 128
N_EXPERTS = N_KEYS * N_KEYS
PEER_HEADS = 8
PEER_TOPK = 16
D_KEY = 256
D_HALF = D_KEY // 2
PEER_CHUNK = 128

RMS_EPS = 1e-6
N_MOD = 6


def rms_norm(x, g):
    xf = x.astype(jnp.float32)
    y = xf * lax.rsqrt(jnp.mean(xf * xf, axis=-1, keepdims=True) + RMS_EPS)
    return (y * g.astype(jnp.float32)).astype(x.dtype)

def alibi_slopes(n_heads):
    return jnp.exp2(-8.0 * jnp.arange(1, n_heads + 1, dtype=jnp.float32) / n_heads)

def multiscale_pool(p, pool_w, pool_scale):
    B, S, _ = p.shape
    pg = p.reshape(B, S, N_POOL_GROUPS, POOL_GROUP)
    cs = jnp.cumsum(pg.astype(jnp.float32), axis=1)
    pos1 = jnp.arange(1, S + 1, dtype=jnp.float32)
    means = []
    for g, w in enumerate(POOL_WINDOWS):
        cg = cs[:, :, g]
        lag = jnp.pad(cg, ((0, 0), (w, 0), (0, 0)))[:, :S]
        means.append((cg - lag) / jnp.minimum(pos1, float(w))[None, :, None])
    pooled = jnp.stack(means, axis=2).astype(p.dtype) - pg
    mixed = jnp.einsum('bsgc,gcd->bsgd', pooled, pool_w)
    return mixed.reshape(B, S, POOL_WIDTH) * pool_scale

def band_blocks(t, nb):
    B = t.shape[0]
    tb = t.reshape(B, nb, BLOCK, N_KV_HEADS, HEAD_DIM)
    prev = jnp.pad(tb, ((0, 0), (1, 0), (0, 0), (0, 0), (0, 0)))[:, :nb]
    return jnp.concatenate([prev, tb], axis=2)

def sliding_window_attention(q, k, v, sinks):
    B, S = q.shape[:2]
    nb = S // BLOCK
    qb = q.reshape(B, nb, BLOCK, N_KV_HEADS, GQA_GROUP, HEAD_DIM)
    kb = band_blocks(k, nb)
    vb = band_blocks(v, nb)
    scores = jnp.einsum('bnqkgd,bnskd->bnkgqs', qb, kb,
                        preferred_element_type=jnp.float32) * (HEAD_DIM ** -0.5)
    qi = jnp.arange(BLOCK)[:, None]
    sj = jnp.arange(2 * BLOCK)[None, :]
    dist = qi + BLOCK - sj
    band_ok = (dist >= 0) & (dist < WINDOW)
    blk = jnp.arange(nb)[:, None, None]
    valid = band_ok[None] & ((blk > 0) | (sj[None] >= BLOCK))
    slopes = alibi_slopes(N_HEADS).reshape(N_KV_HEADS, GQA_GROUP)
    bias = -slopes[:, :, None, None] * dist.astype(jnp.float32)
    scores = jnp.where(valid[None, :, None, None], scores + bias[None, None], -jnp.inf)
    sink = sinks.astype(jnp.float32).reshape(N_KV_HEADS, GQA_GROUP)[None, None, :, :, None, None]
    sink = jnp.broadcast_to(sink, scores.shape[:-1] + (1,))
    probs = jax.nn.softmax(jnp.concatenate([scores, sink], axis=-1), axis=-1)[..., :-1]
    out = jnp.einsum('bnkgqs,bnskd->bnqkgd', probs.astype(v.dtype), vb)
    return out.reshape(B, S, N_HEADS * HEAD_DIM)

def peer_ffn(h, wq, subkeys, u, v):
    B, S, D = h.shape
    T = B * S
    hf = h.reshape(T, D)
    q = (hf @ wq).reshape(T, PEER_HEADS, 2, D_HALF)
    s = jnp.einsum('thpd,pnd->thpn', q, subkeys, preferred_element_type=jnp.float32)
    top_s, top_i = lax.top_k(s, PEER_TOPK)
    cand = top_s[:, :, 0, :, None] + top_s[:, :, 1, None, :]
    best_s, best_j = lax.top_k(cand.reshape(T, PEER_HEADS, PEER_TOPK * PEER_TOPK), PEER_TOPK)
    i1 = jnp.take_along_axis(top_i[:, :, 0], best_j // PEER_TOPK, axis=-1)
    i2 = jnp.take_along_axis(top_i[:, :, 1], best_j % PEER_TOPK, axis=-1)
    expert = (i1 * N_KEYS + i2).reshape(T, PEER_HEADS * PEER_TOPK)
    gate = jax.nn.softmax(best_s, axis=-1).reshape(T, PEER_HEADS * PEER_TOPK).astype(h.dtype)
    nc = T // PEER_CHUNK

    def expert_block(args):
        hc, ec, gc = args
        uc = jnp.take(u, ec, axis=0)
        a = jnp.einsum('cd,ced->ce', hc, uc)
        act = jax.nn.gelu(a, approximate=False) * gc
        vc = jnp.take(v, ec, axis=0)
        return jnp.einsum('ce,ced->cd', act, vc)

    out = lax.map(expert_block, (hf.reshape(nc, PEER_CHUNK, D),
                                 expert.reshape(nc, PEER_CHUNK, -1),
                                 gate.reshape(nc, PEER_CHUNK, -1)))
    return out.reshape(B, S, D)

def first_inputs(seed: int = 0) -> dict:
    key = jax.random.key(seed)
    ks = jax.random.split(key, 20)
    f32 = jnp.float32
    nrm = lambda k, shape, s: jax.random.normal(k, shape, f32) * s
    return {
        "x": nrm(ks[0], (BATCH, SEQ, D_MODEL), 1.0),
        "c": nrm(ks[1], (BATCH, D_MODEL), 1.0),
        "w_ada": nrm(ks[2], (DEPTH, D_MODEL, N_MOD * D_MODEL), 0.5 * D_MODEL ** -0.5),
        "b_ada": nrm(ks[3], (DEPTH, N_MOD * D_MODEL), 0.02),
        "norm1_g": 1.0 + nrm(ks[4], (DEPTH, D_MODEL), 0.05),
        "norm2_g": 1.0 + nrm(ks[5], (DEPTH, D_MODEL), 0.05),
        "w_in": nrm(ks[6], (DEPTH, D_MODEL, IN_WIDTH), D_MODEL ** -0.5),
        "pool_w": nrm(ks[7], (DEPTH, N_POOL_GROUPS, POOL_GROUP, POOL_GROUP), POOL_GROUP ** -0.5),
        "pool_scale": 1.0 + nrm(ks[8], (DEPTH, POOL_WIDTH), 0.1),
        "q_norm_g": 1.0 + nrm(ks[9], (DEPTH, HEAD_DIM), 0.05),
        "k_norm_g": 1.0 + nrm(ks[10], (DEPTH, HEAD_DIM), 0.05),
        "attn_sinks": nrm(ks[11], (DEPTH, N_HEADS), 0.5),
        "mix_norm_g": 1.0 + nrm(ks[12], (DEPTH, MIX_WIDTH), 0.05),
        "w_out": nrm(ks[13], (DEPTH, MIX_WIDTH, D_MODEL), MIX_WIDTH ** -0.5),
        "peer_wq": nrm(ks[14], (DEPTH, D_MODEL, PEER_HEADS * D_KEY), D_MODEL ** -0.5),
        "peer_subkeys": nrm(ks[15], (DEPTH, 2, N_KEYS, D_HALF), D_HALF ** -0.5),
        "peer_u": nrm(ks[16], (DEPTH, N_EXPERTS, D_MODEL), D_MODEL ** -0.5),
        "peer_v": nrm(ks[17], (DEPTH, N_EXPERTS, D_MODEL), PEER_HEADS ** -0.5),
    }

def first_block(x, c, w_ada, b_ada, norm1_g, norm2_g, w_in, pool_w, pool_scale, q_norm_g,
              k_norm_g, attn_sinks, mix_norm_g, w_out, peer_wq, peer_subkeys, peer_u, peer_v):
    B, S, D = x.shape
    cond = jax.nn.silu(c)
    for l in range(DEPTH):
        mod = (cond @ w_ada[l] + b_ada[l])[:, None, :]
        sh1, sc1, g1, sh2, sc2, g2 = jnp.split(mod, N_MOD, axis=-1)

        h = rms_norm(x, norm1_g[l]) * (1.0 + sc1) + sh1
        proj = h @ w_in[l]
        p = proj[..., :Q_OFF]
        q = proj[..., Q_OFF:K_OFF].reshape(B, S, N_HEADS, HEAD_DIM)
        k = proj[..., K_OFF:V_OFF].reshape(B, S, N_KV_HEADS, HEAD_DIM)
        v = proj[..., V_OFF:].reshape(B, S, N_KV_HEADS, HEAD_DIM)
        q = rms_norm(q, q_norm_g[l])
        k = rms_norm(k, k_norm_g[l])
        pool_out = multiscale_pool(p, pool_w[l], pool_scale[l])
        attn_out = sliding_window_attention(q, k, v, attn_sinks[l])
        y = jnp.concatenate([pool_out, attn_out], axis=-1).reshape(B, S, 2, MIX_WIDTH // 2)
        y = rms_norm(y, jnp.ones((MIX_WIDTH // 2,), jnp.float32)).reshape(B, S, MIX_WIDTH) * mix_norm_g[l]
        x = x + g1 * (y @ w_out[l])

        h2 = rms_norm(x, norm2_g[l]) * (1.0 + sc2) + sh2
        x = x + g2 * peer_ffn(h2, peer_wq[l], peer_subkeys[l], peer_u[l], peer_v[l])
    return x


GRID_W = 64
ROPE_THETA = 10000.0
EPS = 1e-6
NEG_INF = -1e30
Q_BLOCK = 128

MLA_HEADS = 4
MLA_Q_RANK = 192
MLA_KV_RANK = 128
MLA_NOPE_DIM = 64
MLA_ROPE_DIM = 32
MLA_V_DIM = 64
DIFF_HEADS = 4
DIFF_QK_DIM = 32
DIFF_V_DIM = 64
SWA_Q_HEADS = 4
SWA_KV_HEADS = 2
SWA_GROUP = SWA_Q_HEADS // SWA_KV_HEADS
SWA_HEAD_DIM = 64
SWA_BLOCK = 128
NA_HEADS = 4
NA_HEAD_DIM = 64
NA_ROWS_MAX = 8
NA_COLS = 16
D_FF = 4 * D_MODEL

A_OUT = MLA_HEADS * MLA_V_DIM
B_OUT = DIFF_HEADS * DIFF_V_DIM
C_OUT = SWA_Q_HEADS * SWA_HEAD_DIM
D_OUT = NA_HEADS * NA_HEAD_DIM
MIX_WIDTH_2 = A_OUT + B_OUT + C_OUT + D_OUT

IN_SPLIT_WIDTHS = (
    MLA_Q_RANK, MLA_KV_RANK, MLA_ROPE_DIM,
    DIFF_HEADS * 2 * DIFF_QK_DIM, DIFF_HEADS * 2 * DIFF_QK_DIM, B_OUT,
    SWA_Q_HEADS * SWA_HEAD_DIM, SWA_KV_HEADS * SWA_HEAD_DIM, SWA_KV_HEADS * SWA_HEAD_DIM,
    NA_HEADS * NA_HEAD_DIM, NA_HEADS * NA_HEAD_DIM, NA_HEADS * NA_HEAD_DIM,
)
IN_COLS = sum(IN_SPLIT_WIDTHS)


def _split_points():
    pts, acc = [], 0
    for w in IN_SPLIT_WIDTHS[:-1]:
        acc += w
        pts.append(acc)
    return pts

def rms_norm_2(x, g):
    xf = x.astype(jnp.float32)
    y = xf * lax.rsqrt(jnp.mean(xf * xf, axis=-1, keepdims=True) + EPS)
    return (y * g.astype(jnp.float32)).astype(x.dtype)

def rope_table(seq_len, dim):
    inv = 1.0 / (ROPE_THETA ** (jnp.arange(0, dim, 2, dtype=jnp.float32) / dim))
    ang = jnp.arange(seq_len, dtype=jnp.float32)[:, None] * inv[None, :]
    return jnp.cos(ang), jnp.sin(ang)

def apply_rope(x, cos, sin):
    shp = (1, x.shape[1]) + (1,) * (x.ndim - 3) + (cos.shape[-1],)
    c, s = cos.reshape(shp), sin.reshape(shp)
    xf = x.astype(jnp.float32)
    half = x.shape[-1] // 2
    x1, x2 = xf[..., :half], xf[..., half:]
    return jnp.concatenate([x1 * c - x2 * s, x2 * c + x1 * s], axis=-1).astype(x.dtype)

def dense_block_attention(q, k, v, scale):
    B, S, H, dq = q.shape
    nb = S // Q_BLOCK
    qb = jnp.moveaxis(q.reshape(B, nb, Q_BLOCK, H, dq), 1, 0)

    def one_block(qi):
        s = jnp.einsum('bqhd,bkhd->bhqk', qi, k, preferred_element_type=jnp.float32) * scale
        p = jax.nn.softmax(s, axis=-1)
        return jnp.einsum('bhqk,bkhd->bqhd', p.astype(v.dtype), v)

    o = lax.map(one_block, qb)
    return jnp.moveaxis(o, 0, 1).reshape(B, S, H, v.shape[-1])

def mla_mixer(cq, ckv, kr, q_norm_g, w_uq, kv_norm_g, w_uk, w_uv, cos, sin):
    B, S, _ = cq.shape
    q = (rms_norm_2(cq, q_norm_g) @ w_uq).reshape(B, S, MLA_HEADS, MLA_NOPE_DIM + MLA_ROPE_DIM)
    q = jnp.concatenate([q[..., :MLA_NOPE_DIM], apply_rope(q[..., MLA_NOPE_DIM:], cos, sin)], axis=-1)
    c = rms_norm_2(ckv, kv_norm_g)
    k_nope = (c @ w_uk).reshape(B, S, MLA_HEADS, MLA_NOPE_DIM)
    v = (c @ w_uv).reshape(B, S, MLA_HEADS, MLA_V_DIM)
    k_pe = apply_rope(kr[:, :, None, :], cos, sin)
    k = jnp.concatenate([k_nope, jnp.broadcast_to(k_pe, (B, S, MLA_HEADS, MLA_ROPE_DIM))], axis=-1)
    o = dense_block_attention(q, k, v, (MLA_NOPE_DIM + MLA_ROPE_DIM) ** -0.5)
    return o.reshape(B, S, A_OUT)

def diff_mixer(q, k, v, lq1, lk1, lq2, lk2, subln_g, lambda_init, cos, sin):
    B, S, _ = q.shape
    q = apply_rope(q.reshape(B, S, DIFF_HEADS, 2, DIFF_QK_DIM), cos, sin)
    k = apply_rope(k.reshape(B, S, DIFF_HEADS, 2, DIFF_QK_DIM), cos, sin)
    v = v.reshape(B, S, DIFF_HEADS, DIFF_V_DIM)
    f32 = jnp.float32
    lam = (jnp.exp(jnp.sum(lq1.astype(f32) * lk1.astype(f32)))
           - jnp.exp(jnp.sum(lq2.astype(f32) * lk2.astype(f32))) + lambda_init)
    scale = DIFF_QK_DIM ** -0.5
    nb = S // Q_BLOCK
    qb = jnp.moveaxis(q.reshape(B, nb, Q_BLOCK, DIFF_HEADS, 2, DIFF_QK_DIM), 1, 0)

    def one_block(qi):
        s = jnp.einsum('bqhcd,bkhcd->bhcqk', qi, k, preferred_element_type=f32) * scale
        p = jax.nn.softmax(s, axis=-1)
        w = p[:, :, 0] - lam * p[:, :, 1]
        return jnp.einsum('bhqk,bkhd->bqhd', w.astype(v.dtype), v)

    o = jnp.moveaxis(lax.map(one_block, qb), 0, 1).reshape(B, S, DIFF_HEADS, DIFF_V_DIM)
    o = rms_norm_2(o, subln_g) * (1.0 - lambda_init)
    return o.reshape(B, S, B_OUT)

def swa_mixer(q, k, v, sinks, cos, sin):
    B, S, _ = q.shape
    q = apply_rope(q.reshape(B, S, SWA_KV_HEADS, SWA_GROUP, SWA_HEAD_DIM), cos, sin)
    k = apply_rope(k.reshape(B, S, SWA_KV_HEADS, SWA_HEAD_DIM), cos, sin)
    v = v.reshape(B, S, SWA_KV_HEADS, SWA_HEAD_DIM)
    nb = S // SWA_BLOCK
    qb = q.reshape(B, nb, SWA_BLOCK, SWA_KV_HEADS, SWA_GROUP, SWA_HEAD_DIM)

    def band(t):
        tp = jnp.pad(t, ((0, 0), (SWA_BLOCK, SWA_BLOCK), (0, 0), (0, 0)))
        tp = tp.reshape(B, nb + 2, SWA_BLOCK, SWA_KV_HEADS, SWA_HEAD_DIM)
        return jnp.concatenate([tp[:, :-2], tp[:, 1:-1], tp[:, 2:]], axis=2)

    kb, vb = band(k), band(v)
    s = jnp.einsum('bnqkgd,bnjkd->bnkgqj', qb, kb,
                   preferred_element_type=jnp.float32) * (SWA_HEAD_DIM ** -0.5)
    qi = jnp.arange(SWA_BLOCK)[:, None]
    kj = jnp.arange(3 * SWA_BLOCK)[None, :]
    rel = kj - SWA_BLOCK - qi
    kabs = jnp.arange(nb)[:, None] * SWA_BLOCK - SWA_BLOCK + jnp.arange(3 * SWA_BLOCK)[None, :]
    valid = (jnp.abs(rel) <= WINDOW)[None] & ((kabs >= 0) & (kabs < S))[:, None, :]
    s = jnp.where(valid[None, :, None, None], s, NEG_INF)
    sink = jnp.broadcast_to(sinks.astype(jnp.float32).reshape(1, 1, SWA_KV_HEADS, SWA_GROUP, 1, 1),
                            s.shape[:-1] + (1,))
    p = jax.nn.softmax(jnp.concatenate([s, sink], axis=-1), axis=-1)[..., :-1]
    o = jnp.einsum('bnkgqj,bnjkd->bnqkgd', p.astype(v.dtype), vb)
    return o.reshape(B, S, C_OUT)

def na_mixer(q, k, v, rpb):
    B, S, _ = q.shape
    rows = S // GRID_W
    kh = min(NA_ROWS_MAX, rows)
    shp = (B, rows, GRID_W, NA_HEADS, NA_HEAD_DIM)
    q, k, v = q.reshape(shp), k.reshape(shp), v.reshape(shp)
    row_start = jnp.clip(jnp.arange(rows) - kh // 2, 0, rows - kh)
    col = np.arange(GRID_W)
    col_start = np.clip(col - NA_COLS // 2, 0, GRID_W - NA_COLS)
    col_idx = col_start[:, None] + np.arange(NA_COLS)[None, :]
    col_off = col_idx - col[:, None]
    rpb_cols = rpb[:, :, col_off + NA_COLS - 1]
    scale = NA_HEAD_DIM ** -0.5

    def one_row(args):
        q_r, start, r = args
        k_r = lax.dynamic_slice_in_dim(k, start, kh, axis=1)[:, :, col_idx]
        v_r = lax.dynamic_slice_in_dim(v, start, kh, axis=1)[:, :, col_idx]
        bias = jnp.take(rpb_cols, start + jnp.arange(kh) - r + NA_ROWS_MAX - 1, axis=1)
        s = jnp.einsum('bwhd,bawchd->bhwac', q_r, k_r, preferred_element_type=jnp.float32) * scale
        s = s + jnp.transpose(bias, (0, 2, 1, 3)).astype(jnp.float32)[None]
        p = jax.nn.softmax(s.reshape(B, NA_HEADS, GRID_W, kh * NA_COLS), axis=-1).reshape(s.shape)
        return jnp.einsum('bhwac,bawchd->bwhd', p.astype(v.dtype), v_r)

    o = lax.map(one_row, (jnp.moveaxis(q, 1, 0), row_start, jnp.arange(rows)))
    return jnp.moveaxis(o, 0, 1).reshape(B, S, D_OUT)

def second_inputs(seed: int = 0) -> dict:
    key = jax.random.key(seed)
    ks = jax.random.split(key, 24)
    f32 = jnp.float32
    L = DEPTH

    def nrm(k, shape, scale):
        return jax.random.normal(k, shape, f32) * scale

    def gain(k, shape):
        return 1.0 + 0.05 * jax.random.normal(k, shape, f32)

    return {
        'x': nrm(ks[0], (BATCH, SEQ, D_MODEL), 1.0),
        'norm1_g': gain(ks[1], (L, D_MODEL)),
        'w_in': nrm(ks[2], (L, D_MODEL, IN_COLS), D_MODEL ** -0.5),
        'mla_q_norm_g': gain(ks[3], (L, MLA_Q_RANK)),
        'mla_w_uq': nrm(ks[4], (L, MLA_Q_RANK, MLA_HEADS * (MLA_NOPE_DIM + MLA_ROPE_DIM)), MLA_Q_RANK ** -0.5),
        'mla_kv_norm_g': gain(ks[5], (L, MLA_KV_RANK)),
        'mla_w_uk': nrm(ks[6], (L, MLA_KV_RANK, MLA_HEADS * MLA_NOPE_DIM), MLA_KV_RANK ** -0.5),
        'mla_w_uv': nrm(ks[7], (L, MLA_KV_RANK, MLA_HEADS * MLA_V_DIM), MLA_KV_RANK ** -0.5),
        'diff_lambda_q1': nrm(ks[8], (L, DIFF_QK_DIM), 0.1),
        'diff_lambda_k1': nrm(ks[9], (L, DIFF_QK_DIM), 0.1),
        'diff_lambda_q2': nrm(ks[10], (L, DIFF_QK_DIM), 0.1),
        'diff_lambda_k2': nrm(ks[11], (L, DIFF_QK_DIM), 0.1),
        'diff_subln_g': gain(ks[12], (L, DIFF_V_DIM)),
        'swa_sinks': nrm(ks[13], (L, SWA_Q_HEADS), 0.5),
        'na_rpb': nrm(ks[14], (L, NA_HEADS, 2 * NA_ROWS_MAX - 1, 2 * NA_COLS - 1), 0.1),
        'out_g_mla': gain(ks[15], (L, A_OUT)),
        'out_g_swa': gain(ks[16], (L, C_OUT)),
        'out_g_na': gain(ks[17], (L, D_OUT)),
        'w_out': nrm(ks[18], (L, MIX_WIDTH_2, D_MODEL), MIX_WIDTH_2 ** -0.5),
        'norm2_g': gain(ks[19], (L, D_MODEL)),
        'w_up': nrm(ks[20], (L, D_MODEL, D_FF), D_MODEL ** -0.5),
        'w_down': nrm(ks[21], (L, D_FF, D_MODEL), D_FF ** -0.5),
        'final_norm_g': gain(ks[22], (D_MODEL,)),
    }

def second_block(x, norm1_g, w_in, mla_q_norm_g, mla_w_uq, mla_kv_norm_g, mla_w_uk, mla_w_uv,
              diff_lambda_q1, diff_lambda_k1, diff_lambda_q2, diff_lambda_k2, diff_subln_g,
              swa_sinks, na_rpb, out_g_mla, out_g_swa, out_g_na, w_out, norm2_g, w_up, w_down,
              final_norm_g):
    S = x.shape[1]
    cos32, sin32 = rope_table(S, MLA_ROPE_DIM)
    cos64, sin64 = rope_table(S, SWA_HEAD_DIM)
    splits = _split_points()
    for l in range(DEPTH):
        h = rms_norm_2(x, norm1_g[l])
        proj = h @ w_in[l]
        (a_cq, a_ckv, a_kr, b_q, b_k, b_v, c_q, c_k, c_v, d_q, d_k, d_v) = jnp.split(proj, splits, axis=-1)
        y_a = mla_mixer(a_cq, a_ckv, a_kr, mla_q_norm_g[l], mla_w_uq[l], mla_kv_norm_g[l],
                        mla_w_uk[l], mla_w_uv[l], cos32, sin32)
        lambda_init = 0.8 - 0.6 * math.exp(-0.3 * l)
        y_b = diff_mixer(b_q, b_k, b_v, diff_lambda_q1[l], diff_lambda_k1[l], diff_lambda_q2[l],
                         diff_lambda_k2[l], diff_subln_g[l], lambda_init, cos32, sin32)
        y_c = swa_mixer(c_q, c_k, c_v, swa_sinks[l], cos64, sin64)
        y_d = na_mixer(d_q, d_k, d_v, na_rpb[l])
        mix = jnp.concatenate([rms_norm_2(y_a, out_g_mla[l]), y_b,
                               rms_norm_2(y_c, out_g_swa[l]), rms_norm_2(y_d, out_g_na[l])], axis=-1)
        x = x + mix @ w_out[l]
        h = rms_norm_2(x, norm2_g[l])
        x = x + jnp.square(jax.nn.relu(h @ w_up[l])) @ w_down[l]
    return rms_norm_2(x, final_norm_g)


def setup_inputs(seed=0):
    out = dict(first_inputs(seed))
    for name, value in second_inputs(seed + 1).items():
        if name != "x":
            out[name + "_2"] = value
    return out


def reference(
    x, c, w_ada, b_ada, norm1_g, norm2_g, w_in, pool_w, pool_scale, q_norm_g, k_norm_g,
    attn_sinks, mix_norm_g, w_out, peer_wq, peer_subkeys, peer_u, peer_v, norm1_g_2, w_in_2,
    mla_q_norm_g_2, mla_w_uq_2, mla_kv_norm_g_2, mla_w_uk_2, mla_w_uv_2, diff_lambda_q1_2,
    diff_lambda_k1_2, diff_lambda_q2_2, diff_lambda_k2_2, diff_subln_g_2, swa_sinks_2, na_rpb_2,
    out_g_mla_2, out_g_swa_2, out_g_na_2, w_out_2, norm2_g_2, w_up_2, w_down_2, final_norm_g_2,
):
    x = first_block(
        x, c, w_ada, b_ada, norm1_g, norm2_g, w_in, pool_w, pool_scale, q_norm_g, k_norm_g,
        attn_sinks, mix_norm_g, w_out, peer_wq, peer_subkeys, peer_u, peer_v,
    )
    return second_block(
        x, norm1_g_2, w_in_2, mla_q_norm_g_2, mla_w_uq_2, mla_kv_norm_g_2, mla_w_uk_2,
        mla_w_uv_2, diff_lambda_q1_2, diff_lambda_k1_2, diff_lambda_q2_2, diff_lambda_k2_2,
        diff_subln_g_2, swa_sinks_2, na_rpb_2, out_g_mla_2, out_g_swa_2, out_g_na_2, w_out_2,
        norm2_g_2, w_up_2, w_down_2, final_norm_g_2,
    )


_drawn_inputs = setup_inputs


def setup_inputs(seed=0):
    import zlib

    import numpy as np

    out = dict(_drawn_inputs(seed))
    spreads = {}
    factors = {'norm2_g': 3.08,
     'q_norm_g': 5.02,
     'k_norm_g': 4.904,
     'mla_q_norm_g_2': 6.429,
     'diff_lambda_q1_2': 3.85,
     'diff_lambda_k1_2': 4.184,
     'diff_lambda_q2_2': 5.688,
     'diff_lambda_k2_2': 8.0,
     'diff_subln_g_2': 2.725,
     'swa_sinks_2': 8.0,
     'attn_sinks': 5.49,
     'out_g_mla_2': 2.982}
    for name, (base, spread) in spreads.items():
        noise = np.random.default_rng([zlib.crc32(name.encode()), seed]).standard_normal(out[name].shape)
        drawn = base * np.exp(spread * noise) if base else spread * noise
        out[name] = __import__('jax').numpy.asarray(drawn.astype(out[name].dtype))
    for name, factor in factors.items():
        out[name] = (out[name] * factor).astype(out[name].dtype)
    return out
```

```python
import math
from contextlib import ExitStack

import numpy as np

import concourse.bass as bass
from concourse import mybir

F32 = mybir.dt.float32
I32 = mybir.dt.int32
U32 = mybir.dt.uint32
ALU = mybir.AluOpType
ACT = mybir.ActivationFunctionType
AX = mybir.AxisListType.X

L = 2
RING = 16
UNIT = 1024
PAR = 3720
TINY = -3.0e38
EPS = 1e-6

C_ID, C_ND, C_SM, C_ROPE, C_IOTA, C_END = 0, 128, 640, 1152, 1536, 1552
P1 = dict(n1=(0, 1024), n2=(1024, 1024), ps=(2048, 512), qg=(2560, 64), kg=(2624, 64), sink=(2688, 8), mg=(2696, 1024))
P2 = dict(n1=(0, 1024), n2=(1024, 1024), q=(2048, 192), kv=(2240, 128), lam=(2368, 128), sub=(2496, 64), sink=(2560, 4),
          oa=(2564, 256), oc=(2820, 256), od=(3076, 256))
X_CQ, X_CKV, X_KR, X_BQ, X_BV, X_SQ, X_SK, X_SV, X_NQ, X_NK, X_NV = 0, 192, 320, 352, 864, 1120, 1376, 1504, 1632, 1888, 2144


class Token:

    def __init__(self, sem, value=None):
        self.sem, self.value, self.used = sem, value, False


class Engine:

    def __init__(self, sem, chained=False):
        self.sem, self.items, self.chained, self.last = sem, [], chained, None

    def __call__(self, waits, fn):
        tok = Token(self.sem)
        self.items.append((flat([waits, self.last]), fn, tok, None))
        if self.chained:
            self.last = tok
        return tok

    def dma(self, waits, fn, sem, value):
        tok = Token(sem, value)
        self.items.append((flat(waits), fn, None, sem))
        return tok

    def number(self):
        n = 0
        for _, _, tok, _ in self.items:
            if tok is not None and tok.used:
                n += 1
                tok.value = n

    def emit(self, eng):
        seen = {}
        for waits, fn, tok, sem in self.items:
            for w in waits:
                if seen.get(id(w.sem), 0) < w.value:
                    seen[id(w.sem)] = w.value
                    eng.wait_ge(w.sem, w.value)
            ins = fn(eng)
            if sem is not None:
                ins.then_inc(sem, 16)
            elif tok is not None and tok.used:
                ins.then_inc(tok.sem, 1)


def flat(waits):
    out = []
    for w in waits:
        if isinstance(w, (list, tuple)):
            out += flat(w)
        elif w is not None:
            w.used = True
            out.append(w)
    return out


def bc(ap, shape):
    return ap.to_broadcast(shape)


def build(nc, I, out):
    with ExitStack() as ctx:
        def sb(name, n, dt=F32):
            return ctx.enter_context(nc.sbuf_tensor(name, [128, n], dt))

        def sem(name):
            return ctx.enter_context(nc.semaphore(name))

        X = sb("X", 2048)[:, :].rearrange("p (t d) -> p t d", t=2)
        MOD = sb("MOD", 6144)[:, :]
        PARB = sb("PARB", PAR)[:, :]
        HT = sb("HT", 2048)[:, :].rearrange("p (c s) -> p c s", c=8)
        H = sb("H", 2048)[:, :].rearrange("p (t d) -> p t d", t=2)
        PRJ = sb("PRJ", 2560)[:, :]
        GRP = sb("GRP", 4096)[:, :]
        QK = sb("QK", 6144)[:, :]
        CST = sb("CST", C_END)[:, :]
        JV = sb("JV", 1024)[:, :]
        ONES = sb("ONES", 128)[:, :]
        CREP = sb("CREP", 3 * 128)[:, :].rearrange("p (k m) -> p k m", k=3)
        ACC = sb("ACC", 1024)[:, :].rearrange("p (b n) -> p b n", b=2)
        DG = sb("DG", 4 * 128)[:, :].rearrange("p (b n) -> p b n", b=4)
        SC = sb("SC", 512)[:, :]
        GATE = sb("GATE", 256)[:, :]
        AV = sb("AV", 256)[:, :]
        AG = sb("AG", 256)[:, :]
        EID = sb("EID", 256, I32)[:, :]
        TV = sb("TV", 2 * 64)[:, :]
        TI = sb("TI", 2 * 64, U32)[:, :]
        TC = sb("TC", 256)[:, :]
        RNG = sb("RNG", RING * UNIT)[:, :]
        PS = ctx.enter_context(nc.psum_tensor("PS", [128, 8, 512], F32))

        pe, act, dve, pool, sp = (Engine(sem("s_" + n), n in ("act", "dve")) for n in ("pe", "act", "dve", "pool", "sp"))
        ld = [sem(f"ld{u}") for u in range(RING)]
        ga = [sem(f"ga{u}") for u in range(RING)]
        s_par, s_mod, s_x, s_out = sem("s_par"), sem("s_mod"), sem("s_x"), sem("s_out")

        ident = CST[:, C_ID:C_ID + 128]

        ring = dict(pos=0, free=[[] for _ in range(RING)], n={})

        class Item:
            def __init__(self, units):
                if ring["pos"] % RING + units > RING:
                    ring["pos"] += RING - ring["pos"] % RING
                self.u0, self.units = ring["pos"] % RING, units
                ring["pos"] += units
                self.waits = []
                for u in range(self.u0, self.u0 + units):
                    assert ring["free"][u] is not None
                    self.waits.append(ring["free"][u])
                    ring["free"][u] = None
                self.ap = RNG[:, self.u0 * UNIT:(self.u0 + units) * UNIT]

            def count(self, sem):
                ring["n"][id(sem)] = ring["n"].get(id(sem), 0) + 16
                return sem, ring["n"][id(sem)]

            def release(self, *toks):
                for u in range(self.u0, self.u0 + self.units):
                    ring["free"][u] = list(toks)

        def load(src, n):
            it = Item(-(-n // UNIT))
            dst = it.ap[:, 0:n]
            it.tok = sp.dma(it.waits, lambda e: e.dma_start(dst, src), *it.count(ld[it.u0]))
            it.ap = dst
            return it

        bank = dict(free=[[] for _ in range(8)], next=0, pair=0)

        def single():
            b = 4 + bank["next"] % 4
            bank["next"] += 1
            return b, bank["free"][b]

        turn = dict(n=0, sc=0)

        def evac(dst, src, waits, scale=1.0):
            turn["n"] += 1
            if turn["n"] % 2:
                return act(waits, lambda e: e.activation(dst, src, ACT.Copy, scale=scale))
            if scale == 1.0:
                return dve(waits, lambda e: e.tensor_copy(dst, src))
            return dve(waits, lambda e: e.tensor_scalar(dst, src, scale, None, ALU.mult))

        def scratch(n):
            if turn["sc"] % 512 + n > 512:
                turn["sc"] += 512 - turn["sc"] % 512
            c = turn["sc"] % 512
            turn["sc"] += n
            return SC[:, c:c + n]

        def tt(dst, a, b, op, waits):
            return dve(waits, lambda e: e.tensor_tensor(dst, a, b, op))

        def stt(dst, a, s, b, op0, op1, waits):
            return dve(waits, lambda e: e.scalar_tensor_tensor(out=dst, in0=a, scalar=s, in1=b, op0=op0, op1=op1))

        def ts(dst, a, s1, s2, op0, op1, waits):
            if op1 is None:
                return dve(waits, lambda e: e.tensor_scalar(dst, a, s1, None, op0))
            return dve(waits, lambda e: e.tensor_scalar(dst, a, s1, s2, op0, op1))

        def mm(dst, a, b, start, stop_, waits=()):
            return pe(waits, lambda e: e.matmul(dst, a, b, start=start, stop=stop_))

        t_cst = sp.dma([], lambda e: e.dma_start(CST, I["cst"]), s_x, 16)
        COND = scratch(24)
        t_c = sp.dma([t_cst], lambda e: e.dma_start(COND[:, 0:8], I["cT"]), s_x, 32)
        t_x = sp.dma([t_c], lambda e: e.dma_start(X, I["x"].rearrange("(t p) d -> p t d", p=128)), s_x, 48)
        EPSC = sb("EPSC", 1)[:, :]
        SKB = sb("SKB", 256)[:, :]
        s_sk = sem("s_sk")
        t_one = dve([], lambda e: e.memset(ONES, 1.0))
        t_eps = dve([], lambda e: e.memset(EPSC, EPS))
        k1 = act([t_c], lambda e: e.activation(COND[:, 8:16], COND[:, 0:8], ACT.Exp, scale=-1.0))
        k1 = ts(COND[:, 8:16], COND[:, 8:16], 1.0, None, ALU.add, None, [k1])
        k1 = dve([k1], lambda e: e.reciprocal(COND[:, 8:16], COND[:, 8:16]))
        t_cond = tt(COND[:, 16:24], COND[:, 0:8], COND[:, 8:16], ALU.mult, [k1])
        t_rep = None
        for k in range(3):
            src = COND[:, 21 + k:22 + k]
            dst = CREP[:, k, :]
            t_rep = dve([t_cond], lambda e, dst=dst, src=src: e.tensor_copy(dst, bc(src, [128, 128])))

        st = dict(x=[t_x, t_x], par=[], mod=[], ht=[], h=[[], []], prj=[], qa=[], qb=[], grp=[[], []], acc=[[], []],
                  npar=0, nmod=0, gi=0, dg=[[] for _ in range(4)], dn=0, tv=[[], []], tn=0)

        def load_par(src, n):
            st["npar"] += 16
            t = sp.dma(st["par"], lambda e: e.dma_start(PARB[:, 0:n], src.partition_broadcast(128)), s_par, st["npar"])
            st["par"] = []
            return t

        def ada(l):
            st["nmod"] += 16
            src = I["bada"][l]
            tb = sp.dma(st["mod"], lambda e: e.dma_start(MOD, src.partition_broadcast(128)), s_mod, st["nmod"])
            st["mod"] = []
            done = []
            for b in range(12):
                w = load(I["wada"][l * 12 + b], 4096)
                wv = w.ap.rearrange("p (k n) -> p k n", k=8)
                a = ACC[:, b % 2, :]
                t = ts(a, wv[:, 0, :], COND[:, 16:17], None, ALU.mult, None, [w.tok, t_cond, st["acc"][b % 2]])
                for k in range(1, 5):
                    t = stt(a, wv[:, k, :], COND[:, 16 + k:17 + k], a, ALU.mult, ALU.add, [t])
                bk, fr = single()
                for k in range(3):
                    mm(PS[:, bk, :], CREP[:, k, :], wv[:, 5 + k, :], k == 0, False, [w.tok, t_rep, fr])
                p = mm(PS[:, bk, :], ONES, a, False, True, [t, t_one])
                w.release(p, t)
                st["acc"][b % 2] = [p]
                m = MOD[:, b * 512:(b + 1) * 512]
                t = tt(m, PS[:, bk, :], m, ALU.add, [p, tb])
                bank["free"][bk] = [t]
                done = [t]
            return done

        def rstd(srcs, D, waits):
            n = len(srcs)
            s = scratch(n)
            last = []
            for i, a in enumerate(srcs):
                w = a.shape[-1]
                last = act([waits[i], st.get("jv", [])], lambda e, a=a, i=i, w=w: e.activation(
                    JV[:, 0:w], a, ACT.Square, accum_out=s[:, i:i + 1]))
                st["jv"] = []
            st["jva"] = [last]
            t = act([last, t_eps], lambda e: e.activation(s, s, ACT.Sqrt, bias=EPSC, scale=1.0 / D))
            t = dve([t], lambda e: e.reciprocal(s, s))
            return s, t

        def transpose_tm(src, dst, waits, free):
            out = []
            for t in range(2):
                for c4 in range(2):
                    bk, fr = single()
                    for c in range(4):
                        a = src[:, t, (c4 * 4 + c) * 128:(c4 * 4 + c + 1) * 128]
                        d = PS[:, bk, c * 128:(c + 1) * 128]
                        p = pe([waits[t], fr, t_cst], lambda e, a=a, d=d: e.transpose(d, a, ident))
                    v = evac(dst[:, c4 * 4:c4 * 4 + 4, t * 128:(t + 1) * 128],
                             PS[:, bk, :].rearrange("p (c s) -> p c s", c=4), [p, free])
                    bank["free"][bk] = [v]
                    out.append(v)
            return out, p

        def norm(g, b, waits):
            s, ts_ = rstd([X[:, 0, :], X[:, 1, :]], 1024.0, [st["x"][0], st["x"][1]])
            hs = []
            for t in range(2):
                k = stt(H[:, t, :], X[:, t, :], s[:, t:t + 1], g, ALU.mult, ALU.mult, [ts_, waits, st["h"][t]])
                if b is not None:
                    k = tt(H[:, t, :], H[:, t, :], b, ALU.add, [k])
                hs.append(k)
            toks, last = transpose_tm(H, HT, hs, st["ht"])
            st["ht"] = []
            st["h"] = [[last], [last]]
            return toks, hs

        def tokens_by(hT, w, width, t, k8, waits, fr, bk):
            wv = w.ap.rearrange("p (k n) -> p k n", k=k8)
            for k in range(k8):
                p = mm(PS[:, bk, 0:width], hT[:, k, t * 128:(t + 1) * 128], wv[:, k, :], k == 0, k == k8 - 1,
                       [w.tok, waits, fr])
            return p

        def residual(items, hT, waits, gate, gw):
            for j, w in enumerate(items):
                last = None
                for t in range(2):
                    bk, fr = single()
                    p = tokens_by(hT, w, 512, t, 8, waits, fr, bk)
                    xs = X[:, t, j * 512:(j + 1) * 512]
                    if gate is not None:
                        k = tt(JV[:, 0:512], PS[:, bk, :], gate[:, j * 512:(j + 1) * 512], ALU.mult,
                               [p, gw, st.get("jva", [])])
                        v = tt(xs, JV[:, 0:512], xs, ALU.add, [k, st["x"][t]])
                        st["jv"] = [v]
                    else:
                        v = tt(xs, PS[:, bk, :], xs, ALU.add, [p, st["x"][t]])
                    bank["free"][bk] = [v]
                    st["x"][t] = [v]
                w.release(p)
            st["ht"] = [p]

        def heads_T(dst, srcs, d, t, waits, free, scale=1.0):
            out = []
            for i in range(0, len(srcs), 4):
                part = srcs[i:i + 4]
                bk, fr = single()
                for j, a in enumerate(part):
                    dd = PS[0:d, bk, j * 128:(j + 1) * 128]
                    p = pe([waits, fr, t_cst], lambda e, a=a, dd=dd: e.transpose(dd, a, ident))
                v = evac(dst[0:d, i:i + len(part), t * 128:(t + 1) * 128],
                         PS[0:d, bk, 0:len(part) * 128].rearrange("p (j s) -> p j s", j=len(part)), [p, free], scale)
                bank["free"][bk] = [v]
                out.append(v)
            return out, p

        def group(t, maps, keys, scale, waits, Y, ycol, bias=None, sink=None, lam=None):
            n, g = len(maps), st["gi"] % 2
            st["gi"] += 1
            nk = keys // 128
            P = GRP[:, g * 2048:g * 2048 + 1024].rearrange("p (i k) -> p i k", i=4)[:, 0:n, 0:keys]
            PT = GRP[:, g * 2048 + 1024:(g + 1) * 2048]
            b0 = 2 * (bank["pair"] % 2)
            bank["pair"] += 1
            sc = PS[:, b0:b0 + 2, :].rearrange("p b (i k) -> p (b i) k", i=2)[:, 0:n, 0:keys]
            fr = [bank["free"][b0], bank["free"][b0 + 1]]
            for i, m in enumerate(maps):
                p = mm(sc[:, i, :], m[0], m[1][:, 0:keys], True, True, [waits, fr])
            src, ready, pfree = sc, p, st["grp"][g]
            if bias is not None:
                ready = bias(P, sc, [p, pfree])
                src, pfree = P, []
                bank["free"][b0] = bank["free"][b0 + 1] = [ready]
            w = scratch(4 * n)
            mx, ng, rs, rd = (w[:, j * n:(j + 1) * n] for j in range(4))
            k = dve([ready], lambda e: e.reduce_max(mx, src, AX))
            if sink is not None:
                k = tt(mx, mx, sink, ALU.max, [k])
            k = ts(ng, mx, -scale, None, ALU.mult, None, [k])
            for i in range(n):
                a = act([k, pfree], lambda e, i=i: e.activation(P[:, i, :], src[:, i, :], ACT.Exp, bias=ng[:, i:i + 1],
                                                                scale=scale, accum_out=rs[:, i:i + 1]))
            if bias is None:
                bank["free"][b0] = bank["free"][b0 + 1] = [a]
            ls = a
            if sink is not None:
                k = tt(mx, sink, mx, ALU.subtract, [k])
                e1 = act([k], lambda e: e.activation(mx, mx, ACT.Exp))
                ls = tt(rs, rs, mx, ALU.add, [e1, a])
            r = dve([ls], lambda e: e.reciprocal(rd, rs))
            no, PO = n, P
            if lam is not None:
                no = n // 2
                k = r
                for i in range(no):
                    k0 = ts(P[:, 2 * i + 1, :], P[:, 2 * i + 1, :], rd[:, 2 * i + 1:2 * i + 2], lam, ALU.mult, ALU.mult, [k])
                    k = stt(P[:, 2 * i, :], P[:, 2 * i, :], rd[:, 2 * i:2 * i + 1], P[:, 2 * i + 1, :],
                            ALU.mult, ALU.subtract, [k0])
                a = k
                maps, PO = maps[::2], P[:, 0:n:2, :]
            pts, idx = [], 0
            total = no * nk
            for j0 in range(0, total, 4):
                m4 = min(4, total - j0)
                bk, fr = single()
                for j in range(m4):
                    i, kc = divmod(j0 + j, nk)
                    s_, d_ = PO[:, i, kc * 128:(kc + 1) * 128], PS[:, bk, j * 128:(j + 1) * 128]
                    p = pe([a, fr], lambda e, s_=s_, d_=d_: e.transpose(d_, s_, ident))
                v = evac(PT[:, j0 * 128:(j0 + m4) * 128], PS[:, bk, 0:m4 * 128], [p, pfree, st["grp"][g]])
                bank["free"][bk] = [v]
                pts.append(v)
            bk, fr = single()
            for i, m in enumerate(maps):
                for kc in range(nk):
                    j = i * nk + kc
                    p = mm(PS[:, bk, i * 64:(i + 1) * 64], PT[:, j * 128:(j + 1) * 128], m[2](kc), kc == 0, kc == nk - 1,
                           [pts[j // 4], fr])
            st["grp"][g] = [p]
            o = PS[:, bk, 0:no * 64]
            if lam is not None:
                v = dve([p, st["yfree"]], lambda e: e.tensor_copy(Y[:, t, ycol:ycol + no * 64], o))
            else:
                yv = Y[:, t, ycol:ycol + no * 64].rearrange("p (i d) -> p i d", i=no)
                v = tt(yv, o.rearrange("p (i d) -> p i d", i=no), bc(rd.unsqueeze(2), [128, no, 64]), ALU.mult,
                       [p, r, st["yfree"]])
            bank["free"][bk] = [v]
            return v, p

        def block1(l, tp, ta):
            c = lambda k: PARB[:, P1[k][0]:P1[k][0] + P1[k][1]]
            sh1, sc1, g1, sh2, sc2, g2 = (MOD[:, i * 1024:(i + 1) * 1024] for i in range(6))
            m1 = stt(sc1, sc1, 1.0, c("n1"), ALU.add, ALU.mult, [ta, tp])
            m2 = stt(sc2, sc2, 1.0, c("n2"), ALU.add, ALU.mult, [ta, tp])
            hts, _ = norm(sc1, sh1, [m1])
            prj = PRJ.rearrange("p (t n) -> p t n", t=2)
            pj = [[None] * 3, [None] * 3]
            for j in range(3):
                wd = 512 if j < 2 else 256
                w = load(I["win1a"][l * 2 + j] if j < 2 else I["win1b"][l], 8 * wd)
                for t in range(2):
                    bk, fr = single()
                    p = tokens_by(HT, w, wd, t, 8, hts, fr, bk)
                    v = evac(prj[:, t, j * 512:j * 512 + wd], PS[:, bk, 0:wd], [p, st["prj"]])
                    bank["free"][bk] = [v]
                    pj[t][j] = v
                w.release(p)
            st["ht"] = [p]
            qT = QK[:, 2048:4096].rearrange("p (i s) -> p i s", i=8)
            kT = QK[:, 0:512].rearrange("p (i s) -> p i s", i=2)
            Y = H
            st["yfree"] = [st["h"][0], st["h"][1]]
            qd = []
            for t in range(2):
                sq = JV[:, 0:640].rearrange("p (i d) -> p i d", i=10)
                v = prj[:, t, 512:1152].rearrange("p (i d) -> p i d", i=10)
                k = tt(sq, v, v, ALU.mult, [pj[t][1], pj[t][2], st.get("jva", [])])
                s = scratch(10)
                k = dve([k], lambda e, s=s, sq=sq: e.reduce_sum(s, sq, AX))
                k = act([k, t_eps], lambda e, s=s: e.activation(s, s, ACT.Sqrt, bias=EPSC, scale=1.0 / 64))
                k = dve([k], lambda e, s=s: e.reciprocal(s, s))
                k = tt(v, v, bc(s.unsqueeze(2), [128, 10, 64]), ALU.mult, [k])
                st["jv"] = [k]
                k1 = tt(v[:, 0:8, :], v[:, 0:8, :], bc(c("qg").unsqueeze(1), [128, 8, 64]), ALU.mult, [k, tp])
                k2 = tt(v[:, 8:10, :], v[:, 8:10, :], bc(c("kg").unsqueeze(1), [128, 2, 64]), ALU.mult, [k, tp])
                a, _ = heads_T(qT, [v[:, i, :] for i in range(8)], 64, t, [k1], st["qb"], 0.125)
                b, _ = heads_T(kT, [v[:, i, :] for i in range(8, 10)], 64, t, [k2], st["qa"])
                qd += a + b
            st["qa"], st["qb"] = [], []
            ym = [[], []]
            for t in range(2):
                for hg in range(2):
                    nd = CST[:, C_ND + t * 256:C_ND + (t + 1) * 256]

                    def bias(P, sc, waits, t=t, hg=hg, nd=nd):
                        for i in range(4):
                            k = stt(P[:, i, :], nd[:, 0:(t + 1) * 128], 2.0 ** -(hg * 4 + i + 1), sc[:, i, :],
                                    ALU.mult, ALU.add, waits)
                        return k
                    maps = [(qT[0:64, hg * 4 + i, t * 128:(t + 1) * 128], kT[0:64, hg, :],
                             lambda kc, hg=hg: prj[:, kc, 1152 + hg * 64:1152 + (hg + 1) * 64]) for i in range(4)]
                    v, lastp = group(t, maps, (t + 1) * 128, 1.0, [qd], Y, 512 + hg * 256, bias=bias,
                                     sink=c("sink")[:, hg * 4:hg * 4 + 4])
                    ym[t].append(v)
            st["qa"], st["qb"] = [lastp], [lastp]
            mg = load(I["mg"], 2048)
            pw = load(I["poolw"][l], 512)
            mgv = mg.ap.rearrange("p (a g s) -> p a g s", a=2, g=4)
            plT = QK[:, 4096:5120].rearrange("p (g s) -> p g s", g=4)
            pt = []
            for g in range(4):
                bk, fr = single()
                for a in range(2):
                    p = mm(PS[:, bk, 0:256], prj[:, a, g * 128:(g + 1) * 128], mgv[:, a, g, :], a == 0, a == 1,
                           [pj[0][0], pj[1][0], mg.tok, fr])
                v = evac(plT[:, g, :], PS[:, bk, 0:256], [p, st.get("plf", [])])
                bank["free"][bk] = [v]
                pt.append(v)
            mg.release(p)
            for t in range(2):
                bk, fr = single()
                for g in range(4):
                    p = mm(PS[:, bk, g * 128:(g + 1) * 128], plT[:, g, t * 128:(t + 1) * 128],
                           pw.ap[:, g * 128:(g + 1) * 128], True, True, [pt, pw.tok, fr])
                v = tt(Y[:, t, 0:512], PS[:, bk, :], c("ps"), ALU.mult, [p, st["yfree"]])
                bank["free"][bk] = [v]
                ym[t].append(v)
            pw.release(p)
            st["plf"] = [p]
            st["prj"] = [p, lastp]
            s, tr = rstd([Y[:, t, j * 512:(j + 1) * 512] for t in range(2) for j in range(2)], 512.0,
                         [ym[t] for t in range(2) for j in range(2)])
            hs = []
            for t in range(2):
                for j in range(2):
                    i = t * 2 + j
                    yy = Y[:, t, j * 512:(j + 1) * 512]
                    k = stt(yy, yy, s[:, i:i + 1], c("mg")[:, j * 512:(j + 1) * 512], ALU.mult, ALU.mult, [tr, tp])
                hs.append(k)
            yt, last = transpose_tm(Y, HT, hs, st["ht"])
            st["h"] = [[last], [last]]
            residual([load(I["wout1"][l * 2 + j], 4096) for j in range(2)], HT, [yt], g1, [ta])
            peer(l, sc2, sh2, g2, m2)
            st["par"] = st["x"][0] + st["x"][1]
            st["mod"] = st["x"][0] + st["x"][1]

        def vmax(dst, src, waits):
            return dve(waits, lambda e: e.max(dst, src))

        def vindex(dst, top, src, waits):
            return dve(waits, lambda e: e.max_index(dst, top, src))

        def vreplace(dst, top, src, waits):
            return dve(waits, lambda e: e.match_replace(dst, top, src, TINY))

        def topk(t, h, S, ready):
            u = st["tn"] % 2
            st["tn"] += 1
            V, Ix = TV[:, u * 64:(u + 1) * 64], TI[:, u * 64:(u + 1) * 64]
            JS = GRP2
            k = None
            for p in range(2):
                s, js = S[:, 2 * h + p, :], JS[:, p * 128:p * 128 + 128]
                v, ix = V[:, p * 16:p * 16 + 16], Ix[:, p * 16:p * 16 + 16]
                k = vmax(v[:, 0:8], s, [ready, st["tv"][u]])
                vindex(ix[:, 0:8], v[:, 0:8], s, [k])
                k = vreplace(js, v[:, 0:8], s, [k])
                k = vmax(v[:, 8:16], js, [k])
                k = vindex(ix[:, 8:16], v[:, 8:16], js, [k])
            cd = TC[:, 0:256]
            cv = cd.rearrange("p (a b) -> p a b", a=16)
            k1 = tt(cv, bc(V[:, 0:16].unsqueeze(2), [128, 16, 16]), bc(V[:, 16:32].unsqueeze(1), [128, 16, 16]), ALU.add, [k])
            v, ix = V[:, 32:48], Ix[:, 32:48]
            k2 = vmax(v[:, 0:8], cd, [k1])
            k3 = vindex(ix[:, 0:8], v[:, 0:8], cd, [k2])
            k4 = vreplace(JS[:, 0:256], v[:, 0:8], cd, [k2])
            k5 = vmax(v[:, 8:16], JS[:, 0:256], [k4])
            k6 = vindex(ix[:, 8:16], v[:, 8:16], JS[:, 0:256], [k5])
            j = (t * 8 + h) * 16
            ng = V[:, 48:49]
            n1 = ts(ng, v[:, 0:1], -1.0, None, ALU.mult, None, [k2])
            ga_ = GATE[:, j:j + 16]
            a = act([n1, k5], lambda e: e.activation(ga_, v, ACT.Exp, bias=ng, scale=1.0, accum_out=V[:, 49:50]))
            q = ts(Ix[:, 48:64], ix, 4, None, ALU.logical_shift_right, None, [k6, k3])
            q2 = ts(ix, ix, 15, None, ALU.bitwise_and, None, [q])
            JF = JS[:, 256:288]
            c1 = dve([q], lambda e: e.tensor_copy(JF[:, 0:16], Ix[:, 48:64]))
            c2 = dve([q2], lambda e: e.tensor_copy(JF[:, 16:32], ix))
            c3 = dve([k], lambda e: e.tensor_copy(JS[:, 288:320], Ix[:, 0:32]))
            oh = JS[:, 512:1024].rearrange("p (a k m) -> p a k m", a=2, k=16)
            for z in range(2):
                c4 = tt(oh[:, z], bc(JF[:, z * 16:z * 16 + 16].unsqueeze(2), [128, 16, 16]),
                        bc(CST[:, C_IOTA:C_IOTA + 16].unsqueeze(1), [128, 16, 16]), ALU.is_equal, [c1, c2])
                c4 = tt(oh[:, z], oh[:, z], bc(JS[:, 288 + z * 16:304 + z * 16].unsqueeze(1), [128, 16, 16]),
                        ALU.mult, [c4, c3])
            sel = JS[:, 320:352]
            c5 = dve([c4], lambda e: e.reduce_sum(sel, JS[:, 512:1024].rearrange("p (k m) -> p k m", m=16), AX))
            eid = EID[:, j:j + 16]
            c6 = stt(eid, sel[:, 0:16], 128.0, sel[:, 16:32], ALU.mult, ALU.add, [c5, st["eidf"]])
            r = dve([a], lambda e: e.reciprocal(V[:, 50:51], V[:, 49:50]))
            g = ts(ga_, ga_, V[:, 50:51], None, ALU.mult, None, [r])
            st["tv"][u] = [g]
            return c6, g

        def peer(l, gA, gB, gate2, mready):
            hts, hs = norm(gA, gB, [mready])
            S = GRP.rearrange("p (t i n) -> p t i n", t=2, i=16)
            st["nsk"] = st.get("nsk", 0) + 16
            t_sk = sp.dma([st.get("skf", [])], lambda e: e.dma_start(SKB, I["skT"][l]), s_sk, st["nsk"])
            skv = SKB.rearrange("p (a n) -> p a n", a=2)
            sready = [[None] * 4, [None] * 4]
            gfree = st["grp"][0] + st["grp"][1]

            def project(b):
                w = load(I["wq"][l * 4 + b], 4096)
                wv = w.ap.rearrange("p (k n) -> p k n", k=8)
                half = QK[:, (b % 2) * 1024:(b % 2 + 1) * 1024].rearrange("p (i s) -> p i s", i=4)
                fre = st["qa"] if b % 2 == 0 else st["qb"]
                ev = []
                for i2 in range(2):
                    bk, fr = single()
                    for i1 in range(2):
                        i = i2 * 2 + i1
                        for k in range(8):
                            p = mm(PS[:, bk, i1 * 256:(i1 + 1) * 256], wv[:, k, i * 128:(i + 1) * 128], HT[:, k, :],
                                   k == 0, k == 7, [w.tok, hts, fr])
                    v = act([p, fre], lambda e, i2=i2, bk=bk: e.activation(
                        half[:, i2 * 2:i2 * 2 + 2, :], PS[:, bk, :].rearrange("p (i s) -> p i s", i=2), ACT.Copy))
                    bank["free"][bk] = [v]
                    ev.append(v)
                w.release(p)
                st["ht"] = [p]
                for t in range(2):
                    bk, fr = single()
                    for i in range(4):
                        p = mm(PS[:, bk, i * 128:(i + 1) * 128], half[:, i, t * 128:(t + 1) * 128], skv[:, i % 2, :],
                               True, True, [ev, t_sk, fr])
                    v = act([p, gfree], lambda e, t=t, b=b, bk=bk: e.activation(
                        S[:, t, b * 4:b * 4 + 4, :], PS[:, bk, :].rearrange("p (i n) -> p i n", i=4), ACT.Copy))
                    bank["free"][bk] = [v]
                    sready[t][b] = v
                if b % 2 == 0:
                    st["qa"] = [p]
                else:
                    st["qb"] = [p]
                return p

            tk = {}
            order = [(t, h) for t in range(2) for h in range(8)]
            nb = 0

            def prepare(n):
                nonlocal nb
                if n >= 16:
                    return
                t, h = order[n]
                while nb <= h // 2:
                    p = project(nb)
                    nb += 1
                    if nb == 4:
                        st["skf"] = [p]
                tk[n] = topk(t, h, S[:, t], sready[t][h // 2])

            prepare(0)
            prepare(1)
            g2h = []
            for n in range(16):
                t, h = order[n]
                te, tg = tk[n]
                its = []
                for kk in range(16):
                    it = Item(2)
                    j = n * 16 + kk
                    it.tok = pool.dma([it.waits, te], lambda e, it=it, j=j: e.indirect_dma_start(
                        out=it.ap, out_offset=None, in_=I[f"uv{l}"],
                        in_offset=bass.IndirectOffsetOnAxis(ap=EID[:, j:j + 1], axis=0)), *it.count(ga[it.u0]))
                    its.append(it)
                    if kk % 4 == 3:
                        j0 = j - 3
                        for q in range(4):
                            x = its[-4 + q]
                            k = dve([x.tok, hs, st["avf"]], lambda e, x=x, j=j0 + q, t=t: e.tensor_tensor_reduce(
                                out=JV2, in0=x.ap[:, 0:1024], in1=H[:, t, :], scale=1.0, scalar=0.0,
                                op0=ALU.mult, op1=ALU.add, accum_out=AV[:, j:j + 1]))
                        a = act([k], lambda e, j0=j0: e.activation(AG[:, j0:j0 + 4], AV[:, j0:j0 + 4], ACT.Gelu))
                        k = tt(AG[:, j0:j0 + 4], AG[:, j0:j0 + 4], GATE[:, j0:j0 + 4], ALU.mult, [a, tg])
                        for q in range(4):
                            x = its[-4 + q]
                            d = st["dn"] % 4
                            st["dn"] += 1
                            jj = j0 + q
                            z = act([k, st["dg"][d], t_cst], lambda e, d=d, jj=jj: e.activation(
                                DG[:, d, :], ident, ACT.Copy, scale=AG[:, jj:jj + 1]))
                            first, lastm = (jj % 128 == 0), (jj % 128 == 127)
                            for hf in range(2):
                                p = mm(PS[:, 2 * t + hf, :], DG[:, d, :], x.ap[:, 1024 + hf * 512:1536 + hf * 512],
                                       first, lastm, [z, x.tok, bank["free"][2 * t + hf]])
                            st["dg"][d] = [p]
                            x.release(p, k)
                prepare(n + 2)
                if h == 7:
                    for hf in range(2):
                        xs = X[:, t, hf * 512:(hf + 1) * 512]
                        k = tt(JV[:, 0:512], PS[:, 2 * t + hf, :], gate2[:, hf * 512:(hf + 1) * 512], ALU.mult,
                               [p, st.get("jva", [])])
                        v = tt(xs, JV[:, 0:512], xs, ALU.add, [k, st["x"][t]])
                        bank["free"][2 * t + hf] = [v]
                    st["jv"] = [v]
                    st["x"][t] = [v]
            st["h"] = [st["x"][0], st["x"][1]]
            st["grp"] = [st["x"][1], st["x"][1]]
            st["eidf"] = [x.tok]
            st["avf"] = []

        GRP2 = QK[:, 2048:3072]
        JV2 = QK[:, 3072:4096]
        st["eidf"], st["avf"] = [], []

        def rope(dst, src, n, half, tab, tmp, waits):
            cc = tab[:, 0:2 * half].rearrange("p (a b) -> p a b", a=2)
            ss = tab[:, 2 * half:4 * half].rearrange("p (a b) -> p a b", a=2)
            for z in range(2):
                c = bc(cc[:, z, :].unsqueeze(1), [128, n, half])
                k = tt(dst[:, :, z, :], src[:, :, z, :], c, ALU.mult, waits)
                s = bc(ss[:, z, :].unsqueeze(1), [128, n, half])
                k = tt(tmp[:, :, z, :], src[:, :, 1 - z, :], s, ALU.mult, waits)
            for z in range(2):
                k = tt(dst[:, :, z, :], dst[:, :, z, :], tmp[:, :, z, :], ALU.add, [k])
            return k

        def block2(l, tp):
            c = lambda k: PARB[:, P2[k][0]:P2[k][0] + P2[k][1]]
            lam0 = 0.8 - 0.6 * math.exp(-0.3 * l)
            prj = MOD[:, 0:4800].rearrange("p (t n) -> p t n", t=2)
            hts, _ = norm(c("n1"), None, [tp])
            pj = [[], []]
            for j in range(5):
                w = load(I["win2"][l * 5 + j], 3840)
                for t in range(2):
                    bk, fr = single()
                    p = tokens_by(HT, w, 480, t, 8, hts, fr, bk)
                    v = evac(prj[:, t, j * 480:(j + 1) * 480], PS[:, bk, 0:480], [p, st["mod"]])
                    bank["free"][bk] = [v]
                    pj[t].append(v)
                w.release(p)
            st["ht"] = [p]
            Y = H
            st["yfree"] = [st["h"][0], st["h"][1]]
            A = QK[:, 0:2048].rearrange("p (i s) -> p i s", i=8)
            B = QK[:, 2048:6144].rearrange("p (i s) -> p i s", i=16)
            rp = lambda t: CST[:, C_ROPE + t * 192:C_ROPE + (t + 1) * 192]
            ls = scratch(8)
            for z in range(2):
                lq = c("lam")[:, z * 64:z * 64 + 32]
                lk = c("lam")[:, z * 64 + 32:z * 64 + 64]
                k = dve([tp, st.get("jva", [])], lambda e, lq=lq, lk=lk, z=z: e.tensor_tensor_reduce(
                    out=JV[:, 0:32], in0=lq, in1=lk, scale=1.0, scalar=0.0, op0=ALU.mult, op1=ALU.add,
                    accum_out=ls[:, z:z + 1]))
            st["jv"] = [k]
            k = act([k], lambda e: e.activation(ls[:, 2:4], ls[:, 0:2], ACT.Exp))
            tlam = stt(ls[:, 4:5], ls[:, 2:3], lam0, ls[:, 3:4], ALU.add, ALU.subtract, [k])
            lam = ls[:, 4:5]
            wu = load(I["wuq"][l], 768)
            wk = load(I["wukv"][l], 512)
            KVB = PRJ[:, 0:1024].rearrange("p (t n) -> p t n", t=2)
            QF = PRJ[:, 1024:1792].rearrange("p (t n) -> p t n", t=2)
            TMP = PRJ[:, 1792:2560]
            tmpf = st["prj"]
            kv_t, qd = [], []
            lastqk = []
            for t in range(2):
                s, tr = rstd([prj[:, t, X_CQ:X_CQ + 192]], 192.0, [[pj[t]]])
                k1 = stt(prj[:, t, X_CQ:X_CQ + 192], prj[:, t, X_CQ:X_CQ + 192], s[:, 0:1], c("q"), ALU.mult, ALU.mult,
                         [tr, tp])
                s2, tr2 = rstd([prj[:, t, X_CKV:X_CKV + 128]], 128.0, [[pj[t]]])
                k2 = stt(prj[:, t, X_CKV:X_CKV + 128], prj[:, t, X_CKV:X_CKV + 128], s2[:, 0:1], c("kv"), ALU.mult,
                         ALU.mult, [tr2, tp])
                bk, fr = single()
                for (dd, a) in ((PS[:, bk, 0:128], prj[:, t, 0:128]), (PS[0:64, bk, 128:256], prj[:, t, 128:192]),
                                (PS[:, bk, 256:384], prj[:, t, X_CKV:X_CKV + 128])):
                    p = pe([k1, k2, fr, t_cst], lambda e, dd=dd, a=a: e.transpose(dd, a, ident))
                CT = GRP[:, t * 384:(t + 1) * 384]
                v1 = act([p, st["grp"]], lambda e, CT=CT, bk=bk: e.activation(CT[:, 0:128], PS[:, bk, 0:128], ACT.Copy))
                v2 = act([v1], lambda e, CT=CT, bk=bk: e.activation(CT[0:64, 128:256], PS[0:64, bk, 128:256], ACT.Copy))
                v3 = act([v2], lambda e, CT=CT, bk=bk: e.activation(CT[:, 256:384], PS[:, bk, 256:384], ACT.Copy))
                bank["free"][bk] = [v1, v2, v3]
                wuv = wu.ap.rearrange("p (k n) -> p k n", k=2)
                bk, fr = single()
                mm(PS[:, bk, 0:384], CT[:, 0:128], wuv[:, 0, :], True, False, [v1, v2, v3, wu.tok, fr])
                pq = mm(PS[:, bk, 0:384], CT[0:64, 128:256], wuv[0:64, 1, :], False, True)
                kq = dve([pq, tmpf], lambda e, t=t, bk=bk: e.tensor_copy(QF[:, t, :], PS[:, bk, 0:384]))
                bank["free"][bk] = [kq]
                bk, fr = single()
                pk = mm(PS[:, bk, :], CT[:, 256:384], wk.ap, True, True, [wk.tok, fr])
                kk_ = act([pk, tmpf], lambda e, t=t, bk=bk: e.activation(KVB[:, t, :], PS[:, bk, :], ACT.Copy))
                bank["free"][bk] = [kk_]
                tab = rp(t)[:, 0:64]
                qv = QF[:, t, :].rearrange("p (i d) -> p i d", i=4)
                RQ = TMP[:, 0:128].rearrange("p (i d) -> p i d", i=4)
                kr_ = rope(RQ.rearrange("p i (a b) -> p i a b", a=2), qv[:, :, 64:96].rearrange("p i (a b) -> p i a b", a=2),
                           4, 16, tab, TMP[:, 128:256].rearrange("p (i a b) -> p i a b", i=4, a=2), [kq, t_cst, lastqk])
                kq2 = dve([kr_], lambda e, qv=qv, RQ=RQ: e.tensor_copy(qv[:, :, 64:96], RQ))
                RK = TMP[:, 256:288]
                kr2 = rope(RK.rearrange("p (i a b) -> p i a b", i=1, a=2),
                           prj[:, t, X_KR:X_KR + 32].rearrange("p (i a b) -> p i a b", i=1, a=2), 1, 16, tab,
                           TMP[:, 288:320].rearrange("p (i a b) -> p i a b", i=1, a=2), [pj[t], t_cst])
                KF = TMP[:, 320:704].rearrange("p (i d) -> p i d", i=4)
                kf1 = dve([kk_], lambda e, t=t, KF=KF: e.tensor_copy(
                    KF[:, :, 0:64], KVB[:, t, 0:256].rearrange("p (i d) -> p i d", i=4)))
                kf2 = dve([kr2], lambda e, KF=KF, RK=RK: e.tensor_copy(KF[:, :, 64:96], bc(RK.unsqueeze(1), [128, 4, 32])))
                a1, _ = heads_T(A[:, 0:4, :], [qv[:, i, :] for i in range(4)], 96, t, [kq2], st["qa"])
                a2, p2 = heads_T(A[:, 4:8, :], [KF[:, i, :] for i in range(4)], 96, t, [kf1, kf2], st["qa"])
                lastqk = [p2]
                qd += a1 + a2
                kv_t.append(kk_)
            wu.release(pq)
            wk.release(pk)
            st["grp"] = [[pk], [pk]]
            ym = [[], []]
            for t in range(2):
                maps = [(A[0:96, i, t * 128:(t + 1) * 128], A[0:96, 4 + i, :],
                         lambda kc, i=i: KVB[:, kc, 256 + i * 64:256 + (i + 1) * 64]) for i in range(4)]
                v, lp = group(t, maps, 256, 96.0 ** -0.5, [qd, kv_t], Y, 0)
                ym[t].append(v)
            st["qa"] = [lp]
            qd, lastqk = [], [st["qb"], st.get("plf", [])]
            RB = PRJ[:, 1024:1536]
            RT = PRJ[:, 1536:2048]
            prev = lp
            for t in range(2):
                v = prj[:, t, X_BQ:X_BQ + 512].rearrange("p (i a b) -> p i a b", i=16, a=2)
                k = rope(RB.rearrange("p (i a b) -> p i a b", i=16, a=2), v, 16, 16, rp(t)[:, 0:64],
                         RT.rearrange("p (i a b) -> p i a b", i=16, a=2), [pj[t], prev])
                a, prev = heads_T(B, [RB[:, i * 32:(i + 1) * 32] for i in range(16)], 32, t, [k], lastqk)
                qd += a
            for t in range(2):
                for hg in range(2):
                    maps = [(B[0:32, hg * 4 + i, t * 128:(t + 1) * 128], B[0:32, 8 + hg * 4 + i, :],
                             lambda kc, i=i, hg=hg: prj[:, kc, X_BV + (hg * 2 + i // 2) * 64:X_BV + (hg * 2 + i // 2 + 1) * 64])
                            for i in range(4)]
                    v, lp = group(t, maps, 256, 32.0 ** -0.5, [qd, tlam], Y, 256 + hg * 128, lam=lam)
                    ym[t].append(v)
            st["qb"], st["plf"] = [lp], []
            qd = []
            for t in range(2):
                v = prj[:, t, X_SQ:X_SQ + 384].rearrange("p (i a b) -> p i a b", i=6, a=2)
                k = rope(RB[:, 0:384].rearrange("p (i a b) -> p i a b", i=6, a=2), v, 6, 32, rp(t)[:, 64:192],
                         RT[:, 0:384].rearrange("p (i a b) -> p i a b", i=6, a=2), [pj[t], prev])
                a, prev = heads_T(A[:, 0:4, :], [RB[:, i * 64:(i + 1) * 64] for i in range(4)], 64, t, [k], st["qa"], 0.125)
                b, prev = heads_T(A[:, 4:6, :], [RB[:, i * 64:(i + 1) * 64] for i in range(4, 6)], 64, t, [k], st["qa"])
                qd += a + b
            for t in range(2):
                sm = CST[:, C_SM + t * 256:C_SM + (t + 1) * 256]

                def bias(P, sc, waits, sm=sm):
                    return tt(P, sc, bc(sm.unsqueeze(1), [128, 4, 256]), ALU.add, waits)
                maps = [(A[0:64, i, t * 128:(t + 1) * 128], A[0:64, 4 + i // 2, :],
                         lambda kc, i=i: prj[:, kc, X_SV + (i // 2) * 64:X_SV + (i // 2 + 1) * 64]) for i in range(4)]
                v, lp = group(t, maps, 256, 1.0, [qd], Y, 512, bias=bias, sink=c("sink"))
                ym[t].append(v)
            st["qa"] = [lp]
            qd = []
            for t in range(2):
                a, _ = heads_T(B[:, 0:4, :], [prj[:, t, X_NQ + i * 64:X_NQ + (i + 1) * 64] for i in range(4)], 64, t,
                               [pj[t]], st["qb"], 0.125)
                b, _ = heads_T(B[:, 4:8, :], [prj[:, t, X_NK + i * 64:X_NK + (i + 1) * 64] for i in range(4)], 64, t,
                               [pj[t]], st["qb"])
                qd += a + b
            for t in range(2):
                nb = load(I["nab"][l * 2 + t], 1024)
                nbv = nb.ap.rearrange("p (i k) -> p i k", i=4)

                def bias(P, sc, waits, nb=nb, nbv=nbv):
                    k = tt(P, sc, nbv, ALU.add, [waits, nb.tok])
                    nb.release(k)
                    return k
                maps = [(B[0:64, i, t * 128:(t + 1) * 128], B[0:64, 4 + i, :],
                         lambda kc, i=i: prj[:, kc, X_NV + i * 64:X_NV + (i + 1) * 64]) for i in range(4)]
                v, lp = group(t, maps, 256, 1.0, [qd], Y, 768, bias=bias)
                ym[t].append(v)
            st["qb"], st["prj"], st["mod"] = [lp], [prev, lp], [lp]
            hs = []
            s, tr = rstd([Y[:, t, o:o + 256] for t in range(2) for o in (0, 512, 768)], 256.0,
                         [ym[t] for t in range(2) for _ in range(3)])
            for t in range(2):
                for i, (o, g) in enumerate(((0, "oa"), (512, "oc"), (768, "od"))):
                    yy = Y[:, t, o:o + 256]
                    k = stt(yy, yy, s[:, t * 3 + i:t * 3 + i + 1], c(g), ALU.mult, ALU.mult, [tr, tp])
                yb = Y[:, t, 256:512].rearrange("p (i d) -> p i d", i=4)
                jb = JV[:, 0:256].rearrange("p (i d) -> p i d", i=4)
                k2 = tt(jb, yb, yb, ALU.mult, [ym[t], st["jva"]])
                q = scratch(4)
                k2 = dve([k2], lambda e, q=q, jb=jb: e.reduce_sum(q, jb, AX))
                st["jv"] = [k2]
                k2 = act([k2], lambda e, q=q: e.activation(q, q, ACT.Sqrt, bias=EPSC, scale=1.0 / 64))
                k2 = dve([k2], lambda e, q=q: e.reciprocal(q, q))
                k2 = tt(yb, yb, bc(q.unsqueeze(2), [128, 4, 64]), ALU.mult, [k2])
                k2 = stt(yb, yb, 1.0 - lam0, bc(c("sub").unsqueeze(1), [128, 4, 64]), ALU.mult, ALU.mult, [k2])
                hs.append([k, k2])
            yt, last = transpose_tm(Y, HT, hs, st["ht"])
            st["h"] = [[last], [last]]
            residual([load(I["wout2"][l * 2 + j], 4096) for j in range(2)], HT, [yt], None, None)
            hts, _ = norm(c("n2"), None, [tp])
            st["par"] = hts
            AT = QK[:, 2048:4096].rearrange("p (b i s) -> p b i s", b=2, i=4)
            atf = [st["qb"], st["qb"]]
            last = None

            def down(b, at, wd):
                for t in range(2):
                    for hf in range(2):
                        for i in range(4):
                            p = mm(PS[:, t * 2 + hf, :], AT[:, b % 2, i, t * 128:(t + 1) * 128],
                                   wd.ap[:, i * 1024 + hf * 512:i * 1024 + (hf + 1) * 512], b == 0 and i == 0,
                                   b == 7 and i == 3, [at, wd.tok, bank["free"][t * 2 + hf]])
                wd.release(p)
                atf[b % 2] = [p]
                return p

            pend = None
            for b in range(8):
                w = load(I["wup"][l * 8 + b], 4096)
                wd = load(I["wdn"][l * 8 + b], 4096)
                wv = w.ap.rearrange("p (k n) -> p k n", k=8)
                at = []
                for i2 in range(2):
                    bk, fr = single()
                    for i1 in range(2):
                        i = i2 * 2 + i1
                        for k in range(8):
                            p = mm(PS[:, bk, i1 * 256:(i1 + 1) * 256], wv[:, k, i * 128:(i + 1) * 128], HT[:, k, :],
                                   k == 0, k == 7, [w.tok, hts, fr])
                    pv = PS[:, bk, :].rearrange("p (i s) -> p i s", i=2)
                    dst = AT[:, b % 2, i2 * 2:i2 * 2 + 2, :]
                    r1 = act([p, atf[b % 2]], lambda e, dst=dst, pv=pv: e.activation(dst, pv, ACT.Relu))
                    v = tt(dst, dst, dst, ALU.mult, [r1])
                    bank["free"][bk] = [r1]
                    at.append(v)
                w.release(p)
                st["ht"] = [p]
                if pend is not None:
                    down(*pend)
                pend = (b, at, wd)
            p = down(*pend)
            st["qb"] = [p]
            for t in range(2):
                for hf in range(2):
                    xs = X[:, t, hf * 512:(hf + 1) * 512]
                    v = tt(xs, PS[:, t * 2 + hf, :], xs, ALU.add, [p, st["x"][t]])
                    bank["free"][t * 2 + hf] = [v]
                st["x"][t] = [v]

        for l in range(L):
            tp = load_par(I["par1"][l], PAR)
            ta = ada(l)
            block1(l, tp, ta)
        for l in range(L):
            tp = load_par(I["par2"][l], 3332)
            block2(l, tp)
        tp = load_par(I["fing"], 1024)
        s, tr = rstd([X[:, 0, :], X[:, 1, :]], 1024.0, st["x"])
        for t in range(2):
            k = stt(X[:, t, :], X[:, t, :], s[:, t:t + 1], PARB[:, 0:1024], ALU.mult, ALU.mult, [tr, tp])
            st["x"][t] = [k]
        ov = out.rearrange("(t p) d -> p t d", p=128)
        t_o = sp.dma([st["x"]], lambda e: e.dma_start(ov, X), s_out, 16)
        sp([t_o], lambda e: e.nop())

        for e in (pe, act, dve, pool, sp):
            e.number()
        block = ctx.enter_context(nc.Block())

        @block.sync
        def _(e):
            sp.emit(e)

        @block.gpsimd
        def _(e):
            pool.emit(e)

        @block.scalar
        def _(e):
            act.emit(e)

        @block.vector
        def _(e):
            dve.emit(e)

        @block.tensor
        def _(e):
            pe.emit(e)


def constants():
    f = np.float32
    cst = np.zeros((128, C_END), f)
    cst[:, C_ID:C_ID + 128] = np.eye(128, dtype=f)
    pos = np.arange(256)
    q = pos.reshape(2, 128)
    d = q[:, :, None] - pos[None, None, :]
    nd = np.where((d >= 0) & (d < 128), -d.astype(f), f(-1e30))
    cst[:, C_ND:C_ND + 512] = nd.transpose(1, 0, 2).reshape(128, 512)
    sm = np.where(np.abs(d) <= 128, f(0), f(-1e30))
    cst[:, C_SM:C_SM + 512] = sm.transpose(1, 0, 2).reshape(128, 512)
    tabs = []
    for dim in (32, 64):
        inv = (f(1.0) / (f(10000.0) ** (np.arange(0, dim, 2, dtype=f) / f(dim)))).astype(f)
        ang = (np.arange(256, dtype=f)[:, None] * inv[None, :]).astype(f)
        c, s = np.cos(ang).astype(f), np.sin(ang).astype(f)
        tabs += [c, c, -s, s]
    tab = np.concatenate(tabs, axis=1)
    cst[:, C_ROPE:C_ROPE + 384] = tab.reshape(2, 128, 192).transpose(1, 0, 2).reshape(128, 384)
    cst[:, C_IOTA:C_IOTA + 16] = np.arange(16, dtype=f)
    mg = np.zeros((4, 256, 256), f)
    for g, w in enumerate((2, 4, 8, 16)):
        dd = pos[None, :] - pos[:, None]
        mg[g] = np.where((dd >= 0) & (dd < w), f(1) / np.minimum(pos + 1, w).astype(f)[None, :], f(0))
        mg[g] -= np.eye(256, dtype=f)
    mg = mg.reshape(4, 2, 128, 256).transpose(2, 1, 0, 3).reshape(128, 2048)
    return cst, mg


def layout(v):
    f = np.float32
    a = {k: np.asarray(x) for k, x in v.items()}

    def cols(w, n):
        l_, k, m = w.shape
        w = w.reshape(l_, k // 128, 128, m // n, n).transpose(0, 3, 2, 1, 4)
        return np.ascontiguousarray(w).reshape(l_ * (m // n), 128, (k // 128) * n)

    cst, mg = constants()
    o = {"cst": cst, "mg": mg}
    o["x"] = a["x"].reshape(256, 1024)
    o["cT"] = np.ascontiguousarray(a["c"].reshape(8, 128).T)
    o["wada"] = cols(a["w_ada"], 512)
    o["bada"] = a["b_ada"]
    par = np.concatenate([a["norm1_g"], a["norm2_g"], a["pool_scale"], a["q_norm_g"], a["k_norm_g"], a["attn_sinks"],
                          a["mix_norm_g"]], axis=1)
    o["par1"] = par
    o["win1a"] = cols(a["w_in"][:, :, 0:1024], 512)
    o["win1b"] = cols(a["w_in"][:, :, 1024:1280], 256)
    o["poolw"] = np.ascontiguousarray(a["pool_w"].transpose(0, 2, 1, 3)).reshape(L, 128, 512)
    o["wout1"] = cols(a["w_out"], 512)
    o["wq"] = cols(a["peer_wq"], 512)
    o["skT"] = np.ascontiguousarray(a["peer_subkeys"].transpose(0, 3, 1, 2)).reshape(L, 128, 256)
    for l in range(L):
        o[f"uv{l}"] = np.concatenate([a["peer_u"][l], a["peer_v"][l]], axis=1)
    o["par2"] = np.concatenate([a["norm1_g_2"], a["norm2_g_2"], a["mla_q_norm_g_2"], a["mla_kv_norm_g_2"],
                                a["diff_lambda_q1_2"], a["diff_lambda_k1_2"], a["diff_lambda_q2_2"], a["diff_lambda_k2_2"],
                                a["diff_subln_g_2"], a["swa_sinks_2"], a["out_g_mla_2"], a["out_g_swa_2"],
                                a["out_g_na_2"]], axis=1)
    o["fing"] = a["final_norm_g_2"]
    o["win2"] = cols(a["w_in_2"], 480)
    wuq = np.zeros((L, 256, 384), f)
    wuq[:, 0:192] = a["mla_w_uq_2"]
    o["wuq"] = np.ascontiguousarray(wuq.reshape(L, 2, 128, 384).transpose(0, 2, 1, 3)).reshape(L, 128, 768)
    o["wukv"] = np.concatenate([a["mla_w_uk_2"], a["mla_w_uv_2"]], axis=2)
    pos = np.arange(256)
    r, c = pos // 64, pos % 64
    start = np.clip(c - 8, 0, 48)
    inside = (c[None, :] >= start[:, None]) & (c[None, :] < start[:, None] + 16)
    ri = r[None, :] - r[:, None] + 7
    ci = np.clip(c[None, :] - c[:, None] + 15, 0, 30)
    nab = np.where(inside[None, None], a["na_rpb_2"][:, :, ri, ci], f(-1e30)).astype(f)
    o["nab"] = np.ascontiguousarray(nab.reshape(L, 4, 2, 128, 256).transpose(0, 2, 3, 1, 4)).reshape(L * 2, 128, 1024)
    o["wout2"] = cols(a["w_out_2"], 512)
    o["wup"] = cols(a["w_up_2"], 512)
    wd = a["w_down_2"].reshape(L, 8, 4, 128, 1024).transpose(0, 1, 3, 2, 4)
    o["wdn"] = np.ascontiguousarray(wd).reshape(L * 8, 128, 4096)
    return {k: np.ascontiguousarray(x) for k, x in o.items()}


def declare(nc, arrays):
    I = {k: nc.dram_tensor("in_" + k, a.shape, mybir.dt.from_np(a.dtype), kind="ExternalInput").ap()
         for k, a in arrays.items()}
    out = nc.dram_tensor("out_x", (256, 1024), F32, kind="ExternalOutput").ap()
    build(nc, I, out)


def kernel(**inputs):
    import concourse.bacc as _bacc
    from concourse.bass_utils import run_bass_kernel_spmd as _run

    arrays = layout(inputs)
    nc = _bacc.Bacc("TRN2", target_bir_lowering=False, num_devices=1)
    declare(nc, arrays)
    r = _run(nc, [{"in_" + k: a for k, a in arrays.items()}], core_ids=[0])
    return r.results[0]["out_x"].reshape(1, 256, 1024)
```

```python
import math
from contextlib import ExitStack

import numpy as np

import concourse.bass as bass
from concourse import mybir

F32 = mybir.dt.float32
I32 = mybir.dt.int32
U32 = mybir.dt.uint32
ALU = mybir.AluOpType
ACT = mybir.ActivationFunctionType
AX = mybir.AxisListType.X

L = 2
SLOTS = 8
SLOT = 2048
AHEAD = 1
BATCH = 2
RATE = 1.7
PAR = 3720
TINY = -3.0e38
EPS = 1e-6

C_ID, C_ND, C_SM, C_ROPE, C_IOTA, C_END = 0, 128, 640, 1152, 1536, 1552
P1 = dict(n1=(0, 1024), n2=(1024, 1024), ps=(2048, 512), qg=(2560, 64), kg=(2624, 64), sink=(2688, 8), mg=(2696, 1024))
P2 = dict(n1=(0, 1024), n2=(1024, 1024), q=(2048, 192), kv=(2240, 128), lam=(2368, 128), sub=(2496, 64), sink=(2560, 4),
          oa=(2564, 256), oc=(2820, 256), od=(3076, 256))
X_CQ, X_CKV, X_KR, X_BQ, X_BV, X_SQ, X_SK, X_SV, X_NQ, X_NK, X_NV = 0, 192, 320, 352, 864, 1120, 1376, 1504, 1632, 1888, 2144


class Token:

    def __init__(self, sem, value=None):
        self.sem, self.value, self.used = sem, value, False


class Engine:

    def __init__(self, sem, chained=False):
        self.sem, self.items, self.chained, self.last = sem, [], chained, None

    def __call__(self, waits, fn):
        tok = Token(self.sem)
        self.items.append((flat([waits, self.last]), fn, tok, None))
        if self.chained:
            self.last = tok
        return tok

    def dma(self, waits, fn, sem, value):
        tok = Token(sem, value)
        self.items.append((flat(waits), fn, None, sem))
        return tok

    def number(self):
        n = 0
        for _, _, tok, _ in self.items:
            if tok is not None and tok.used:
                n += 1
                tok.value = n

    def emit(self, eng):
        seen = {}
        for waits, fn, tok, sem in self.items:
            for w in waits:
                if seen.get(id(w.sem), 0) < w.value:
                    seen[id(w.sem)] = w.value
                    eng.wait_ge(w.sem, w.value)
            ins = fn(eng)
            if sem is not None:
                ins.then_inc(sem, 16)
            elif tok is not None and tok.used:
                ins.then_inc(tok.sem, 1)


def flat(waits):
    out = []
    for w in waits:
        if isinstance(w, (list, tuple)):
            out += flat(w)
        elif w is not None:
            w.used = True
            out.append(w)
    return out


def bc(ap, shape):
    return ap.to_broadcast(shape)


def build(nc, I, out):
    with ExitStack() as ctx:
        def sb(name, n, dt=F32):
            return ctx.enter_context(nc.sbuf_tensor(name, [128, n], dt))

        def sem(name):
            return ctx.enter_context(nc.semaphore(name))

        X = sb("X", 2048)[:, :].rearrange("p (t d) -> p t d", t=2)
        MOD = sb("MOD", 5120)[:, :]
        G2 = sb("G2", 2048)[:, :]
        PARB = sb("PARB", PAR)[:, :]
        HT = sb("HT", 2048)[:, :].rearrange("p (c s) -> p c s", c=8)
        H = sb("H", 2048)[:, :].rearrange("p (t d) -> p t d", t=2)
        PRJ = sb("PRJ", 2560)[:, :]
        GRP = sb("GRP", 4096)[:, :]
        QK = sb("QK", 6144)[:, :]
        CST = sb("CST", C_END)[:, :]
        JV = sb("JV", 1024)[:, :]
        ONES = sb("ONES", 128)[:, :]
        CREP = sb("CREP", 3 * 128)[:, :].rearrange("p (k m) -> p k m", k=3)
        ACC = sb("ACC", 1024)[:, :].rearrange("p (b n) -> p b n", b=2)
        DG = sb("DG", 4 * 128)[:, :].rearrange("p (b n) -> p b n", b=4)
        SC = sb("SC", 512)[:, :]
        GATE = sb("GATE", 256)[:, :]
        AV = sb("AV", 256)[:, :]
        AG = sb("AG", 256)[:, :]
        EID = sb("EID", 256, I32)[:, :]
        TV = sb("TV", 2 * 64)[:, :]
        TI = sb("TI", 2 * 64, U32)[:, :]
        TC = sb("TC", 256)[:, :]
        RNG = sb("RNG", SLOTS * SLOT)[:, :]
        PS = ctx.enter_context(nc.psum_tensor("PS", [128, 8, 512], F32))

        pe, act, dve, pool, sp = (Engine(sem("s_" + n), n in ("act", "dve")) for n in ("pe", "act", "dve", "pool", "sp"))
        ld = [sem(f"ld{u}") for u in range(SLOTS)]
        ga = [sem(f"ga{u}") for u in range(SLOTS)]
        s_par, s_mod, s_x, s_out = sem("s_par"), sem("s_mod"), sem("s_x"), sem("s_out")
        s_md, s_row = sem("s_md"), sem("s_row")

        ident = CST[:, C_ID:C_ID + 128]

        slots = dict(free=[(u, []) for u in range(SLOTS)], n={})

        class Item:
            def __init__(self):
                self.u, self.waits = slots["free"].pop(0)
                self.ap = RNG[:, self.u * SLOT:(self.u + 1) * SLOT]

            def count(self, sem):
                slots["n"][id(sem)] = slots["n"].get(id(sem), 0) + 16
                return sem, slots["n"][id(sem)]

            def release(self, *toks):
                slots["free"].append((self.u, list(toks)))

        def load(src, n):
            it = Item()
            dst = it.ap[:, 0:n]
            it.tok = sp.dma(it.waits, lambda e: e.dma_start(dst, src), *it.count(ld[it.u]))
            it.ap = dst
            return it

        def stream(srcs):
            todo, under = list(srcs), []
            while todo or under:
                while todo and len(under) < 1 + AHEAD:
                    under.append(load(*todo.pop(0)))
                yield under.pop(0)

        bank = dict(free=[[] for _ in range(8)], next=0, pair=0, pairs=(2,))

        def single():
            b = 4 + bank["next"] % 4
            bank["next"] += 1
            return b, bank["free"][b]

        turn = dict(n=0, sc=0)

        def evac(dst, src, waits, scale=1.0):
            turn["n"] += 1
            if turn["n"] % 2:
                return act(waits, lambda e: e.activation(dst, src, ACT.Copy, scale=scale))
            if scale == 1.0:
                return dve(waits, lambda e: e.tensor_copy(dst, src))
            return dve(waits, lambda e: e.tensor_scalar(dst, src, scale, None, ALU.mult))

        def scratch(n):
            if turn["sc"] % 512 + n > 512:
                turn["sc"] += 512 - turn["sc"] % 512
            c = turn["sc"] % 512
            turn["sc"] += n
            return SC[:, c:c + n]

        def tt(dst, a, b, op, waits):
            return dve(waits, lambda e: e.tensor_tensor(dst, a, b, op))

        def stt(dst, a, s, b, op0, op1, waits):
            return dve(waits, lambda e: e.scalar_tensor_tensor(out=dst, in0=a, scalar=s, in1=b, op0=op0, op1=op1))

        def ts(dst, a, s1, s2, op0, op1, waits):
            if op1 is None:
                return dve(waits, lambda e: e.tensor_scalar(dst, a, s1, None, op0))
            return dve(waits, lambda e: e.tensor_scalar(dst, a, s1, s2, op0, op1))

        def mm(dst, a, b, start, stop_, waits=()):
            return pe(waits, lambda e: e.matmul(dst, a, b, start=start, stop=stop_))

        t_cst = sp.dma([], lambda e: e.dma_start(CST, I["cst"]), s_x, 16)
        COND = scratch(24)
        t_c = sp.dma([t_cst], lambda e: e.dma_start(COND[:, 0:8], I["cT"]), s_x, 32)
        t_x = sp.dma([t_c], lambda e: e.dma_start(X, I["x"].rearrange("(t p) d -> p t d", p=128)), s_x, 48)
        EPSC = sb("EPSC", 1)[:, :]
        SKB = sb("SKB", 256)[:, :]
        BB = ACC.rearrange("p b n -> p (b n)")
        s_bb = sem("s_bb")
        s_row2 = [sem("s_row0"), sem("s_row1")]
        s_sk = sem("s_sk")
        t_one = dve([], lambda e: e.memset(ONES, 1.0))
        t_eps = dve([], lambda e: e.memset(EPSC, EPS))
        k1 = act([t_c], lambda e: e.activation(COND[:, 8:16], COND[:, 0:8], ACT.Exp, scale=-1.0))
        k1 = ts(COND[:, 8:16], COND[:, 8:16], 1.0, None, ALU.add, None, [k1])
        k1 = dve([k1], lambda e: e.reciprocal(COND[:, 8:16], COND[:, 8:16]))
        t_cond = tt(COND[:, 16:24], COND[:, 0:8], COND[:, 8:16], ALU.mult, [k1])
        t_rep = None
        for k in range(3):
            src = COND[:, 21 + k:22 + k]
            dst = CREP[:, k, :]
            t_rep = dve([t_cond], lambda e, dst=dst, src=src: e.tensor_copy(dst, bc(src, [128, 128])))

        st = dict(x=[[t_x], [t_x]], par=[], mod=[], ht=[], h=[[], []], prj=[], qa=[], qb=[], grp=[[], []], acc=[[], []],
                  npar=0, nmod=0, row=[[], []], gi=0, dg=[[] for _ in range(4)], dn=0, tv=[[], []], tn=0)

        def load_par(src, n):
            st["npar"] += 16
            t = sp.dma(st["par"], lambda e: e.dma_start(PARB[:, 0:n], src.partition_broadcast(128)), s_par, st["npar"])
            st["par"] = []
            return t

        def ada(l):
            if l == 0:
                tb = sp.dma([], lambda e: e.dma_start(MOD, I["bada"][0][0:5120].partition_broadcast(128)), s_mod, 16)
                tb2 = sp.dma([tb], lambda e: e.dma_start(G2[:, 0:1024], I["bada"][0][5120:6144].partition_broadcast(128)),
                             s_mod, 32)
            else:
                tb2 = None
            ws = stream([(I["wada"][l * 24 + b], 2048) for b in range(24)])
            done = []
            for b in range(24):
                w = next(ws)
                wv = w.ap.rearrange("p (k n) -> p k n", k=8)
                a = ACC[:, b % 2, 0:256]
                t = ts(a, wv[:, 0, :], COND[:, 16:17], None, ALU.mult, None, [w.tok, t_cond, st["acc"][b % 2]])
                for k in range(1, 5):
                    t = stt(a, wv[:, k, :], COND[:, 16 + k:17 + k], a, ALU.mult, ALU.add, [t])
                yield
                bk, fr = single()
                for k in range(3):
                    mm(PS[:, bk, 0:256], CREP[:, k, :], wv[:, 5 + k, :], k == 0, False, [w.tok, t_rep, fr])
                p = mm(PS[:, bk, 0:256], ONES, a, False, True, [t, t_one])
                w.release(p, t)
                st["acc"][b % 2] = [p]
                yield
                if l == 0:
                    m = MOD[:, b * 256:(b + 1) * 256] if b < 20 else G2[:, (b - 20) * 256:(b - 19) * 256]
                    t = tt(m, PS[:, bk, 0:256], m, ALU.add, [p, tb2])
                else:
                    m = ACC[0:1, b % 2, 256:512]
                    t = act([p, st["row"][b % 2]], lambda e, m=m, bk=bk: e.activation(m, PS[0:1, bk, 0:256], ACT.Copy))
                    dr = I["modd"][0:1, b * 256:(b + 1) * 256]
                    d = sp.dma([t], lambda e, m=m, dr=dr: e.dma_start(dr, m), s_row2[b % 2], 16 * (b // 2 + 1))
                    st["row"][b % 2] = [d]
                bank["free"][bk] = [t]
            st["ada"] = [t] if l == 0 else st["row"][0] + st["row"][1]

        def rstd(srcs, D, waits):
            n = len(srcs)
            s = scratch(n)
            last = []
            for i, a in enumerate(srcs):
                w = a.shape[-1]
                last = act([waits[i], st.get("jv", [])], lambda e, a=a, i=i, w=w: e.activation(
                    JV[:, 0:w], a, ACT.Square, accum_out=s[:, i:i + 1]))
                st["jv"] = []
            st["jva"] = [last]
            t = act([last, t_eps], lambda e: e.activation(s, s, ACT.Sqrt, bias=EPSC, scale=1.0 / D))
            t = dve([t], lambda e: e.reciprocal(s, s))
            return s, t

        def transpose_tm(src, dst, waits, free):
            out = []
            for t in range(2):
                for c4 in range(2):
                    bk, fr = single()
                    for c in range(4):
                        a = src[:, t, (c4 * 4 + c) * 128:(c4 * 4 + c + 1) * 128]
                        d = PS[:, bk, c * 128:(c + 1) * 128]
                        p = pe([waits[t], fr, t_cst], lambda e, a=a, d=d: e.transpose(d, a, ident))
                    v = evac(dst[:, c4 * 4:c4 * 4 + 4, t * 128:(t + 1) * 128],
                             PS[:, bk, :].rearrange("p (c s) -> p c s", c=4), [p, free])
                    bank["free"][bk] = [v]
                    out.append(v)
            return out, p

        def norm(g, b, waits):
            s, ts_ = rstd([X[:, 0, :], X[:, 1, :]], 1024.0, [st["x"][0], st["x"][1]])
            hs = []
            for t in range(2):
                k = stt(H[:, t, :], X[:, t, :], s[:, t:t + 1], g, ALU.mult, ALU.mult, [ts_, waits, st["h"][t]])
                if b is not None:
                    k = tt(H[:, t, :], H[:, t, :], b, ALU.add, [k])
                hs.append(k)
            toks, last = transpose_tm(H, HT, hs, st["ht"])
            st["ht"] = []
            st["h"] = [[last], [last]]
            return toks, hs

        def tokens_by(hT, w, width, t, k8, waits, fr, bk):
            wv = w.ap.rearrange("p (k n) -> p k n", k=k8)
            for k in range(k8):
                p = mm(PS[:, bk, 0:width], hT[:, k, t * 128:(t + 1) * 128], wv[:, k, :], k == 0, k == k8 - 1,
                       [w.tok, waits, fr])
            return p

        def residual(items, hT, waits):
            for j, w in enumerate(items):
                for t in range(2):
                    bk, fr = single()
                    p = tokens_by(hT, w, 256, t, 8, waits, fr, bk)
                    xs = X[:, t, j * 256:(j + 1) * 256]
                    v = tt(xs, PS[:, bk, 0:256], xs, ALU.add, [p, st["x"][t]])
                    bank["free"][bk] = [v]
                    st["x"][t] = [v]
                w.release(p)
            st["ht"] = [p]

        def heads_T(dst, srcs, d, t, waits, free, scale=1.0):
            out = []
            for i in range(0, len(srcs), 4):
                part = srcs[i:i + 4]
                bk, fr = single()
                for j, a in enumerate(part):
                    dd = PS[0:d, bk, j * 128:(j + 1) * 128]
                    p = pe([waits, fr, t_cst], lambda e, a=a, dd=dd: e.transpose(dd, a, ident))
                v = evac(dst[0:d, i:i + len(part), t * 128:(t + 1) * 128],
                         PS[0:d, bk, 0:len(part) * 128].rearrange("p (j s) -> p j s", j=len(part)), [p, free], scale)
                bank["free"][bk] = [v]
                out.append(v)
            return out, p

        def group(t, maps, keys, scale, waits, Y, ycol, res, bias=None, sink=None, lam=None):
            n, g = len(maps), st["gi"] % 2
            st["gi"] += 1
            nk = keys // 128
            P = GRP[:, g * 2048:g * 2048 + 1024].rearrange("p (i k) -> p i k", i=4)[:, 0:n, 0:keys]
            PT = GRP[:, g * 2048 + 1024:(g + 1) * 2048]
            b0 = bank["pairs"][bank["pair"] % len(bank["pairs"])]
            bank["pair"] += 1
            sc = PS[:, b0:b0 + 2, :].rearrange("p b (i k) -> p (b i) k", i=2)[:, 0:n, 0:keys]
            fr = [bank["free"][b0], bank["free"][b0 + 1]]
            for i, m in enumerate(maps):
                p = mm(sc[:, i, :], m[0], m[1][:, 0:keys], True, True, [waits, fr])
            yield
            src, ready, pfree = sc, p, st["grp"][g]
            if bias is not None:
                ready = bias(P, sc, [p, pfree])
                src, pfree = P, []
                bank["free"][b0] = bank["free"][b0 + 1] = [ready]
            w = scratch(4 * n)
            mx, ng, rs, rd = (w[:, j * n:(j + 1) * n] for j in range(4))
            k = dve([ready], lambda e: e.reduce_max(mx, src, AX))
            if sink is not None:
                k = tt(mx, mx, sink, ALU.max, [k])
            k = ts(ng, mx, -scale, None, ALU.mult, None, [k])
            for i in range(n):
                a = act([k, pfree], lambda e, i=i: e.activation(P[:, i, :], src[:, i, :], ACT.Exp, bias=ng[:, i:i + 1],
                                                                scale=scale, accum_out=rs[:, i:i + 1]))
            if bias is None:
                bank["free"][b0] = bank["free"][b0 + 1] = [a]
            if sink is not None:
                k = tt(mx, sink, mx, ALU.subtract, [k])
                e1 = act([k], lambda e: e.activation(mx, mx, ACT.Exp))
            yield
            ls = a
            if sink is not None:
                ls = tt(rs, rs, mx, ALU.add, [e1, a])
            r = dve([ls], lambda e: e.reciprocal(rd, rs))
            no, PO = n, P
            if lam is not None:
                no = n // 2
                k = r
                for i in range(no):
                    k0 = ts(P[:, 2 * i + 1, :], P[:, 2 * i + 1, :], rd[:, 2 * i + 1:2 * i + 2], lam, ALU.mult, ALU.mult, [k])
                    k = stt(P[:, 2 * i, :], P[:, 2 * i, :], rd[:, 2 * i:2 * i + 1], P[:, 2 * i + 1, :],
                            ALU.mult, ALU.subtract, [k0])
                a = k
                maps, PO = maps[::2], P[:, 0:n:2, :]
            pts = []
            total = no * nk
            for j0 in range(0, total, 4):
                m4 = min(4, total - j0)
                bk, fr = single()
                for j in range(m4):
                    i, kc = divmod(j0 + j, nk)
                    s_, d_ = PO[:, i, kc * 128:(kc + 1) * 128], PS[:, bk, j * 128:(j + 1) * 128]
                    p = pe([a, fr], lambda e, s_=s_, d_=d_: e.transpose(d_, s_, ident))
                v = evac(PT[:, j0 * 128:(j0 + m4) * 128], PS[:, bk, 0:m4 * 128], [p, pfree, st["grp"][g]])
                bank["free"][bk] = [v]
                pts.append(v)
            yield
            bk, fr = single()
            for i, m in enumerate(maps):
                for kc in range(nk):
                    j = i * nk + kc
                    p = mm(PS[:, bk, i * 64:(i + 1) * 64], PT[:, j * 128:(j + 1) * 128], m[2](kc), kc == 0, kc == nk - 1,
                           [pts[j // 4], fr])
            st["grp"][g] = [p]
            yield
            o = PS[:, bk, 0:no * 64]
            if lam is not None:
                v = dve([p, st["yfree"]], lambda e: e.tensor_copy(Y[:, t, ycol:ycol + no * 64], o))
            else:
                yv = Y[:, t, ycol:ycol + no * 64].rearrange("p (i d) -> p i d", i=no)
                v = tt(yv, o.rearrange("p (i d) -> p i d", i=no), bc(rd.unsqueeze(2), [128, no, 64]), ALU.mult,
                       [p, r, st["yfree"]])
            bank["free"][bk] = [v]
            res.append((v, p))

        def overlapped(gens, wide=2):
            live, todo = [], list(gens)
            while live or todo:
                if todo and len(live) < 2:
                    live.append(todo.pop(0))
                for g in list(live):
                    if next(g, 0) == 0:
                        live.remove(g)
                yield

        def run(gen):
            for _ in gen:
                pass

        kT = QK[:, 0:512].rearrange("p (i s) -> p i s", i=2)
        qT = QK[:, 512:1536].rearrange("p (i s) -> p i s", i=8)
        plT = QK[:, 1536:2048].rearrange("p (g s) -> p g s", g=4)
        JS = QK[:, 2048:3072]
        JD = QK[:, 3072:4096]
        HALF = QK[:, 4096:4608].rearrange("p (b i s) -> p b i s", b=2, i=2)
        S = QK[:, 4608:5120].rearrange("p (b i s) -> p b i s", b=2, i=2)
        st.update(kt=[[], []], qt=[], pl=[], half=[[], []], s=[[], []], pj=[[], []], hfree=[[], []], htf=[[], []])
        st.update(eid=[[], []])

        def norm1t(t, g, b, waits):
            s, tr = rstd([X[:, t, :]], 1024.0, [st["x"][t]])
            yield
            k = stt(H[:, t, :], X[:, t, :], s[:, 0:1], g, ALU.mult, ALU.mult, [tr, waits, st["hfree"][t]])
            hs = tt(H[:, t, :], H[:, t, :], b, ALU.add, [k])
            yield
            yield from transposed(t, hs)

        def transposed(t, hs):
            out = []
            for c4 in range(2):
                bk, fr = single()
                for c in range(4):
                    a = H[:, t, (c4 * 4 + c) * 128:(c4 * 4 + c + 1) * 128]
                    d = PS[:, bk, c * 128:(c + 1) * 128]
                    p = pe([hs, fr, t_cst], lambda e, a=a, d=d: e.transpose(d, a, ident))
                v = evac(HT[:, c4 * 4:c4 * 4 + 4, t * 128:(t + 1) * 128],
                         PS[:, bk, :].rearrange("p (c s) -> p c s", c=4), [p, st["htf"][t]])
                bank["free"][bk] = [v]
                out.append(v)
                yield
            st["hfree"][t] = [p]
            st["htf"][t] = []
            st["hready"], st["htready"] = hs, out

        def mix(l, t, tk):
            c = lambda k: PARB[:, P1[k][0]:P1[k][0] + P1[k][1]]
            sh1, sc1, g1, sh2, sc2 = (MOD[:, i * 1024:(i + 1) * 1024] for i in range(5))
            if t == 0:
                tp = load_par(I["par1"][l], PAR)
                st["skn"] = st.get("skn", 0) + 16
                st["sk"] = sp.dma([st.get("skf", [])], lambda e: e.dma_start(SKB, I["skT"][l]), s_sk, st["skn"])
                if l > 0:
                    t1 = sp.dma([st["ada"], st["modf"]], lambda e: e.dma_start(
                        MOD, I["modd"][0, 0:5120].partition_broadcast(128)), s_md, 16)
                    t2 = sp.dma([t1], lambda e: e.dma_start(
                        G2[:, 1024:2048], I["modd"][0, 5120:6144].partition_broadcast(128)), s_md, 32)
                    t3 = t2
                    for a0 in range(0, 6144, 1024):
                        m = MOD[:, a0:a0 + 1024] if a0 < 5120 else G2[:, 1024:2048]
                        src = I["bada"][1][a0:a0 + 1024]
                        t3 = sp.dma([t3, st["bf"]], lambda e, src=src: e.dma_start(
                            BB, src.partition_broadcast(128)), s_bb, 16 * (a0 // 1024 + 1))
                        st["bf"] = [tt(m, m, BB, ALU.add, [t3, t2])]
                        yield
                    st["ada"] = st["bf"]
                m1 = stt(sc1, sc1, 1.0, c("n1"), ALU.add, ALU.mult, [st["ada"], tp])
                m2 = stt(sc2, sc2, 1.0, c("n2"), ALU.add, ALU.mult, [st["ada"], tp])
                st["m"] = [m1, m2, tp]
                st["tp"] = tp
                yield
            tp = st["tp"]
            ws = stream([(I["win1"][l * 5 + j], 2048) for j in range(5)] + [(I[f"mg{t}"], 512 * (t + 1)), (I["poolw"][l], 512)])
            prj = PRJ.rearrange("p (t n) -> p t n", t=2)
            yield from norm1t(t, sc1, sh1, st["m"])
            hts = st["htready"]
            pj = [None] * 5
            for j in range(5):
                w = next(ws)
                bk, fr = single()
                p = tokens_by(HT, w, 256, t, 8, hts, fr, bk)
                yield
                v = evac(prj[:, t, j * 256:(j + 1) * 256], PS[:, bk, 0:256], [p, st["prj"]])
                bank["free"][bk] = [v]
                pj[j] = v
                w.release(p)
            st["htf"][t] = [p]
            st["pj"][t] = [pj[0], pj[1]]
            sq = JD[:, 0:640].rearrange("p (i d) -> p i d", i=10)
            v = prj[:, t, 512:1152].rearrange("p (i d) -> p i d", i=10)
            k = tt(sq, v, v, ALU.mult, [pj])
            s = scratch(10)
            k = dve([k], lambda e, s=s, sq=sq: e.reduce_sum(s, sq, AX))
            k = act([k, t_eps], lambda e, s=s: e.activation(s, s, ACT.Sqrt, bias=EPSC, scale=1.0 / 64))
            yield
            k = dve([k], lambda e, s=s: e.reciprocal(s, s))
            k = tt(v, v, bc(s.unsqueeze(2), [128, 10, 64]), ALU.mult, [k])
            k1 = tt(v[:, 0:8, :], v[:, 0:8, :], bc(c("qg").unsqueeze(1), [128, 8, 64]), ALU.mult, [k, tp])
            k2 = tt(v[:, 8:10, :], v[:, 8:10, :], bc(c("kg").unsqueeze(1), [128, 2, 64]), ALU.mult, [k, tp])
            yield
            mg, pw = next(ws), next(ws)
            mgv = mg.ap.rearrange("p (a g s) -> p a g s", a=t + 1, g=4)
            bk, fr = single()
            for g in range(4):
                for a in range(t + 1):
                    p = mm(PS[:, bk, g * 128:(g + 1) * 128], prj[:, a, g * 128:(g + 1) * 128], mgv[:, a, g, :],
                           a == 0, a == t, [st["pj"], mg.tok, fr])
            pt = evac(plT, PS[:, bk, :].rearrange("p (g s) -> p g s", g=4), [p, st["pl"]])
            bank["free"][bk] = [pt]
            mg.release(p)
            yield
            a, _ = heads_T1(qT, [v[:, i, :] for i in range(8)], 0, [k1], st["qt"], 0.125)
            b, _ = heads_T1(kT, [v[:, i, :] for i in range(8, 10)], t, [k2], st["kt"], 1.0)
            qd = a + b + st["kt"]
            yield
            st["yfree"] = [st["hfree"][t]]
            bk, fr = single()
            for g in range(4):
                p = mm(PS[:, bk, g * 128:(g + 1) * 128], plT[:, g, :], pw.ap[:, g * 128:(g + 1) * 128], True, True,
                       [pt, pw.tok, fr])
            pw.release(p)
            st["pl"] = [p]
            yield
            v = tt(H[:, t, 0:512], PS[:, bk, :], c("ps"), ALU.mult, [p, st["yfree"], tp])
            bank["free"][bk] = [v]
            ym = [v]
            res, groups = [], []
            for hg in range(2):
                nd = CST[:, C_ND + t * 256:C_ND + (t + 1) * 256]

                def bias(P, sc, waits, hg=hg, nd=nd):
                    for i in range(4):
                        k = stt(P[:, i, :], nd[:, 0:(t + 1) * 128], 2.0 ** -(hg * 4 + i + 1), sc[:, i, :],
                                ALU.mult, ALU.add, waits)
                    return k
                maps = [(qT[0:64, hg * 4 + i, :], kT[0:64, hg, :],
                         lambda kc, hg=hg: prj[:, kc, 1152 + hg * 64:1152 + (hg + 1) * 64]) for i in range(4)]
                groups.append(group(t, maps, (t + 1) * 128, 1.0, [qd, tp], H, 512 + hg * 256, res, bias=bias,
                                    sink=c("sink")[:, hg * 4:hg * 4 + 4]))
            yield from overlapped(groups)
            ym += [v for v, _ in res]
            lastp = res[-1][1]
            st["qt"], st["kt"] = [lastp], [lastp]
            if t == 1:
                st["prj"] = [lastp]
            ws = stream([(I["wout1"][l * 4 + j], 2048) for j in range(4)])
            s, tr = rstd([H[:, t, j * 512:(j + 1) * 512] for j in range(2)], 512.0, [ym, ym])
            yield
            for j in range(2):
                yy = H[:, t, j * 512:(j + 1) * 512]
                k = stt(yy, yy, s[:, j:j + 1], c("mg")[:, j * 512:(j + 1) * 512], ALU.mult, ALU.mult, [tr, tp])
            yield
            yield from transposed(t, k)
            yt = st["htready"]
            for j in range(4):
                w = next(ws)
                bk, fr = single()
                p = tokens_by(HT, w, 256, t, 8, yt, fr, bk)
                w.release(p)
                yield
                xs = X[:, t, j * 256:(j + 1) * 256]
                k = tt(JD[:, 0:256], PS[:, bk, 0:256], g1[:, j * 256:(j + 1) * 256], ALU.mult, [p])
                v = tt(xs, JD[:, 0:256], xs, ALU.add, [k, st["x"][t]])
                bank["free"][bk] = [v]
            st["x"][t] = [v]
            st["htf"][t] = [p]
            ws = stream([(I["wq"][l * 8 + j], 2048) for j in range(8)])
            yield from norm1t(t, sc2, sh2, st["m"])
            hts = st["htready"]
            st["h2"][t] = [st["hready"]]
            if t == 1:
                st["par"] = [st["hready"], v]
                st["modf"] = [st["hready"]]
            skv = SKB.rearrange("p (a n) -> p a n", a=2)
            for h in range(8):
                w = next(ws)
                wv = w.ap.rearrange("p (k n) -> p k n", k=8)
                bk, fr = single()
                for i in range(2):
                    for k in range(8):
                        p = mm(PS[:, bk, i * 128:(i + 1) * 128], wv[:, k, i * 128:(i + 1) * 128],
                               HT[:, k, t * 128:(t + 1) * 128], k == 0, k == 7, [w.tok, hts, fr])
                w.release(p)
                yield
                half, u = HALF[:, h % 2], h % 2
                v = act([p, st["half"][u]], lambda e, half=half, bk=bk: e.activation(
                    half, PS[:, bk, 0:256].rearrange("p (i s) -> p i s", i=2), ACT.Copy))
                bank["free"][bk] = [v]
                bk, fr = single()
                for i in range(2):
                    p = mm(PS[:, bk, i * 128:(i + 1) * 128], half[:, i, :], skv[:, i, :], True, True, [v, st["sk"], fr])
                st["half"][u] = [p]
                yield
                v = act([p, st["s"][u]], lambda e, u=u, bk=bk: e.activation(
                    S[:, u], PS[:, bk, 0:256].rearrange("p (i s) -> p i s", i=2), ACT.Copy))
                bank["free"][bk] = [v]
                yield from topk(t, h, S[:, u], v, tk)
                yield
            st["htf"][t] = [p]
            st["skf"] = [p]

        def heads_T1(dst, srcs, t, waits, free, scale):
            out = []
            for i in range(0, len(srcs), 4):
                part = srcs[i:i + 4]
                bk, fr = single()
                for j, a in enumerate(part):
                    dd = PS[0:64, bk, j * 128:(j + 1) * 128]
                    p = pe([waits, fr, t_cst], lambda e, a=a, dd=dd: e.transpose(dd, a, ident))
                v = evac(dst[0:64, i:i + len(part), t * 128:(t + 1) * 128],
                         PS[0:64, bk, 0:len(part) * 128].rearrange("p (j s) -> p j s", j=len(part)), [p, free], scale)
                bank["free"][bk] = [v]
                out.append(v)
            return out, p

        def vmax(dst, src, waits):
            return dve(waits, lambda e: e.max(dst, src))

        def vindex(dst, top, src, waits):
            return dve(waits, lambda e: e.max_index(dst, top, src))

        def vreplace(dst, top, src, waits):
            return dve(waits, lambda e: e.match_replace(dst, top, src, TINY))

        def topk(t, h, S, ready, tk):
            u = st["tn"] % 2
            st["tn"] += 1
            V, Ix = TV[:, u * 64:(u + 1) * 64], TI[:, u * 64:(u + 1) * 64]
            k = None
            for p in range(2):
                s, js = S[:, p, :], JS[:, p * 128:p * 128 + 128]
                v, ix = V[:, p * 16:p * 16 + 16], Ix[:, p * 16:p * 16 + 16]
                k = vmax(v[:, 0:8], s, [ready, st["tv"][u]])
                vindex(ix[:, 0:8], v[:, 0:8], s, [k])
                k = vreplace(js, v[:, 0:8], s, [k])
                k = vmax(v[:, 8:16], js, [k])
                k = vindex(ix[:, 8:16], v[:, 8:16], js, [k])
                yield
            st["s"][h % 2] = [k]
            cd = TC[:, 0:256]
            cv = cd.rearrange("p (a b) -> p a b", a=16)
            k1 = tt(cv, bc(V[:, 0:16].unsqueeze(2), [128, 16, 16]), bc(V[:, 16:32].unsqueeze(1), [128, 16, 16]), ALU.add, [k])
            v, ix = V[:, 32:48], Ix[:, 32:48]
            k2 = vmax(v[:, 0:8], cd, [k1])
            k3 = vindex(ix[:, 0:8], v[:, 0:8], cd, [k2])
            k4 = vreplace(JS[:, 0:256], v[:, 0:8], cd, [k2])
            k5 = vmax(v[:, 8:16], JS[:, 0:256], [k4])
            k6 = vindex(ix[:, 8:16], v[:, 8:16], JS[:, 0:256], [k5])
            yield
            j = (t * 8 + h) * 16
            ng = V[:, 48:49]
            n1 = ts(ng, v[:, 0:1], -1.0, None, ALU.mult, None, [k2])
            ga_ = GATE[:, j:j + 16]
            a = act([n1, k5, st["gate"][t]], lambda e: e.activation(ga_, v, ACT.Exp, bias=ng, scale=1.0, accum_out=V[:, 49:50]))
            q = ts(Ix[:, 48:64], ix, 4, None, ALU.logical_shift_right, None, [k6, k3])
            q2 = ts(ix, ix, 15, None, ALU.bitwise_and, None, [q])
            JF = JS[:, 256:288]
            c1 = dve([q], lambda e: e.tensor_copy(JF[:, 0:16], Ix[:, 48:64]))
            c2 = dve([q2], lambda e: e.tensor_copy(JF[:, 16:32], ix))
            c3 = dve([k], lambda e: e.tensor_copy(JS[:, 288:320], Ix[:, 0:32]))
            oh = JS[:, 512:1024].rearrange("p (a k m) -> p a k m", a=2, k=16)
            for z in range(2):
                c4 = tt(oh[:, z], bc(JF[:, z * 16:z * 16 + 16].unsqueeze(2), [128, 16, 16]),
                        bc(CST[:, C_IOTA:C_IOTA + 16].unsqueeze(1), [128, 16, 16]), ALU.is_equal, [c1, c2])
                c4 = tt(oh[:, z], oh[:, z], bc(JS[:, 288 + z * 16:304 + z * 16].unsqueeze(1), [128, 16, 16]),
                        ALU.mult, [c4, c3])
            sel = JS[:, 320:352]
            c5 = dve([c4], lambda e: e.reduce_sum(sel, JS[:, 512:1024].rearrange("p (k m) -> p k m", m=16), AX))
            eid = EID[:, j:j + 16]
            c6 = stt(eid, sel[:, 0:16], 128.0, sel[:, 16:32], ALU.mult, ALU.add, [c5, st["eid"][t]])
            r = dve([a], lambda e: e.reciprocal(V[:, 50:51], V[:, 49:50]))
            g = ts(ga_, ga_, V[:, 50:51], None, ALU.mult, None, [r])
            st["tv"][u] = [g]
            tk.append((c6, g))

        st.update(h2=[[], []], gate=[[], []], ada=[], modf=[], bf=[])

        def experts(l, t, tk, own, behind, rate):
            owed = 0.0
            j1 = t * 128
            pend = []

            def finish(its, j0):
                a = act([its[-1].dot], lambda e: e.activation(AG[:, j0:j0 + BATCH], AV[:, j0:j0 + BATCH], ACT.Gelu))
                k = tt(AG[:, j0:j0 + BATCH], AG[:, j0:j0 + BATCH], GATE[:, j0:j0 + BATCH], ALU.mult, [a, its[-1].tg])
                for q, x in enumerate(its):
                    d = st["dn"] % 4
                    st["dn"] += 1
                    jj = j0 + q
                    z = act([k, st["dg"][d], t_cst], lambda e, d=d, jj=jj: e.activation(
                        DG[:, d, :], ident, ACT.Copy, scale=AG[:, jj:jj + 1]))
                    for hf in range(2):
                        p = mm(PS[:, hf, :], DG[:, d, :], x.ap[:, 1024 + hf * 512:1536 + hf * 512],
                               jj == j1, jj == j1 + 127, [z, x.tok, bank["free"][hf]])
                    st["dg"][d] = [p]
                    x.release(p, x.dot)
                return k, p, x.tok

            for b in range(128 // BATCH):
                h = b * BATCH // 16
                while len(tk) <= h:
                    next(own)
                te, tg = tk[h]
                its = []
                for q in range(BATCH):
                    j = j1 + b * BATCH + q
                    it = Item()
                    it.tok = pool.dma([it.waits, te], lambda e, it=it, j=j: e.indirect_dma_start(
                        out=it.ap, out_offset=None, in_=I[f"uv{l}"],
                        in_offset=bass.IndirectOffsetOnAxis(ap=EID[:, j:j + 1], axis=0)), *it.count(ga[it.u]))
                    it.tg = tg
                    its.append(it)
                for q, x in enumerate(its):
                    j = j1 + b * BATCH + q
                    x.dot = dve([x.tok, st["h2"][t]], lambda e, x=x, j=j: e.tensor_tensor_reduce(
                        out=JD, in0=x.ap[:, 0:1024], in1=H[:, t, :], scale=1.0, scalar=0.0,
                        op0=ALU.mult, op1=ALU.add, accum_out=AV[:, j:j + 1]))
                k, p, lt = finish(its, j1 + b * BATCH)
                if len(tk) < 8:
                    next(own)
                if len(tk) == 8:
                    run(own)
                owed += rate
                while owed >= 1 and behind is not None and len(tk) >= 8:
                    owed -= 1
                    next(behind, None)
                if len(tk) < 8:
                    owed = 0.0
            g2 = G2[:, l * 1024:(l + 1) * 1024]
            for hf in range(2):
                xs = X[:, t, hf * 512:(hf + 1) * 512]
                k2 = tt(JD[:, 0:512], PS[:, hf, :], g2[:, hf * 512:(hf + 1) * 512], ALU.mult, [p, st["ada"]])
                v = tt(xs, JD[:, 0:512], xs, ALU.add, [k2, st["x"][t]])
                bank["free"][hf] = [v]
            st["x"][t] = [v]
            st["hfree"][t] = [v]
            st["eid"][t], st["gate"][t] = [lt], [k]
            st["htf"][t] = st["htf"][t]

        def rope(dst, src, n, half, tab, tmp, waits):
            cc = tab[:, 0:2 * half].rearrange("p (a b) -> p a b", a=2)
            ss = tab[:, 2 * half:4 * half].rearrange("p (a b) -> p a b", a=2)
            for z in range(2):
                c = bc(cc[:, z, :].unsqueeze(1), [128, n, half])
                k = tt(dst[:, :, z, :], src[:, :, z, :], c, ALU.mult, waits)
                s = bc(ss[:, z, :].unsqueeze(1), [128, n, half])
                k = tt(tmp[:, :, z, :], src[:, :, 1 - z, :], s, ALU.mult, waits)
            for z in range(2):
                k = tt(dst[:, :, z, :], dst[:, :, z, :], tmp[:, :, z, :], ALU.add, [k])
            return k

        def block2(l, tp):
            c = lambda k: PARB[:, P2[k][0]:P2[k][0] + P2[k][1]]
            lam0 = 0.8 - 0.6 * math.exp(-0.3 * l)
            prj = MOD[:, 0:4800].rearrange("p (t n) -> p t n", t=2)
            hts, _ = norm(c("n1"), None, [tp])
            pj = [[], []]
            for j in range(10):
                w = load(I["win2"][l * 10 + j], 1920)
                for t in range(2):
                    bk, fr = single()
                    p = tokens_by(HT, w, 240, t, 8, hts, fr, bk)
                    v = evac(prj[:, t, j * 240:(j + 1) * 240], PS[:, bk, 0:240], [p, st["mod"]])
                    bank["free"][bk] = [v]
                    pj[t].append(v)
                w.release(p)
            st["ht"] = [p]
            Y = H
            st["yfree"] = [st["h"][0], st["h"][1]]
            A = QK[:, 0:2048].rearrange("p (i s) -> p i s", i=8)
            B = QK[:, 2048:6144].rearrange("p (i s) -> p i s", i=16)
            rp = lambda t: CST[:, C_ROPE + t * 192:C_ROPE + (t + 1) * 192]
            ls = scratch(8)
            for z in range(2):
                lq = c("lam")[:, z * 64:z * 64 + 32]
                lk = c("lam")[:, z * 64 + 32:z * 64 + 64]
                k = dve([tp, st.get("jva", [])], lambda e, lq=lq, lk=lk, z=z: e.tensor_tensor_reduce(
                    out=JV[:, 0:32], in0=lq, in1=lk, scale=1.0, scalar=0.0, op0=ALU.mult, op1=ALU.add,
                    accum_out=ls[:, z:z + 1]))
            st["jv"] = [k]
            k = act([k], lambda e: e.activation(ls[:, 2:4], ls[:, 0:2], ACT.Exp))
            tlam = stt(ls[:, 4:5], ls[:, 2:3], lam0, ls[:, 3:4], ALU.add, ALU.subtract, [k])
            lam = ls[:, 4:5]
            wu = load(I["wuq"][l], 768)
            wk = load(I["wukv"][l], 512)
            KVB = PRJ[:, 0:1024].rearrange("p (t n) -> p t n", t=2)
            QF = PRJ[:, 1024:1792].rearrange("p (t n) -> p t n", t=2)
            TMP = PRJ[:, 1792:2560]
            tmpf = st["prj"]
            kv_t, qd = [], []
            lastqk = []
            for t in range(2):
                s, tr = rstd([prj[:, t, X_CQ:X_CQ + 192]], 192.0, [[pj[t]]])
                k1 = stt(prj[:, t, X_CQ:X_CQ + 192], prj[:, t, X_CQ:X_CQ + 192], s[:, 0:1], c("q"), ALU.mult, ALU.mult,
                         [tr, tp])
                s2, tr2 = rstd([prj[:, t, X_CKV:X_CKV + 128]], 128.0, [[pj[t]]])
                k2 = stt(prj[:, t, X_CKV:X_CKV + 128], prj[:, t, X_CKV:X_CKV + 128], s2[:, 0:1], c("kv"), ALU.mult,
                         ALU.mult, [tr2, tp])
                bk, fr = single()
                for (dd, a) in ((PS[:, bk, 0:128], prj[:, t, 0:128]), (PS[0:64, bk, 128:256], prj[:, t, 128:192]),
                                (PS[:, bk, 256:384], prj[:, t, X_CKV:X_CKV + 128])):
                    p = pe([k1, k2, fr, t_cst], lambda e, dd=dd, a=a: e.transpose(dd, a, ident))
                CT = GRP[:, t * 384:(t + 1) * 384]
                v1 = act([p, st["grp"]], lambda e, CT=CT, bk=bk: e.activation(CT[:, 0:128], PS[:, bk, 0:128], ACT.Copy))
                v2 = act([v1], lambda e, CT=CT, bk=bk: e.activation(CT[0:64, 128:256], PS[0:64, bk, 128:256], ACT.Copy))
                v3 = act([v2], lambda e, CT=CT, bk=bk: e.activation(CT[:, 256:384], PS[:, bk, 256:384], ACT.Copy))
                bank["free"][bk] = [v1, v2, v3]
                wuv = wu.ap.rearrange("p (k n) -> p k n", k=2)
                bk, fr = single()
                mm(PS[:, bk, 0:384], CT[:, 0:128], wuv[:, 0, :], True, False, [v1, v2, v3, wu.tok, fr])
                pq = mm(PS[:, bk, 0:384], CT[0:64, 128:256], wuv[0:64, 1, :], False, True)
                kq = dve([pq, tmpf], lambda e, t=t, bk=bk: e.tensor_copy(QF[:, t, :], PS[:, bk, 0:384]))
                bank["free"][bk] = [kq]
                bk, fr = single()
                pk = mm(PS[:, bk, :], CT[:, 256:384], wk.ap, True, True, [wk.tok, fr])
                kk_ = act([pk, tmpf], lambda e, t=t, bk=bk: e.activation(KVB[:, t, :], PS[:, bk, :], ACT.Copy))
                bank["free"][bk] = [kk_]
                tab = rp(t)[:, 0:64]
                qv = QF[:, t, :].rearrange("p (i d) -> p i d", i=4)
                RQ = TMP[:, 0:128].rearrange("p (i d) -> p i d", i=4)
                kr_ = rope(RQ.rearrange("p i (a b) -> p i a b", a=2), qv[:, :, 64:96].rearrange("p i (a b) -> p i a b", a=2),
                           4, 16, tab, TMP[:, 128:256].rearrange("p (i a b) -> p i a b", i=4, a=2), [kq, t_cst, lastqk])
                kq2 = dve([kr_], lambda e, qv=qv, RQ=RQ: e.tensor_copy(qv[:, :, 64:96], RQ))
                RK = TMP[:, 256:288]
                kr2 = rope(RK.rearrange("p (i a b) -> p i a b", i=1, a=2),
                           prj[:, t, X_KR:X_KR + 32].rearrange("p (i a b) -> p i a b", i=1, a=2), 1, 16, tab,
                           TMP[:, 288:320].rearrange("p (i a b) -> p i a b", i=1, a=2), [pj[t], t_cst])
                KF = TMP[:, 320:704].rearrange("p (i d) -> p i d", i=4)
                kf1 = dve([kk_], lambda e, t=t, KF=KF: e.tensor_copy(
                    KF[:, :, 0:64], KVB[:, t, 0:256].rearrange("p (i d) -> p i d", i=4)))
                kf2 = dve([kr2], lambda e, KF=KF, RK=RK: e.tensor_copy(KF[:, :, 64:96], bc(RK.unsqueeze(1), [128, 4, 32])))
                a1, _ = heads_T(A[:, 0:4, :], [qv[:, i, :] for i in range(4)], 96, t, [kq2], st["qa"])
                a2, p2 = heads_T(A[:, 4:8, :], [KF[:, i, :] for i in range(4)], 96, t, [kf1, kf2], st["qa"])
                lastqk = [p2]
                qd += a1 + a2
                kv_t.append(kk_)
            wu.release(pq)
            wk.release(pk)
            st["grp"] = [[pk], [pk]]
            latent, diff, window, near = [], [], [], []
            gm = []
            for t in range(2):
                maps = [(A[0:96, i, t * 128:(t + 1) * 128], A[0:96, 4 + i, :],
                         lambda kc, i=i: KVB[:, kc, 256 + i * 64:256 + (i + 1) * 64]) for i in range(4)]
                gm.append(group(t, maps, 256, 96.0 ** -0.5, [qd, kv_t], Y, 0, latent))
            RB = PRJ[:, 1024:1536]
            RT = PRJ[:, 1536:2048]
            prev = p2
            qdd = []
            for t in range(2):
                v = prj[:, t, X_BQ:X_BQ + 512].rearrange("p (i a b) -> p i a b", i=16, a=2)
                k = rope(RB.rearrange("p (i a b) -> p i a b", i=16, a=2), v, 16, 16, rp(t)[:, 0:64],
                         RT.rearrange("p (i a b) -> p i a b", i=16, a=2), [pj[t], prev])
                a, prev = heads_T(B, [RB[:, i * 32:(i + 1) * 32] for i in range(16)], 32, t, [k], [st["qb"], st["plf"]])
                qdd += a
            gd = []
            for t in range(2):
                for hg in range(2):
                    maps = [(B[0:32, hg * 4 + i, t * 128:(t + 1) * 128], B[0:32, 8 + hg * 4 + i, :],
                             lambda kc, i=i, hg=hg: prj[:, kc, X_BV + (hg * 2 + i // 2) * 64:X_BV + (hg * 2 + i // 2 + 1) * 64])
                            for i in range(4)]
                    gd.append(group(t, maps, 256, 32.0 ** -0.5, [qdd, tlam], Y, 256 + hg * 128, diff, lam=lam))
            qs, qn = [], []

            def window_heads():
                pv = prev
                for t in range(2):
                    v = prj[:, t, X_SQ:X_SQ + 384].rearrange("p (i a b) -> p i a b", i=6, a=2)
                    k = rope(RB[:, 0:384].rearrange("p (i a b) -> p i a b", i=6, a=2), v, 6, 32, rp(t)[:, 64:192],
                             RT[:, 0:384].rearrange("p (i a b) -> p i a b", i=6, a=2), [pj[t], pv])
                    yield
                    fr = [w for _, w in latent]
                    a, pv = heads_T(A[:, 0:4, :], [RB[:, i * 64:(i + 1) * 64] for i in range(4)], 64, t, [k], fr, 0.125)
                    b, pv = heads_T(A[:, 4:6, :], [RB[:, i * 64:(i + 1) * 64] for i in range(4, 6)], 64, t, [k], fr)
                    qs.extend(a + b)
                st["prj"] = [pv]

            gw = []
            for t in range(2):
                sm = CST[:, C_SM + t * 256:C_SM + (t + 1) * 256]

                def bias(P, sc, waits, sm=sm):
                    return tt(P, sc, bc(sm.unsqueeze(1), [128, 4, 256]), ALU.add, waits)
                maps = [(A[0:64, i, t * 128:(t + 1) * 128], A[0:64, 4 + i // 2, :],
                         lambda kc, i=i: prj[:, kc, X_SV + (i // 2) * 64:X_SV + (i // 2 + 1) * 64]) for i in range(4)]
                gw.append(group(t, maps, 256, 1.0, qs, Y, 512, window, bias=bias, sink=c("sink")))

            def near_heads():
                fr = [w for _, w in diff]
                for t in range(2):
                    a, _ = heads_T(B[:, 0:4, :], [prj[:, t, X_NQ + i * 64:X_NQ + (i + 1) * 64] for i in range(4)], 64, t,
                                   [pj[t]], fr, 0.125)
                    b, _ = heads_T(B[:, 4:8, :], [prj[:, t, X_NK + i * 64:X_NK + (i + 1) * 64] for i in range(4)], 64, t,
                                   [pj[t]], fr)
                    qn.extend(a + b)
                    yield

            gn = []
            for t in range(2):
                def bias(P, sc, waits, t=t):
                    nb = load(I["nab"][l * 2 + t], 1024)
                    k = tt(P, sc, nb.ap.rearrange("p (i k) -> p i k", i=4), ALU.add, [waits, nb.tok])
                    nb.release(k)
                    return k
                maps = [(B[0:64, i, t * 128:(t + 1) * 128], B[0:64, 4 + i, :],
                         lambda kc, i=i: prj[:, kc, X_NV + i * 64:X_NV + (i + 1) * 64]) for i in range(4)]
                gn.append(group(t, maps, 256, 1.0, qn, Y, 768, near, bias=bias))
            run(overlapped([*gm, gd[0], gd[1], gd[2], window_heads(), gd[3], gw[0], gw[1], near_heads(), *gn]))
            last = [w for r in (latent, diff, window, near) for _, w in r]
            st["qa"], st["qb"], st["plf"], st["mod"] = last, last, [], last
            st["prj"] = st["prj"] + last
            ym = [[v for r in (latent, diff, window, near) for v, _ in r]] * 2
            hs = []
            s, tr = rstd([Y[:, t, o:o + 256] for t in range(2) for o in (0, 512, 768)], 256.0,
                         [ym[t] for t in range(2) for _ in range(3)])
            for t in range(2):
                for i, (o, g) in enumerate(((0, "oa"), (512, "oc"), (768, "od"))):
                    yy = Y[:, t, o:o + 256]
                    k = stt(yy, yy, s[:, t * 3 + i:t * 3 + i + 1], c(g), ALU.mult, ALU.mult, [tr, tp])
                yb = Y[:, t, 256:512].rearrange("p (i d) -> p i d", i=4)
                jb = JV[:, 0:256].rearrange("p (i d) -> p i d", i=4)
                k2 = tt(jb, yb, yb, ALU.mult, [ym[t], st["jva"]])
                q = scratch(4)
                k2 = dve([k2], lambda e, q=q, jb=jb: e.reduce_sum(q, jb, AX))
                st["jv"] = [k2]
                k2 = act([k2], lambda e, q=q: e.activation(q, q, ACT.Sqrt, bias=EPSC, scale=1.0 / 64))
                k2 = dve([k2], lambda e, q=q: e.reciprocal(q, q))
                k2 = tt(yb, yb, bc(q.unsqueeze(2), [128, 4, 64]), ALU.mult, [k2])
                k2 = stt(yb, yb, 1.0 - lam0, bc(c("sub").unsqueeze(1), [128, 4, 64]), ALU.mult, ALU.mult, [k2])
                hs.append([k, k2])
            yt, last = transpose_tm(Y, HT, hs, st["ht"])
            st["h"] = [[last], [last]]
            residual([load(I["wout2"][l * 4 + j], 2048) for j in range(4)], HT, [yt])
            hts, _ = norm(c("n2"), None, [tp])
            st["par"] = hts
            AT = QK[:, 2048:3072].rearrange("p (b i s) -> p b i s", b=2, i=2)
            atf = [st["qb"], st["qb"]]
            last = None

            def down(b, at, wd):
                for t in range(2):
                    for hf in range(2):
                        for i in range(2):
                            p = mm(PS[:, t * 2 + hf, :], AT[:, b % 2, i, t * 128:(t + 1) * 128],
                                   wd.ap[:, i * 1024 + hf * 512:i * 1024 + (hf + 1) * 512], b == 0 and i == 0,
                                   b == 15 and i == 1, [at, wd.tok, bank["free"][t * 2 + hf]])
                wd.release(p)
                atf[b % 2] = [p]
                return p

            pend = None
            for b in range(16):
                w = load(I["wup"][l * 16 + b], 2048)
                wd = load(I["wdn"][l * 16 + b], 2048)
                wv = w.ap.rearrange("p (k n) -> p k n", k=8)
                bk, fr = single()
                for i in range(2):
                    for k in range(8):
                        p = mm(PS[:, bk, i * 256:(i + 1) * 256], wv[:, k, i * 128:(i + 1) * 128], HT[:, k, :],
                               k == 0, k == 7, [w.tok, hts, fr])
                pv = PS[:, bk, :].rearrange("p (i s) -> p i s", i=2)
                dst = AT[:, b % 2, :, :]
                r1 = act([p, atf[b % 2]], lambda e, dst=dst, pv=pv: e.activation(dst, pv, ACT.Relu))
                at = tt(dst, dst, dst, ALU.mult, [r1])
                bank["free"][bk] = [r1]
                w.release(p)
                st["ht"] = [p]
                if pend is not None:
                    down(*pend)
                pend = (b, at, wd)
            p = down(*pend)
            st["qb"] = [p]
            for t in range(2):
                for hf in range(2):
                    xs = X[:, t, hf * 512:(hf + 1) * 512]
                    v = tt(xs, PS[:, t * 2 + hf, :], xs, ALU.add, [p, st["x"][t]])
                    bank["free"][t * 2 + hf] = [v]
                st["x"][t] = [v]

        run(ada(0))
        heads = {(l, t): [] for l in range(L) for t in range(2)}
        order = [(l, t) for l in range(L) for t in range(2)]
        gens = {k: mix(*k, heads[k]) for k in order}
        second = ada(1)
        own = gens[(0, 0)]
        for _ in range(200):
            if heads[(0, 0)]:
                break
            next(own)
            for _ in range(2):
                next(second, None)
        run(second)
        for i, k in enumerate(order):
            behind = gens[order[i + 1]] if i + 1 < 4 else None
            experts(*k, heads[k], gens[k], behind, RATE)
            run(gens[k])
        st["qa"] = st["qt"] + st["kt"] + st["pl"]
        st["qb"] = st["x"][1] + st["half"][0] + st["half"][1]
        st["mod"] = st["x"][0] + st["x"][1]
        st["h"] = [st["x"][0] + st["htf"][0], st["x"][1]]
        st["ht"] = st["htf"][0] + st["htf"][1]
        st["par"] = st["x"][0] + st["x"][1]
        st["plf"] = []
        bank["pairs"] = (0, 2)
        for l in range(L):
            tp = load_par(I["par2"][l], 3332)
            block2(l, tp)
        tp = load_par(I["fing"], 1024)
        s, tr = rstd([X[:, 0, :], X[:, 1, :]], 1024.0, st["x"])
        for t in range(2):
            k = stt(X[:, t, :], X[:, t, :], s[:, t:t + 1], PARB[:, 0:1024], ALU.mult, ALU.mult, [tr, tp])
            st["x"][t] = [k]
        ov = out.rearrange("(t p) d -> p t d", p=128)
        t_o = sp.dma([st["x"]], lambda e: e.dma_start(ov, X), s_out, 16)
        sp([t_o], lambda e: e.nop())

        for e in (pe, act, dve, pool, sp):
            e.number()
        block = ctx.enter_context(nc.Block())

        @block.sync
        def _(e):
            sp.emit(e)

        @block.gpsimd
        def _(e):
            pool.emit(e)

        @block.scalar
        def _(e):
            act.emit(e)

        @block.vector
        def _(e):
            dve.emit(e)

        @block.tensor
        def _(e):
            pe.emit(e)


def constants():
    f = np.float32
    cst = np.zeros((128, C_END), f)
    cst[:, C_ID:C_ID + 128] = np.eye(128, dtype=f)
    pos = np.arange(256)
    q = pos.reshape(2, 128)
    d = q[:, :, None] - pos[None, None, :]
    nd = np.where((d >= 0) & (d < 128), -d.astype(f), f(-1e30))
    cst[:, C_ND:C_ND + 512] = nd.transpose(1, 0, 2).reshape(128, 512)
    sm = np.where(np.abs(d) <= 128, f(0), f(-1e30))
    cst[:, C_SM:C_SM + 512] = sm.transpose(1, 0, 2).reshape(128, 512)
    tabs = []
    for dim in (32, 64):
        inv = (f(1.0) / (f(10000.0) ** (np.arange(0, dim, 2, dtype=f) / f(dim)))).astype(f)
        ang = (np.arange(256, dtype=f)[:, None] * inv[None, :]).astype(f)
        c, s = np.cos(ang).astype(f), np.sin(ang).astype(f)
        tabs += [c, c, -s, s]
    tab = np.concatenate(tabs, axis=1)
    cst[:, C_ROPE:C_ROPE + 384] = tab.reshape(2, 128, 192).transpose(1, 0, 2).reshape(128, 384)
    cst[:, C_IOTA:C_IOTA + 16] = np.arange(16, dtype=f)
    mg = np.zeros((4, 256, 256), f)
    for g, w in enumerate((2, 4, 8, 16)):
        dd = pos[None, :] - pos[:, None]
        mg[g] = np.where((dd >= 0) & (dd < w), f(1) / np.minimum(pos + 1, w).astype(f)[None, :], f(0))
        mg[g] -= np.eye(256, dtype=f)
    mg = mg.reshape(4, 2, 128, 2, 128).transpose(3, 2, 1, 0, 4)
    return cst, mg


def layout(v):
    f = np.float32
    a = {k: np.asarray(x) for k, x in v.items()}

    def cols(w, n):
        l_, k, m = w.shape
        w = w.reshape(l_, k // 128, 128, m // n, n).transpose(0, 3, 2, 1, 4)
        return np.ascontiguousarray(w).reshape(l_ * (m // n), 128, (k // 128) * n)

    cst, mg = constants()
    o = {"cst": cst}
    o["x"] = a["x"].reshape(256, 1024)
    o["mg0"], o["mg1"] = mg[0, :, 0:1].reshape(128, 512), mg[1].reshape(128, 1024)
    o["cT"] = np.ascontiguousarray(a["c"].reshape(8, 128).T)
    o["wada"] = cols(a["w_ada"], 256)
    o["bada"] = a["b_ada"]
    par = np.concatenate([a["norm1_g"], a["norm2_g"], a["pool_scale"], a["q_norm_g"], a["k_norm_g"], a["attn_sinks"],
                          a["mix_norm_g"]], axis=1)
    o["par1"] = par
    o["win1"] = cols(a["w_in"], 256)
    o["poolw"] = np.ascontiguousarray(a["pool_w"].transpose(0, 2, 1, 3)).reshape(L, 128, 512)
    o["wout1"] = cols(a["w_out"], 256)
    o["wq"] = cols(a["peer_wq"], 256)
    o["skT"] = np.ascontiguousarray(a["peer_subkeys"].transpose(0, 3, 1, 2)).reshape(L, 128, 256)
    for l in range(L):
        o[f"uv{l}"] = np.concatenate([a["peer_u"][l], a["peer_v"][l]], axis=1)
    o["par2"] = np.concatenate([a["norm1_g_2"], a["norm2_g_2"], a["mla_q_norm_g_2"], a["mla_kv_norm_g_2"],
                                a["diff_lambda_q1_2"], a["diff_lambda_k1_2"], a["diff_lambda_q2_2"], a["diff_lambda_k2_2"],
                                a["diff_subln_g_2"], a["swa_sinks_2"], a["out_g_mla_2"], a["out_g_swa_2"],
                                a["out_g_na_2"]], axis=1)
    o["fing"] = a["final_norm_g_2"]
    o["win2"] = cols(a["w_in_2"], 240)
    wuq = np.zeros((L, 256, 384), f)
    wuq[:, 0:192] = a["mla_w_uq_2"]
    o["wuq"] = np.ascontiguousarray(wuq.reshape(L, 2, 128, 384).transpose(0, 2, 1, 3)).reshape(L, 128, 768)
    o["wukv"] = np.concatenate([a["mla_w_uk_2"], a["mla_w_uv_2"]], axis=2)
    pos = np.arange(256)
    r, c = pos // 64, pos % 64
    start = np.clip(c - 8, 0, 48)
    inside = (c[None, :] >= start[:, None]) & (c[None, :] < start[:, None] + 16)
    ri = r[None, :] - r[:, None] + 7
    ci = np.clip(c[None, :] - c[:, None] + 15, 0, 30)
    nab = np.where(inside[None, None], a["na_rpb_2"][:, :, ri, ci], f(-1e30)).astype(f)
    o["nab"] = np.ascontiguousarray(nab.reshape(L, 4, 2, 128, 256).transpose(0, 2, 3, 1, 4)).reshape(L * 2, 128, 1024)
    o["wout2"] = cols(a["w_out_2"], 256)
    o["wup"] = cols(a["w_up_2"], 256)
    wd = a["w_down_2"].reshape(L, 16, 2, 128, 1024).transpose(0, 1, 3, 2, 4)
    o["wdn"] = np.ascontiguousarray(wd).reshape(L * 16, 128, 2048)
    return {k: np.ascontiguousarray(x) for k, x in o.items()}


def declare(nc, arrays):
    I = {k: nc.dram_tensor("in_" + k, a.shape, mybir.dt.from_np(a.dtype), kind="ExternalInput").ap()
         for k, a in arrays.items()}
    I["modd"] = nc.dram_tensor("modd", (1, 6144), F32).ap()
    out = nc.dram_tensor("out_x", (256, 1024), F32, kind="ExternalOutput").ap()
    build(nc, I, out)


def kernel(**inputs):
    import concourse.bacc as _bacc
    from concourse.bass_utils import run_bass_kernel_spmd as _run

    arrays = layout(inputs)
    nc = _bacc.Bacc("TRN2", target_bir_lowering=False, num_devices=1)
    declare(nc, arrays)
    r = _run(nc, [{"in_" + k: a for k, a in arrays.items()}], core_ids=[0])
    return r.results[0]["out_x"].reshape(1, 256, 1024)
```

```python
import math
from contextlib import ExitStack

import numpy as np

import concourse.bass as bass
from concourse import mybir

F32 = mybir.dt.float32
I32 = mybir.dt.int32
U32 = mybir.dt.uint32
ALU = mybir.AluOpType
ACT = mybir.ActivationFunctionType
AX = mybir.AxisListType.X

L = 2
SLOTS = 11
SLOT = 2048
AHEAD = 2
MODS = 3
WIDE = 5
BATCH = 1
LIGHT = "light"
STEPS = 50
SPARE = 3
OWN = 1
SKEW = 1
PACE = 0
PAR = 3720
TINY = -3.0e38
EPS = 1e-6

C_ID, C_ND, C_ROPE, C_IOTA, C_END = 0, 128, 640, 1024, 1040
C_SM = C_ND
P1 = dict(n1=(0, 1024), n2=(1024, 1024), ps=(2048, 512), qg=(2560, 64), kg=(2624, 64), sink=(2688, 8), mg=(2696, 1024))
P2 = dict(n1=(0, 1024), n2=(1024, 1024), q=(2048, 192), kv=(2240, 128), lam=(2368, 128), sub=(2496, 64), sink=(2560, 4),
          oa=(2564, 256), oc=(2820, 256), od=(3076, 256))
X_CQ, X_CKV, X_KR, X_BQ, X_BV, X_SQ, X_SK, X_SV, X_NQ, X_NK, X_NV = 0, 192, 320, 352, 864, 1120, 1376, 1504, 1632, 1888, 2144


class Token:

    def __init__(self, sem, value=None):
        self.sem, self.value, self.used = sem, value, False


class Engine:

    def __init__(self, sem, chained=False):
        self.sem, self.items, self.chained, self.last = sem, [], chained, None

    def __call__(self, waits, fn):
        tok = Token(self.sem)
        self.items.append((flat([waits, self.last]), fn, tok, None))
        if self.chained:
            self.last = tok
        return tok

    def dma(self, waits, fn, sem, value):
        tok = Token(sem, value)
        self.items.append((flat(waits), fn, None, sem))
        return tok

    def number(self):
        n = 0
        for _, _, tok, _ in self.items:
            if tok is not None and tok.used:
                n += 1
                tok.value = n

    def emit(self, eng):
        seen = {}
        for waits, fn, tok, sem in self.items:
            for w in waits:
                if seen.get(id(w.sem), 0) < w.value:
                    seen[id(w.sem)] = w.value
                    eng.wait_ge(w.sem, w.value)
            ins = fn(eng)
            if sem is not None:
                ins.then_inc(sem, 16)
            elif tok is not None and tok.used:
                ins.then_inc(tok.sem, 1)


def flat(waits):
    out = []
    for w in waits:
        if isinstance(w, (list, tuple)):
            out += flat(w)
        elif w is not None:
            w.used = True
            out.append(w)
    return out


def bc(ap, shape):
    return ap.to_broadcast(shape)


def build(nc, I, out):
    with ExitStack() as ctx:
        def sb(name, n, dt=F32):
            return ctx.enter_context(nc.sbuf_tensor(name, [128, n], dt))

        def sem(name):
            return ctx.enter_context(nc.semaphore(name))

        X = sb("X", 2048)[:, :].rearrange("p (t d) -> p t d", t=2)
        MOD = sb("MOD", 5120)[:, :]
        G2 = sb("G2", 2048)[:, :]
        PARB = sb("PARB", PAR)[:, :]
        HT = sb("HT", 2048)[:, :].rearrange("p (c s) -> p c s", c=8)
        H = sb("H", 2048)[:, :].rearrange("p (t d) -> p t d", t=2)
        PRJ = sb("PRJ", 2560)[:, :]
        QK = sb("QK", 6144)[:, :]
        CST = sb("CST", C_END)[:, :]
        ONES = sb("ONES", 128)[:, :]
        ACC = sb("ACC", 1024)[:, :].rearrange("p (b n) -> p b n", b=2)
        DG = sb("DG", 4 * 128)[:, :].rearrange("p (b n) -> p b n", b=4)
        CREP = DG[:, 0:3, :]
        SC = sb("SC", 512)[:, :]
        GATE = sb("GATE", 256)[:, :]
        AV = sb("AV", 256)[:, :]
        EID = sb("EID", 256, I32)[:, :]
        TV = sb("TV", 2 * 64)[:, :]
        TI = sb("TI", 2 * 64, U32)[:, :]
        TC = sb("TC", 256)[:, :]
        RNG = sb("RNG", SLOTS * SLOT)[:, :]
        PS = ctx.enter_context(nc.psum_tensor("PS", [128, 8, 512], F32))

        pe, act, dve, pool, sp = (Engine(sem("s_" + n), n in ("act", "dve")) for n in ("pe", "act", "dve", "pool", "sp"))
        ld = [sem(f"ld{u}") for u in range(SLOTS)]
        ga = [sem(f"ga{u}") for u in range(SLOTS)]
        s_par, s_mod, s_x, s_out = sem("s_par"), sem("s_mod"), sem("s_x"), sem("s_out")
        s_md, s_row = sem("s_md"), sem("s_row")

        ident = CST[:, C_ID:C_ID + 128]
        JVS = [QK[:, 5120:6144]]

        slots = dict(free=[(u, []) for u in range(SLOTS)], n={})

        class Item:
            def __init__(self):
                self.u, self.waits = slots["free"].pop(0)
                self.ap = RNG[:, self.u * SLOT:(self.u + 1) * SLOT]

            def count(self, sem):
                slots["n"][id(sem)] = slots["n"].get(id(sem), 0) + 16
                return sem, slots["n"][id(sem)]

            def release(self, *toks):
                slots["free"].append((self.u, list(toks)))

        def load(src, n):
            it = Item()
            dst = it.ap[:, 0:n]
            it.tok = sp.dma(it.waits, lambda e: e.dma_start(dst, src), *it.count(ld[it.u]))
            it.ap = dst
            return it

        def stream(srcs):
            todo, under = list(srcs), []
            while todo or under:
                while todo and len(under) < 1 + AHEAD:
                    under.append(load(*todo.pop(0)))
                yield under.pop(0)

        bank = dict(free=[[] for _ in range(8)], next=0, pair=0, pairs=(2,))

        def single():
            while bank["free"][4 + bank["next"] % 4] is None:
                bank["next"] += 1
            b = 4 + bank["next"] % 4
            bank["next"] += 1
            fr, bank["free"][b] = bank["free"][b], None
            return b, fr

        turn = dict(n=0, sc=0)

        def evac(dst, src, waits, scale=1.0):
            turn["n"] += 1
            if turn["n"] % 2:
                return act(waits, lambda e: e.activation(dst, src, ACT.Copy, scale=scale))
            if scale == 1.0:
                return dve(waits, lambda e: e.tensor_copy(dst, src))
            return dve(waits, lambda e: e.tensor_scalar(dst, src, scale, None, ALU.mult))

        def scratch(n):
            if turn["sc"] % 512 + n > 512:
                turn["sc"] += 512 - turn["sc"] % 512
            c = turn["sc"] % 512
            turn["sc"] += n
            return SC[:, c:c + n]

        def tt(dst, a, b, op, waits):
            return dve(waits, lambda e: e.tensor_tensor(dst, a, b, op))

        def stt(dst, a, s, b, op0, op1, waits):
            return dve(waits, lambda e: e.scalar_tensor_tensor(out=dst, in0=a, scalar=s, in1=b, op0=op0, op1=op1))

        def ts(dst, a, s1, s2, op0, op1, waits):
            if op1 is None:
                return dve(waits, lambda e: e.tensor_scalar(dst, a, s1, None, op0))
            return dve(waits, lambda e: e.tensor_scalar(dst, a, s1, s2, op0, op1))

        def mm(dst, a, b, start, stop_, waits=()):
            return pe(waits, lambda e: e.matmul(dst, a, b, start=start, stop=stop_))

        t_cst = sp.dma([], lambda e: e.dma_start(CST, I["cst"]), s_x, 16)
        COND = scratch(24)
        t_c = sp.dma([t_cst], lambda e: e.dma_start(COND[:, 0:8], I["cT"]), s_x, 32)
        t_x = sp.dma([t_c], lambda e: e.dma_start(X, I["x"].rearrange("(t p) d -> p t d", p=128)), s_x, 48)
        EPSC = sb("EPSC", 1)[:, :]
        SKB = sb("SKB", 256)[:, :]
        BB = ACC.rearrange("p b n -> p (b n)")
        s_bb = sem("s_bb")
        s_sm = sem("s_sm")
        s_row2 = [sem("s_row0"), sem("s_row1")]
        s_sk = sem("s_sk")
        t_one = dve([], lambda e: e.memset(ONES, 1.0))
        t_eps = dve([], lambda e: e.memset(EPSC, EPS))
        k1 = act([t_c], lambda e: e.activation(COND[:, 8:16], COND[:, 0:8], ACT.Exp, scale=-1.0))
        k1 = ts(COND[:, 8:16], COND[:, 8:16], 1.0, None, ALU.add, None, [k1])
        k1 = dve([k1], lambda e: e.reciprocal(COND[:, 8:16], COND[:, 8:16]))
        t_cond = tt(COND[:, 16:24], COND[:, 0:8], COND[:, 8:16], ALU.mult, [k1])
        t_rep = None
        for k in range(3):
            src = COND[:, 21 + k:22 + k]
            dst = CREP[:, k, :]
            t_rep = dve([t_cond], lambda e, dst=dst, src=src: e.tensor_copy(dst, bc(src, [128, 128])))

        st = dict(x=[[t_x], [t_x]], par=[], mod=[], ht=[], h=[[], []], prj=[], qa=[], qb=[], grp=[[], []], acc=[[], []],
                  npar=0, nmod=0, blocks=0, row=[[], []], gi=0, dg=[[] for _ in range(4)], dn=0, tv=[[], []], tn=0)

        def load_par(src, n):
            st["npar"] += 16
            t = sp.dma(st["par"], lambda e: e.dma_start(PARB[:, 0:n], src.partition_broadcast(128)), s_par, st["npar"])
            st["par"] = []
            return t

        def ada(l):
            if l == 0:
                tb = sp.dma([], lambda e: e.dma_start(MOD, I["bada"][0][0:5120].partition_broadcast(128)), s_mod, 16)
                tb2 = sp.dma([tb], lambda e: e.dma_start(G2[:, 0:1024], I["bada"][0][5120:6144].partition_broadcast(128)),
                             s_mod, 32)
            else:
                tb2 = None
            ws = stream([(I["wada"][l * 24 + b], 2048) for b in range(24)])
            done = []
            for b in range(24):
                w = next(ws)
                wv = w.ap.rearrange("p (k n) -> p k n", k=8)
                a = ACC[:, b % 2, 0:256]
                t = ts(a, wv[:, 0, :], COND[:, 16:17], None, ALU.mult, None, [w.tok, t_cond, st["acc"][b % 2]])
                for k in range(1, 5):
                    t = stt(a, wv[:, k, :], COND[:, 16 + k:17 + k], a, ALU.mult, ALU.add, [t])
                yield
                bk, fr = single()
                for k in range(3):
                    mm(PS[:, bk, 0:256], CREP[:, k, :], wv[:, 5 + k, :], k == 0, False, [w.tok, t_rep, fr])
                p = mm(PS[:, bk, 0:256], ONES, a, False, True, [t, t_one])
                w.release(p, t)
                st["acc"][b % 2] = [p]
                yield
                if l == 0:
                    m = MOD[:, b * 256:(b + 1) * 256] if b < 20 else G2[:, (b - 20) * 256:(b - 19) * 256]
                    t = tt(m, PS[:, bk, 0:256], m, ALU.add, [p, tb2])
                    st["blocks"] = b + 1
                else:
                    m = ACC[0:1, b % 2, 256:512]
                    t = act([p, st["row"][b % 2]], lambda e, m=m, bk=bk: e.activation(m, PS[0:1, bk, 0:256], ACT.Copy))
                    dr = I["modd"][0:1, b * 256:(b + 1) * 256]
                    d = act.dma([t], lambda e, m=m, dr=dr: e.dma_start(dr, m), s_row2[b % 2], 16 * (b // 2 + 1))
                    st["row"][b % 2] = [d]
                bank["free"][bk] = [t]
            if l == 1:
                st["ada"] = st["row"][0] + st["row"][1]

        def rstd(srcs, D, waits):
            n = len(srcs)
            s = scratch(n)
            last = []
            jv = JVS[0]
            for i, a in enumerate(srcs):
                w = a.shape[-1]
                last = act([waits[i], st.get("jv", [])], lambda e, a=a, i=i, w=w: e.activation(
                    jv[:, 0:w], a, ACT.Square, accum_out=s[:, i:i + 1]))
                st["jv"] = []
            st["jva"] = [last]
            t = act([last, t_eps], lambda e: e.activation(s, s, ACT.Sqrt, bias=EPSC, scale=1.0 / D))
            t = dve([t], lambda e: e.reciprocal(s, s))
            return s, t

        def transpose_tm(t, waits, free):
            out = []
            for c4 in range(2):
                bk, fr = single()
                for c in range(4):
                    a = H[:, t, (c4 * 4 + c) * 128:(c4 * 4 + c + 1) * 128]
                    d = PS[:, bk, c * 128:(c + 1) * 128]
                    p = pe([waits, fr, t_cst], lambda e, a=a, d=d: e.transpose(d, a, ident))
                v = evac(HT[:, c4 * 4:c4 * 4 + 4, t * 128:(t + 1) * 128],
                         PS[:, bk, :].rearrange("p (c s) -> p c s", c=4), [p, free])
                bank["free"][bk] = [v]
                out.append(v)
            st["h"][t] = [p]
            return out

        def norm(t, g, waits):
            s, tr = rstd([X[:, t, :]], 1024.0, [st["x"][t]])
            k = stt(H[:, t, :], X[:, t, :], s[:, 0:1], g, ALU.mult, ALU.mult, [tr, waits, st["h"][t]])
            return transpose_tm(t, k, st["ht"][t])

        def tokens_by(hT, w, width, t, k8, waits, fr, bk):
            wv = w.ap.rearrange("p (k n) -> p k n", k=k8)
            for k in range(k8):
                p = mm(PS[:, bk, 0:width], hT[:, k, t * 128:(t + 1) * 128], wv[:, k, :], k == 0, k == k8 - 1,
                       [w.tok, waits, fr])
            return p

        def residual(t, items, hT, waits):
            for j, w in enumerate(items):
                bk, fr = single()
                p = tokens_by(hT, w, 256, t, 8, waits, fr, bk)
                xs = X[:, t, j * 256:(j + 1) * 256]
                v = tt(xs, PS[:, bk, 0:256], xs, ALU.add, [p, st["x"][t]])
                bank["free"][bk] = [v]
                if t == 1:
                    w.release(p)
            st["x"][t] = [v]
            st["ht"][t] = [p]

        def heads_T(dst, srcs, d, t, waits, free, scale=1.0):
            out = []
            for i in range(0, len(srcs), 4):
                part = srcs[i:i + 4]
                bk, fr = single()
                for j, a in enumerate(part):
                    dd = PS[0:d, bk, j * 128:(j + 1) * 128]
                    p = pe([waits, fr, t_cst], lambda e, a=a, dd=dd: e.transpose(dd, a, ident))
                v = evac(dst[0:d, i:i + len(part), t * 128:(t + 1) * 128],
                         PS[0:d, bk, 0:len(part) * 128].rearrange("p (j s) -> p j s", j=len(part)), [p, free], scale)
                bank["free"][bk] = [v]
                out.append(v)
            return out, p

        def group(t, maps, keys, scale, waits, Y, ycol, res, bias=None, sink=None, lam=None):
            n, it = len(maps), Item()
            nk = keys // 128
            P = it.ap[:, 0:1024].rearrange("p (i k) -> p i k", i=4)[:, 0:n, 0:keys]
            PT = it.ap[:, 1024:2048]
            b0 = bank["pairs"][bank["pair"] % len(bank["pairs"])]
            bank["pair"] += 1
            sc = PS[:, b0:b0 + 2, :].rearrange("p b (i k) -> p (b i) k", i=2)[:, 0:n, 0:keys]
            fr = [bank["free"][b0], bank["free"][b0 + 1]]
            for i, m in enumerate(maps):
                p = mm(sc[:, i, :], m[0], m[1][:, 0:keys], True, True, [waits, fr])
            yield
            src, ready, pfree = sc, p, it.waits
            if bias is not None:
                ready = bias(P, sc, [p, pfree])
                src, pfree = P, []
                bank["free"][b0] = bank["free"][b0 + 1] = [ready]
            w = scratch(4 * n)
            mx, ng, rs, rd = (w[:, j * n:(j + 1) * n] for j in range(4))
            k = dve([ready], lambda e: e.reduce_max(mx, src, AX))
            if sink is not None:
                k = tt(mx, mx, sink, ALU.max, [k])
            k = ts(ng, mx, -scale, None, ALU.mult, None, [k])
            for i in range(n):
                a = act([k, pfree], lambda e, i=i: e.activation(P[:, i, :], src[:, i, :], ACT.Exp, bias=ng[:, i:i + 1],
                                                                scale=scale, accum_out=rs[:, i:i + 1]))
            if bias is None:
                bank["free"][b0] = bank["free"][b0 + 1] = [a]
            if sink is not None:
                k = tt(mx, sink, mx, ALU.subtract, [k])
                e1 = act([k], lambda e: e.activation(mx, mx, ACT.Exp))
            yield
            ls = a
            if sink is not None:
                ls = tt(rs, rs, mx, ALU.add, [e1, a])
            r = dve([ls], lambda e: e.reciprocal(rd, rs))
            no, PO = n, P
            if lam is not None:
                no = n // 2
                k = r
                for i in range(no):
                    k0 = ts(P[:, 2 * i + 1, :], P[:, 2 * i + 1, :], rd[:, 2 * i + 1:2 * i + 2], lam, ALU.mult, ALU.mult, [k])
                    k = stt(P[:, 2 * i, :], P[:, 2 * i, :], rd[:, 2 * i:2 * i + 1], P[:, 2 * i + 1, :],
                            ALU.mult, ALU.subtract, [k0])
                a = k
                maps, PO = maps[::2], P[:, 0:n:2, :]
            pts = []
            total = no * nk
            for j0 in range(0, total, 4):
                m4 = min(4, total - j0)
                bk, fr = single()
                for j in range(m4):
                    i, kc = divmod(j0 + j, nk)
                    s_, d_ = PO[:, i, kc * 128:(kc + 1) * 128], PS[:, bk, j * 128:(j + 1) * 128]
                    p = pe([a, fr], lambda e, s_=s_, d_=d_: e.transpose(d_, s_, ident))
                v = evac(PT[:, j0 * 128:(j0 + m4) * 128], PS[:, bk, 0:m4 * 128], [p, it.waits])
                bank["free"][bk] = [v]
                pts.append(v)
            yield
            bk, fr = single()
            for i, m in enumerate(maps):
                for kc in range(nk):
                    j = i * nk + kc
                    p = mm(PS[:, bk, i * 64:(i + 1) * 64], PT[:, j * 128:(j + 1) * 128], m[2](kc), kc == 0, kc == nk - 1,
                           [pts[j // 4], fr])
            it.release(p)
            yield
            o = PS[:, bk, 0:no * 64]
            if lam is not None:
                v = dve([p, st["yfree"]], lambda e: e.tensor_copy(Y[:, t, ycol:ycol + no * 64], o))
            else:
                yv = Y[:, t, ycol:ycol + no * 64].rearrange("p (i d) -> p i d", i=no)
                v = tt(yv, o.rearrange("p (i d) -> p i d", i=no), bc(rd.unsqueeze(2), [128, no, 64]), ALU.mult,
                       [p, r, st["yfree"]])
            bank["free"][bk] = [v]
            res.append((v, p))

        def overlapped(gens, wide=2):
            live, todo = [], list(gens)
            while live or todo:
                if todo and len(live) < wide:
                    live.append(todo.pop(0))
                for g in list(live):
                    if next(g, 0) == 0:
                        live.remove(g)
                yield

        def advance(gen):
            for _ in range(3):
                if next(gen, None) is not LIGHT:
                    return

        def after(ready, gen):
            while not ready():
                yield
            yield from gen

        def run(gen):
            for _ in gen:
                pass

        kT = QK[:, 0:512].rearrange("p (i s) -> p i s", i=2)
        qT = QK[:, 512:1536].rearrange("p (i s) -> p i s", i=8)
        plT = QK[:, 1536:2048].rearrange("p (g s) -> p g s", g=4)
        JS = QK[:, 2048:3072]
        JD = QK[:, 3072:4096]
        HALF = QK[:, 4096:4608].rearrange("p (b i s) -> p b i s", b=2, i=2)
        S = QK[:, 4608:5120].rearrange("p (b i s) -> p b i s", b=2, i=2)
        st.update(kt=[[], []], qt=[], pl=[], half=[[], []], s=[[], []], pj=[[], []], hfree=[[], []], htf=[[], []])
        st.update(eid=[[], []])

        def norm1t(t, g, b, waits):
            s, tr = rstd([X[:, t, :]], 1024.0, [st["x"][t]])
            yield
            k = stt(H[:, t, :], X[:, t, :], s[:, 0:1], g, ALU.mult, ALU.mult, [tr, waits, st["hfree"][t]])
            hs = tt(H[:, t, :], H[:, t, :], b, ALU.add, [k])
            yield
            yield from transposed(t, hs)

        def transposed(t, hs):
            out = []
            for c4 in range(2):
                bk, fr = single()
                for c in range(4):
                    a = H[:, t, (c4 * 4 + c) * 128:(c4 * 4 + c + 1) * 128]
                    d = PS[:, bk, c * 128:(c + 1) * 128]
                    p = pe([hs, fr, t_cst], lambda e, a=a, d=d: e.transpose(d, a, ident))
                v = evac(HT[:, c4 * 4:c4 * 4 + 4, t * 128:(t + 1) * 128],
                         PS[:, bk, :].rearrange("p (c s) -> p c s", c=4), [p, st["htf"][t]])
                bank["free"][bk] = [v]
                out.append(v)
            yield
            st["hfree"][t] = [p]
            st["htf"][t] = []
            st["hready"], st["htready"] = hs, out

        def mix(l, t, tk):
            c = lambda k: PARB[:, P1[k][0]:P1[k][0] + P1[k][1]]
            sh1, sc1, g1, sh2, sc2 = (MOD[:, i * 1024:(i + 1) * 1024] for i in range(5))
            if t == 0:
                tp = load_par(I["par1"][l], PAR)
                st["skn"] = st.get("skn", 0) + 16
                st["sk"] = sp.dma([st.get("skf", [])], lambda e: e.dma_start(SKB, I["skT"][l]), s_sk, st["skn"])
                if l > 0:
                    t1 = sp.dma([st["ada"], st["modf"]], lambda e: e.dma_start(
                        MOD, I["modd"][0, 0:5120].partition_broadcast(128)), s_md, 16)
                    t2 = sp.dma([t1], lambda e: e.dma_start(
                        G2[:, 1024:2048], I["modd"][0, 5120:6144].partition_broadcast(128)), s_md, 32)
                    t3 = t2
                    for a0 in range(0, 6144, 1024):
                        m = MOD[:, a0:a0 + 1024] if a0 < 5120 else G2[:, 1024:2048]
                        src = I["bada"][1][a0:a0 + 1024]
                        t3 = sp.dma([t3, st["bf"]], lambda e, src=src: e.dma_start(
                            BB, src.partition_broadcast(128)), s_bb, 16 * (a0 // 1024 + 1))
                        st["bf"] = [tt(m, m, BB, ALU.add, [t3, t2])]
                        yield
                    st["ada"] = st["bf"]
                while l == 0 and st["blocks"] < 8:
                    yield
                m1 = stt(sc1, sc1, 1.0, c("n1"), ALU.add, ALU.mult, [st["ada"], tp])
                st["m"] = [m1, tp]
                st["tp"] = tp
                yield
            tp = st["tp"]
            ws = stream([(I["win1"][l * 5 + j], 2048) for j in range(5)] + [(I[f"mg{t}"], 512 * (t + 1)), (I["poolw"][l], 512)])
            prj = PRJ.rearrange("p (t n) -> p t n", t=2)
            yield from norm1t(t, sc1, sh1, st["m"])
            hts = st["htready"]
            pj = [None] * 5
            for j in range(5):
                w = next(ws)
                bk, fr = single()
                p = tokens_by(HT, w, 256, t, 8, hts, fr, bk)
                yield
                v = evac(prj[:, t, j * 256:(j + 1) * 256], PS[:, bk, 0:256], [p, st["prj"]])
                bank["free"][bk] = [v]
                pj[j] = v
                w.release(p)
                for _ in range(PACE):
                    yield
            st["htf"][t] = [p]
            st["pj"][t] = [pj[0], pj[1]]
            sq = JD[:, 0:640].rearrange("p (i d) -> p i d", i=10)
            v = prj[:, t, 512:1152].rearrange("p (i d) -> p i d", i=10)
            k = tt(sq, v, v, ALU.mult, [pj])
            s = scratch(10)
            k = dve([k], lambda e, s=s, sq=sq: e.reduce_sum(s, sq, AX))
            k = act([k, t_eps], lambda e, s=s: e.activation(s, s, ACT.Sqrt, bias=EPSC, scale=1.0 / 64))
            yield
            k = dve([k], lambda e, s=s: e.reciprocal(s, s))
            k = tt(v, v, bc(s.unsqueeze(2), [128, 10, 64]), ALU.mult, [k])
            k1 = tt(v[:, 0:8, :], v[:, 0:8, :], bc(c("qg").unsqueeze(1), [128, 8, 64]), ALU.mult, [k, tp])
            k2 = tt(v[:, 8:10, :], v[:, 8:10, :], bc(c("kg").unsqueeze(1), [128, 2, 64]), ALU.mult, [k, tp])
            yield
            mg, pw = next(ws), next(ws)
            mgv = mg.ap.rearrange("p (a g s) -> p a g s", a=t + 1, g=4)
            bk, fr = single()
            for g in range(4):
                for a in range(t + 1):
                    p = mm(PS[:, bk, g * 128:(g + 1) * 128], prj[:, a, g * 128:(g + 1) * 128], mgv[:, a, g, :],
                           a == 0, a == t, [st["pj"], mg.tok, fr])
            pt = evac(plT, PS[:, bk, :].rearrange("p (g s) -> p g s", g=4), [p, st["pl"]])
            bank["free"][bk] = [pt]
            mg.release(p)
            yield
            a, _ = heads_T1(qT, [v[:, i, :] for i in range(8)], 0, [k1], st["qt"], 0.125)
            b, _ = heads_T1(kT, [v[:, i, :] for i in range(8, 10)], t, [k2], st["kt"], 1.0)
            qd = a + b + st["kt"]
            yield
            st["yfree"] = [st["hfree"][t]]
            bk, fr = single()
            for g in range(4):
                p = mm(PS[:, bk, g * 128:(g + 1) * 128], plT[:, g, :], pw.ap[:, g * 128:(g + 1) * 128], True, True,
                       [pt, pw.tok, fr])
            pw.release(p)
            st["pl"] = [p]
            yield
            v = tt(H[:, t, 0:512], PS[:, bk, :], c("ps"), ALU.mult, [p, st["yfree"], tp])
            bank["free"][bk] = [v]
            ym = [v]
            res, groups = [], []
            for hg in range(2):
                nd = CST[:, C_ND + t * 256:C_ND + (t + 1) * 256]

                def bias(P, sc, waits, hg=hg, nd=nd):
                    for i in range(4):
                        k = stt(P[:, i, :], nd[:, 0:(t + 1) * 128], 2.0 ** -(hg * 4 + i + 1), sc[:, i, :],
                                ALU.mult, ALU.add, waits)
                    return k
                maps = [(qT[0:64, hg * 4 + i, :], kT[0:64, hg, :],
                         lambda kc, hg=hg: prj[:, kc, 1152 + hg * 64:1152 + (hg + 1) * 64]) for i in range(4)]
                groups.append(group(t, maps, (t + 1) * 128, 1.0, [qd, tp], H, 512 + hg * 256, res, bias=bias,
                                    sink=c("sink")[:, hg * 4:hg * 4 + 4]))
            yield from overlapped(groups)
            ym += [v for v, _ in res]
            lastp = res[-1][1]
            st["qt"], st["kt"] = [lastp], [lastp]
            if t == 1:
                st["prj"] = [lastp]
            while l == 0 and st["blocks"] < 12:
                yield
            ws = stream([(I["wout1"][l * 4 + j], 2048) for j in range(4)])
            s, tr = rstd([H[:, t, j * 512:(j + 1) * 512] for j in range(2)], 512.0, [ym, ym])
            yield
            for j in range(2):
                yy = H[:, t, j * 512:(j + 1) * 512]
                k = stt(yy, yy, s[:, j:j + 1], c("mg")[:, j * 512:(j + 1) * 512], ALU.mult, ALU.mult, [tr, tp])
            yield
            yield from transposed(t, k)
            yt = st["htready"]
            for j in range(4):
                w = next(ws)
                bk, fr = single()
                p = tokens_by(HT, w, 256, t, 8, yt, fr, bk)
                w.release(p)
                yield
                xs = X[:, t, j * 256:(j + 1) * 256]
                k = tt(JD[:, 0:256], PS[:, bk, 0:256], g1[:, j * 256:(j + 1) * 256], ALU.mult, [p])
                v = tt(xs, JD[:, 0:256], xs, ALU.add, [k, st["x"][t]])
                bank["free"][bk] = [v]
                for _ in range(PACE):
                    yield
            st["x"][t] = [v]
            st["htf"][t] = [p]
            while l == 0 and st["blocks"] < 24:
                yield
            ws = stream([(I["wq"][l * 8 + j], 2048) for j in range(8)])
            if t == 0:
                st["m"] = [stt(sc2, sc2, 1.0, c("n2"), ALU.add, ALU.mult, [st["ada"], tp]), tp]
            yield from norm1t(t, sc2, sh2, st["m"])
            hts = st["htready"]
            st["h2"][t] = [st["hready"]]
            if t == 1:
                st["par"] = [st["hready"], v]
                st["modf"] = [st["hready"]]
            skv = SKB.rearrange("p (a n) -> p a n", a=2)
            for h in range(8):
                w = next(ws)
                wv = w.ap.rearrange("p (k n) -> p k n", k=8)
                bk, fr = single()
                for i in range(2):
                    for k in range(8):
                        p = mm(PS[:, bk, i * 128:(i + 1) * 128], wv[:, k, i * 128:(i + 1) * 128],
                               HT[:, k, t * 128:(t + 1) * 128], k == 0, k == 7, [w.tok, hts, fr])
                w.release(p)
                yield
                half, u = HALF[:, h % 2], h % 2
                v = act([p, st["half"][u]], lambda e, half=half, bk=bk: e.activation(
                    half, PS[:, bk, 0:256].rearrange("p (i s) -> p i s", i=2), ACT.Copy))
                bank["free"][bk] = [v]
                bk, fr = single()
                for i in range(2):
                    p = mm(PS[:, bk, i * 128:(i + 1) * 128], half[:, i, :], skv[:, i, :], True, True, [v, st["sk"], fr])
                st["half"][u] = [p]
                yield
                v = act([p, st["s"][u]], lambda e, u=u, bk=bk: e.activation(
                    S[:, u], PS[:, bk, 0:256].rearrange("p (i s) -> p i s", i=2), ACT.Copy))
                bank["free"][bk] = [v]
                yield from topk(t, h, S[:, u], v, tk)
            st["htf"][t] = [p]
            st["skf"] = [p]

        def heads_T1(dst, srcs, t, waits, free, scale):
            out = []
            for i in range(0, len(srcs), 4):
                part = srcs[i:i + 4]
                bk, fr = single()
                for j, a in enumerate(part):
                    dd = PS[0:64, bk, j * 128:(j + 1) * 128]
                    p = pe([waits, fr, t_cst], lambda e, a=a, dd=dd: e.transpose(dd, a, ident))
                v = evac(dst[0:64, i:i + len(part), t * 128:(t + 1) * 128],
                         PS[0:64, bk, 0:len(part) * 128].rearrange("p (j s) -> p j s", j=len(part)), [p, free], scale)
                bank["free"][bk] = [v]
                out.append(v)
            return out, p

        def vmax(dst, src, waits):
            return dve(waits, lambda e: e.max(dst, src))

        def vindex(dst, top, src, waits):
            return dve(waits, lambda e: e.max_index(dst, top, src))

        def vreplace(dst, top, src, waits):
            return dve(waits, lambda e: e.match_replace(dst, top, src, TINY))

        def topk(t, h, S, ready, tk):
            u = st["tn"] % 2
            st["tn"] += 1
            V, Ix = TV[:, u * 64:(u + 1) * 64], TI[:, u * 64:(u + 1) * 64]
            k = None
            for p in range(2):
                s, js = S[:, p, :], JS[:, p * 128:p * 128 + 128]
                v, ix = V[:, p * 16:p * 16 + 16], Ix[:, p * 16:p * 16 + 16]
                k = vmax(v[:, 0:8], s, [ready, st["tv"][u]])
                vindex(ix[:, 0:8], v[:, 0:8], s, [k])
                k = vreplace(js, v[:, 0:8], s, [k])
                k = vmax(v[:, 8:16], js, [k])
                k = vindex(ix[:, 8:16], v[:, 8:16], js, [k])
                yield LIGHT
            st["s"][h % 2] = [k]
            cd = TC[:, 0:256]
            cv = cd.rearrange("p (a b) -> p a b", a=16)
            k1 = tt(cv, bc(V[:, 0:16].unsqueeze(2), [128, 16, 16]), bc(V[:, 16:32].unsqueeze(1), [128, 16, 16]), ALU.add, [k])
            v, ix = V[:, 32:48], Ix[:, 32:48]
            k2 = vmax(v[:, 0:8], cd, [k1])
            k3 = vindex(ix[:, 0:8], v[:, 0:8], cd, [k2])
            k4 = vreplace(JS[:, 0:256], v[:, 0:8], cd, [k2])
            k5 = vmax(v[:, 8:16], JS[:, 0:256], [k4])
            k6 = vindex(ix[:, 8:16], v[:, 8:16], JS[:, 0:256], [k5])
            yield LIGHT
            j = (t * 8 + h) * 16
            ng = V[:, 48:49]
            n1 = ts(ng, v[:, 0:1], -1.0, None, ALU.mult, None, [k2])
            ga_ = GATE[:, j:j + 16]
            a = act([n1, k5, st["gate"][t]], lambda e: e.activation(ga_, v, ACT.Exp, bias=ng, scale=1.0, accum_out=V[:, 49:50]))
            q = ts(Ix[:, 48:64], ix, 4, None, ALU.logical_shift_right, None, [k6, k3])
            q2 = ts(ix, ix, 15, None, ALU.bitwise_and, None, [q])
            JF = JS[:, 256:288]
            c1 = dve([q], lambda e: e.tensor_copy(JF[:, 0:16], Ix[:, 48:64]))
            c2 = dve([q2], lambda e: e.tensor_copy(JF[:, 16:32], ix))
            c3 = dve([k], lambda e: e.tensor_copy(JS[:, 288:320], Ix[:, 0:32]))
            oh = JS[:, 512:1024].rearrange("p (a k m) -> p a k m", a=2, k=16)
            for z in range(2):
                c4 = tt(oh[:, z], bc(JF[:, z * 16:z * 16 + 16].unsqueeze(2), [128, 16, 16]),
                        bc(CST[:, C_IOTA:C_IOTA + 16].unsqueeze(1), [128, 16, 16]), ALU.is_equal, [c1, c2])
                c4 = tt(oh[:, z], oh[:, z], bc(JS[:, 288 + z * 16:304 + z * 16].unsqueeze(1), [128, 16, 16]),
                        ALU.mult, [c4, c3])
            sel = JS[:, 320:352]
            c5 = dve([c4], lambda e: e.reduce_sum(sel, JS[:, 512:1024].rearrange("p (k m) -> p k m", m=16), AX))
            eid = EID[:, j:j + 16]
            c6 = stt(eid, sel[:, 0:16], 128.0, sel[:, 16:32], ALU.mult, ALU.add, [c5, st["eid"][t]])
            r = dve([a], lambda e: e.reciprocal(V[:, 50:51], V[:, 49:50]))
            g = ts(ga_, ga_, V[:, 50:51], None, ALU.mult, None, [r])
            st["tv"][u] = [g]
            tk.append((c6, g))

        st.update(h2=[[], []], gate=[[], []], ada=[], modf=[], bf=[])

        def experts(l, t, tk, own, behind):
            owed, done = 0.0, 0
            j1 = t * 128
            pend = []

            def finish(its, j0):
                a = act([its[-1].dot], lambda e: e.activation(AV[:, j0:j0 + BATCH], AV[:, j0:j0 + BATCH], ACT.Gelu))
                k = tt(AV[:, j0:j0 + BATCH], AV[:, j0:j0 + BATCH], GATE[:, j0:j0 + BATCH], ALU.mult, [a, its[-1].tg])
                for q, x in enumerate(its):
                    d = st["dn"] % 4
                    st["dn"] += 1
                    jj = j0 + q
                    z = act([k, st["dg"][d], t_cst], lambda e, d=d, jj=jj: e.activation(
                        DG[:, d, :], ident, ACT.Copy, scale=AV[:, jj:jj + 1]))
                    for hf in range(2):
                        p = mm(PS[:, hf, :], DG[:, d, :], x.ap[:, 1024 + hf * 512:1536 + hf * 512],
                               jj == j1, jj == j1 + 127, [z, x.tok, bank["free"][hf]])
                    st["dg"][d] = [p]
                    x.release(p, x.dot)
                return k, p, x.tok

            for b in range(128 // BATCH):
                h = b * BATCH // 16
                while len(tk) <= h:
                    next(own)
                te, tg = tk[h]
                its = []
                for q in range(BATCH):
                    j = j1 + b * BATCH + q
                    it = Item()
                    it.tok = pool.dma([it.waits, te], lambda e, it=it, j=j: e.indirect_dma_start(
                        out=it.ap, out_offset=None, in_=I[f"uv{l}"],
                        in_offset=bass.IndirectOffsetOnAxis(ap=EID[:, j:j + 1], axis=0)), *it.count(ga[it.u]))
                    it.tg = tg
                    its.append(it)
                for q, x in enumerate(its):
                    j = j1 + b * BATCH + q
                    x.dot = dve([x.tok, st["h2"][t]], lambda e, x=x, j=j: e.tensor_tensor_reduce(
                        out=JD, in0=x.ap[:, 0:1024], in1=H[:, t, :], scale=1.0, scalar=0.0,
                        op0=ALU.mult, op1=ALU.add, accum_out=AV[:, j:j + 1]))
                pend.append((its, j1 + b * BATCH))
                if len(pend) > SKEW:
                    k, p, lt = finish(*pend.pop(0))
                if len(tk) < 8:
                    for _ in range(OWN):
                        advance(own)
                if len(tk) == 8:
                    run(own)
                if len(tk) == 8 and behind is not None:
                    owed += max(0.0, (STEPS - done) / max(1, 128 // BATCH - SPARE - b))
                    while owed >= 1:
                        owed -= 1
                        done += 1
                        advance(behind)
            while pend:
                k, p, lt = finish(*pend.pop(0))
            g2 = G2[:, l * 1024:(l + 1) * 1024]
            for hf in range(2):
                xs = X[:, t, hf * 512:(hf + 1) * 512]
                k2 = tt(JD[:, 0:512], PS[:, hf, :], g2[:, hf * 512:(hf + 1) * 512], ALU.mult, [p, st["ada"]])
                v = tt(xs, JD[:, 0:512], xs, ALU.add, [k2, st["x"][t]])
                bank["free"][hf] = [v]
            st["x"][t] = [v]
            st["hfree"][t] = [v]
            st["eid"][t], st["gate"][t] = [lt], [k]
            st["htf"][t] = st["htf"][t]

        JD2 = PRJ[:, 2048:2304]
        def rope(dst, src, n, half, tab, tmp, waits):
            cc = tab[:, 0:2 * half].rearrange("p (a b) -> p a b", a=2)
            ss = tab[:, 2 * half:4 * half].rearrange("p (a b) -> p a b", a=2)
            for z in range(2):
                c = bc(cc[:, z, :].unsqueeze(1), [128, n, half])
                k = tt(dst[:, :, z, :], src[:, :, z, :], c, ALU.mult, waits)
                s = bc(ss[:, z, :].unsqueeze(1), [128, n, half])
                k = tt(tmp[:, :, z, :], src[:, :, 1 - z, :], s, ALU.mult, waits)
            for z in range(2):
                k = tt(dst[:, :, z, :], dst[:, :, z, :], tmp[:, :, z, :], ALU.add, [k])
            return k

        def block2(l, tp):
            c = lambda k: PARB[:, P2[k][0]:P2[k][0] + P2[k][1]]
            lam0 = 0.8 - 0.6 * math.exp(-0.3 * l)
            prj = MOD[:, 0:4800].rearrange("p (t n) -> p t n", t=2)
            hts = [norm(t, c("n1"), [tp]) for t in range(2)]
            pj = [[], []]
            for j in range(10):
                w = load(I["win2"][l * 10 + j], 1920)
                for t in range(2):
                    bk, fr = single()
                    p = tokens_by(HT, w, 240, t, 8, hts[t], fr, bk)
                    v = evac(prj[:, t, j * 240:(j + 1) * 240], PS[:, bk, 0:240], [p, st["mod"]])
                    bank["free"][bk] = [v]
                    pj[t].append(v)
                w.release(p)
            st["ht"] = [[p], [p]]
            Y = H
            st["yfree"] = [st["h"][0], st["h"][1]]
            A = QK[:, 0:2048].rearrange("p (i s) -> p i s", i=8)
            B = QK[:, 2048:6144].rearrange("p (i s) -> p i s", i=16)
            rp = lambda t: CST[:, C_ROPE + t * 192:C_ROPE + (t + 1) * 192]
            ls = scratch(8)
            for z in range(2):
                lq = c("lam")[:, z * 64:z * 64 + 32]
                lk = c("lam")[:, z * 64 + 32:z * 64 + 64]
                k = dve([tp, st["prj"]], lambda e, lq=lq, lk=lk, z=z: e.tensor_tensor_reduce(
                    out=JD2[:, 0:32], in0=lq, in1=lk, scale=1.0, scalar=0.0, op0=ALU.mult, op1=ALU.add,
                    accum_out=ls[:, z:z + 1]))
            k = act([k], lambda e: e.activation(ls[:, 2:4], ls[:, 0:2], ACT.Exp))
            tlam = stt(ls[:, 4:5], ls[:, 2:3], lam0, ls[:, 3:4], ALU.add, ALU.subtract, [k])
            lam = ls[:, 4:5]
            wu = load(I["wuq"][l], 768)
            ct = Item()
            wk = load(I["wukv"][l], 512)
            KVB = PRJ[:, 0:1024].rearrange("p (t n) -> p t n", t=2)
            QF = PRJ[:, 1024:1792].rearrange("p (t n) -> p t n", t=2)
            TMP = PRJ[:, 1792:2560]
            tmpf = st["prj"]
            kv_t, qd = [], []
            lastqk = []
            for t in range(2):
                s, tr = rstd([prj[:, t, X_CQ:X_CQ + 192]], 192.0, [[pj[t]]])
                k1 = stt(prj[:, t, X_CQ:X_CQ + 192], prj[:, t, X_CQ:X_CQ + 192], s[:, 0:1], c("q"), ALU.mult, ALU.mult,
                         [tr, tp])
                s2, tr2 = rstd([prj[:, t, X_CKV:X_CKV + 128]], 128.0, [[pj[t]]])
                k2 = stt(prj[:, t, X_CKV:X_CKV + 128], prj[:, t, X_CKV:X_CKV + 128], s2[:, 0:1], c("kv"), ALU.mult,
                         ALU.mult, [tr2, tp])
                bk, fr = single()
                for (dd, a) in ((PS[:, bk, 0:128], prj[:, t, 0:128]), (PS[0:64, bk, 128:256], prj[:, t, 128:192]),
                                (PS[:, bk, 256:384], prj[:, t, X_CKV:X_CKV + 128])):
                    p = pe([k1, k2, fr, t_cst], lambda e, dd=dd, a=a: e.transpose(dd, a, ident))
                CT = ct.ap[:, t * 384:(t + 1) * 384]
                v1 = act([p, ct.waits], lambda e, CT=CT, bk=bk: e.activation(CT[:, 0:128], PS[:, bk, 0:128], ACT.Copy))
                v2 = act([v1], lambda e, CT=CT, bk=bk: e.activation(CT[0:64, 128:256], PS[0:64, bk, 128:256], ACT.Copy))
                v3 = act([v2], lambda e, CT=CT, bk=bk: e.activation(CT[:, 256:384], PS[:, bk, 256:384], ACT.Copy))
                bank["free"][bk] = [v1, v2, v3]
                wuv = wu.ap.rearrange("p (k n) -> p k n", k=2)
                bk, fr = single()
                mm(PS[:, bk, 0:384], CT[:, 0:128], wuv[:, 0, :], True, False, [v1, v2, v3, wu.tok, fr])
                pq = mm(PS[:, bk, 0:384], CT[0:64, 128:256], wuv[0:64, 1, :], False, True)
                kq = dve([pq, tmpf], lambda e, t=t, bk=bk: e.tensor_copy(QF[:, t, :], PS[:, bk, 0:384]))
                bank["free"][bk] = [kq]
                bk, fr = single()
                pk = mm(PS[:, bk, :], CT[:, 256:384], wk.ap, True, True, [wk.tok, fr])
                kk_ = act([pk, tmpf], lambda e, t=t, bk=bk: e.activation(KVB[:, t, :], PS[:, bk, :], ACT.Copy))
                bank["free"][bk] = [kk_]
                tab = rp(t)[:, 0:64]
                qv = QF[:, t, :].rearrange("p (i d) -> p i d", i=4)
                RQ = TMP[:, 0:128].rearrange("p (i d) -> p i d", i=4)
                kr_ = rope(RQ.rearrange("p i (a b) -> p i a b", a=2), qv[:, :, 64:96].rearrange("p i (a b) -> p i a b", a=2),
                           4, 16, tab, TMP[:, 128:256].rearrange("p (i a b) -> p i a b", i=4, a=2), [kq, t_cst, lastqk])
                kq2 = dve([kr_], lambda e, qv=qv, RQ=RQ: e.tensor_copy(qv[:, :, 64:96], RQ))
                RK = TMP[:, 256:288]
                kr2 = rope(RK.rearrange("p (i a b) -> p i a b", i=1, a=2),
                           prj[:, t, X_KR:X_KR + 32].rearrange("p (i a b) -> p i a b", i=1, a=2), 1, 16, tab,
                           TMP[:, 288:320].rearrange("p (i a b) -> p i a b", i=1, a=2), [pj[t], t_cst])
                KF = TMP[:, 320:704].rearrange("p (i d) -> p i d", i=4)
                kf1 = dve([kk_], lambda e, t=t, KF=KF: e.tensor_copy(
                    KF[:, :, 0:64], KVB[:, t, 0:256].rearrange("p (i d) -> p i d", i=4)))
                kf2 = dve([kr2], lambda e, KF=KF, RK=RK: e.tensor_copy(KF[:, :, 64:96], bc(RK.unsqueeze(1), [128, 4, 32])))
                a1, _ = heads_T(A[:, 0:4, :], [qv[:, i, :] for i in range(4)], 96, t, [kq2], st["qa"])
                a2, p2 = heads_T(A[:, 4:8, :], [KF[:, i, :] for i in range(4)], 96, t, [kf1, kf2], st["qa"])
                lastqk = [p2]
                qd += a1 + a2
                kv_t.append(kk_)
            wu.release(pq)
            wk.release(pk)
            ct.release(pk)
            latent, diff, window, near = [], [], [], []
            gm = []
            for t in range(2):
                maps = [(A[0:96, i, t * 128:(t + 1) * 128], A[0:96, 4 + i, :],
                         lambda kc, i=i: KVB[:, kc, 256 + i * 64:256 + (i + 1) * 64]) for i in range(4)]
                gm.append(group(t, maps, 256, 96.0 ** -0.5, [qd, kv_t], Y, 0, latent))
            RB = PRJ[:, 1024:1536]
            RT = PRJ[:, 1536:2048]
            prev = p2
            qdd = []
            for t in range(2):
                v = prj[:, t, X_BQ:X_BQ + 512].rearrange("p (i a b) -> p i a b", i=16, a=2)
                k = rope(RB.rearrange("p (i a b) -> p i a b", i=16, a=2), v, 16, 16, rp(t)[:, 0:64],
                         RT.rearrange("p (i a b) -> p i a b", i=16, a=2), [pj[t], prev])
                a, prev = heads_T(B, [RB[:, i * 32:(i + 1) * 32] for i in range(16)], 32, t, [k], [st["qb"], st["plf"]])
                qdd += a
            gd = []
            for t in range(2):
                for hg in range(2):
                    maps = [(B[0:32, hg * 4 + i, t * 128:(t + 1) * 128], B[0:32, 8 + hg * 4 + i, :],
                             lambda kc, i=i, hg=hg: prj[:, kc, X_BV + (hg * 2 + i // 2) * 64:X_BV + (hg * 2 + i // 2 + 1) * 64])
                            for i in range(4)]
                    gd.append(group(t, maps, 256, 32.0 ** -0.5, [qdd, tlam], Y, 256 + hg * 128, diff, lam=lam))
            qs, qn = [], []

            def window_heads():
                pv = prev
                for t in range(2):
                    v = prj[:, t, X_SQ:X_SQ + 384].rearrange("p (i a b) -> p i a b", i=6, a=2)
                    k = rope(RB[:, 0:384].rearrange("p (i a b) -> p i a b", i=6, a=2), v, 6, 32, rp(t)[:, 64:192],
                             RT[:, 0:384].rearrange("p (i a b) -> p i a b", i=6, a=2), [pj[t], pv])
                    yield
                    fr = [w for _, w in latent]
                    a, pv = heads_T(A[:, 0:4, :], [RB[:, i * 64:(i + 1) * 64] for i in range(4)], 64, t, [k], fr, 0.125)
                    b, pv = heads_T(A[:, 4:6, :], [RB[:, i * 64:(i + 1) * 64] for i in range(4, 6)], 64, t, [k], fr)
                    qs.extend(a + b)
                st["prj"] = [pv]

            gw = []
            for t in range(2):
                sm = CST[:, C_SM + t * 256:C_SM + (t + 1) * 256]

                def bias(P, sc, waits, sm=sm):
                    return tt(P, sc, bc(sm.unsqueeze(1), [128, 4, 256]), ALU.add, [waits, st["smw"]])
                maps = [(A[0:64, i, t * 128:(t + 1) * 128], A[0:64, 4 + i // 2, :],
                         lambda kc, i=i: prj[:, kc, X_SV + (i // 2) * 64:X_SV + (i // 2 + 1) * 64]) for i in range(4)]
                gw.append(group(t, maps, 256, 1.0, qs, Y, 512, window, bias=bias, sink=c("sink")))

            def near_heads():
                fr = [w for _, w in diff]
                for t in range(2):
                    a, _ = heads_T(B[:, 0:4, :], [prj[:, t, X_NQ + i * 64:X_NQ + (i + 1) * 64] for i in range(4)], 64, t,
                                   [pj[t]], fr, 0.125)
                    b, _ = heads_T(B[:, 4:8, :], [prj[:, t, X_NK + i * 64:X_NK + (i + 1) * 64] for i in range(4)], 64, t,
                                   [pj[t]], fr)
                    qn.extend(a + b)
                    yield

            gn = []
            for t in range(2):
                def bias(P, sc, waits, t=t):
                    nb = load(I["nab"][l * 2 + t], 1024)
                    k = tt(P, sc, nb.ap.rearrange("p (i k) -> p i k", i=4), ALU.add, [waits, nb.tok])
                    nb.release(k)
                    return k
                maps = [(B[0:64, i, t * 128:(t + 1) * 128], B[0:64, 4 + i, :],
                         lambda kc, i=i: prj[:, kc, X_NV + i * 64:X_NV + (i + 1) * 64]) for i in range(4)]
                gn.append(group(t, maps, 256, 1.0, qn, Y, 768, near, bias=bias))
            gw = [after(lambda: len(qs) >= 4, g) for g in gw]
            gn = [after(lambda: len(qn) >= 4, g) for g in gn]
            run(overlapped([*gm, gd[0], gd[1], gd[2], after(lambda: len(latent) == 2, window_heads()), gd[3], gw[0],
                            after(lambda: len(diff) == 4, near_heads()), gw[1], *gn], WIDE))
            last = [w for r in (latent, diff, window, near) for _, w in r]
            st["qa"], st["qb"], st["plf"], st["mod"] = last, last, [], last
            st["prj"] = st["prj"] + last
            ym = [[v for r in (latent, diff, window, near) for v, _ in r]] * 2
            wo = [load(I["wout2"][l * 4 + j], 2048) for j in range(4)]
            hts = []

            def outputs(t):
                s, tr = rstd([Y[:, t, o:o + 256] for o in (0, 512, 768)], 256.0, [ym[t]] * 3)
                yb = Y[:, t, 256:512].rearrange("p (i d) -> p i d", i=4)
                jb = JD2[:, 0:256].rearrange("p (i d) -> p i d", i=4)
                k2 = tt(jb, yb, yb, ALU.mult, [ym[t], st["prj"]])
                q = scratch(4)
                k2 = dve([k2], lambda e: e.reduce_sum(q, jb, AX))
                k2 = act([k2], lambda e: e.activation(q, q, ACT.Sqrt, bias=EPSC, scale=1.0 / 64))
                for i, (o, g) in enumerate(((0, "oa"), (512, "oc"), (768, "od"))):
                    yy = Y[:, t, o:o + 256]
                    k = stt(yy, yy, s[:, i:i + 1], c(g), ALU.mult, ALU.mult, [tr, tp])
                k2 = dve([k2], lambda e: e.reciprocal(q, q))
                k2 = tt(yb, yb, bc(q.unsqueeze(2), [128, 4, 64]), ALU.mult, [k2])
                k2 = stt(yb, yb, 1.0 - lam0, bc(c("sub").unsqueeze(1), [128, 4, 64]), ALU.mult, ALU.mult, [k2])
                return transpose_tm(t, [k, k2], st["ht"][t])

            yts = [outputs(t) for t in range(2)]
            for t in range(2):
                residual(t, wo, HT, yts[t])
                hts.append(norm(t, c("n2"), [tp]))
            st["par"] = hts
            AT = QK[:, 2048:3072].rearrange("p (b i s) -> p b i s", b=2, i=2)
            atf = [st["qb"], st["qb"]]
            last = None

            def down(b, at, wd):
                for t in range(2):
                    for hf in range(2):
                        for i in range(2):
                            p = mm(PS[:, t * 2 + hf, :], AT[:, b % 2, i, t * 128:(t + 1) * 128],
                                   wd.ap[:, i * 1024 + hf * 512:i * 1024 + (hf + 1) * 512], b == 0 and i == 0,
                                   b == 15 and i == 1, [at, wd.tok, bank["free"][t * 2 + hf]])
                wd.release(p)
                atf[b % 2] = [p]
                return p

            pend = None
            for b in range(16):
                w = load(I["wup"][l * 16 + b], 2048)
                wd = load(I["wdn"][l * 16 + b], 2048)
                wv = w.ap.rearrange("p (k n) -> p k n", k=8)
                bk, fr = single()
                for t in (range(2) if b < 2 else (None,)):
                    cols = slice(0, 256) if t is None else slice(t * 128, (t + 1) * 128)
                    for i in range(2):
                        for k in range(8):
                            p = mm(PS[:, bk, i * 256 + cols.start:i * 256 + cols.stop], wv[:, k, i * 128:(i + 1) * 128],
                                   HT[:, k, cols], k == 0, k == 7, [w.tok, hts if t is None else hts[t], fr])
                pv = PS[:, bk, :].rearrange("p (i s) -> p i s", i=2)
                dst = AT[:, b % 2, :, :]
                r1 = act([p, atf[b % 2]], lambda e, dst=dst, pv=pv: e.activation(dst, pv, ACT.Relu))
                at = tt(dst, dst, dst, ALU.mult, [r1])
                bank["free"][bk] = [r1]
                w.release(p)
                st["ht"] = [[p], [p]]
                if pend is not None:
                    down(*pend)
                pend = (b, at, wd)
            p = down(*pend)
            st["qb"] = [p]
            for t in range(2):
                for hf in range(2):
                    xs = X[:, t, hf * 512:(hf + 1) * 512]
                    v = tt(xs, PS[:, t * 2 + hf, :], xs, ALU.add, [p, st["x"][t]])
                    bank["free"][t * 2 + hf] = [v]
                st["x"][t] = [v]

        heads = {(l, t): [] for l in range(L) for t in range(2)}
        order = [(l, t) for l in range(L) for t in range(2)]
        gens = {k: mix(*k, heads[k]) for k in order}

        def modulations():
            yield from ada(0)
            yield from ada(1)

        both = modulations()
        own = gens[(0, 0)]
        while not heads[(0, 0)]:
            next(own)
            for _ in range(MODS):
                next(both, None)
        run(both)
        st["dg"] = [st["acc"][0] + st["acc"][1]] * 4
        for i, k in enumerate(order):
            behind = gens[order[i + 1]] if i + 1 < 4 else None
            experts(*k, heads[k], gens[k], behind)
            run(gens[k])
        st["qa"] = st["qt"] + st["kt"] + st["pl"]
        st["qb"] = st["x"][1] + st["half"][0] + st["half"][1]
        st["mod"] = st["x"][0] + st["x"][1]
        st["h"] = [st["x"][0] + st["htf"][0], st["x"][1]]
        st["ht"] = [st["htf"][0], st["htf"][1]]
        st["par"] = st["x"][0] + st["x"][1]
        st["plf"] = []
        bank["pairs"] = (0, 2)
        t_sm = sp.dma([st["x"]], lambda e: e.dma_start(CST[:, C_SM:C_SM + 512], I["sm"]), s_sm, 16)
        JVS[0] = ACC.rearrange("p b n -> p (b n)")
        st["jv"], st["smw"] = [st["bf"], st["acc"]], [t_sm]
        for l in range(L):
            tp = load_par(I["par2"][l], 3332)
            block2(l, tp)
        tp = load_par(I["fing"], 1024)
        s, tr = rstd([X[:, 0, :], X[:, 1, :]], 1024.0, st["x"])
        for t in range(2):
            k = stt(X[:, t, :], X[:, t, :], s[:, t:t + 1], PARB[:, 0:1024], ALU.mult, ALU.mult, [tr, tp])
            st["x"][t] = [k]
        ov = out.rearrange("(t p) d -> p t d", p=128)
        t_o = sp.dma([st["x"]], lambda e: e.dma_start(ov, X), s_out, 16)
        sp([t_o], lambda e: e.nop())

        for e in (pe, act, dve, pool, sp):
            e.number()
        block = ctx.enter_context(nc.Block())

        @block.sync
        def _(e):
            sp.emit(e)

        @block.gpsimd
        def _(e):
            pool.emit(e)

        @block.scalar
        def _(e):
            act.emit(e)

        @block.vector
        def _(e):
            dve.emit(e)

        @block.tensor
        def _(e):
            pe.emit(e)


def constants():
    f = np.float32
    cst = np.zeros((128, C_END), f)
    cst[:, C_ID:C_ID + 128] = np.eye(128, dtype=f)
    pos = np.arange(256)
    q = pos.reshape(2, 128)
    d = q[:, :, None] - pos[None, None, :]
    nd = np.where((d >= 0) & (d < 128), -d.astype(f), f(-1e30))
    cst[:, C_ND:C_ND + 512] = nd.transpose(1, 0, 2).reshape(128, 512)
    sm = np.where(np.abs(d) <= 128, f(0), f(-1e30))
    tabs = []
    for dim in (32, 64):
        inv = (f(1.0) / (f(10000.0) ** (np.arange(0, dim, 2, dtype=f) / f(dim)))).astype(f)
        ang = (np.arange(256, dtype=f)[:, None] * inv[None, :]).astype(f)
        c, s = np.cos(ang).astype(f), np.sin(ang).astype(f)
        tabs += [c, c, -s, s]
    tab = np.concatenate(tabs, axis=1)
    cst[:, C_ROPE:C_ROPE + 384] = tab.reshape(2, 128, 192).transpose(1, 0, 2).reshape(128, 384)
    cst[:, C_IOTA:C_IOTA + 16] = np.arange(16, dtype=f)
    mg = np.zeros((4, 256, 256), f)
    for g, w in enumerate((2, 4, 8, 16)):
        dd = pos[None, :] - pos[:, None]
        mg[g] = np.where((dd >= 0) & (dd < w), f(1) / np.minimum(pos + 1, w).astype(f)[None, :], f(0))
        mg[g] -= np.eye(256, dtype=f)
    mg = mg.reshape(4, 2, 128, 2, 128).transpose(3, 2, 1, 0, 4)
    return cst, mg, sm.transpose(1, 0, 2).reshape(128, 512)


def layout(v):
    f = np.float32
    a = {k: np.asarray(x) for k, x in v.items()}

    def cols(w, n):
        l_, k, m = w.shape
        w = w.reshape(l_, k // 128, 128, m // n, n).transpose(0, 3, 2, 1, 4)
        return np.ascontiguousarray(w).reshape(l_ * (m // n), 128, (k // 128) * n)

    cst, mg, sm = constants()
    o = {"cst": cst, "sm": np.ascontiguousarray(sm.astype(f))}
    o["x"] = a["x"].reshape(256, 1024)
    o["mg0"], o["mg1"] = mg[0, :, 0:1].reshape(128, 512), mg[1].reshape(128, 1024)
    o["cT"] = np.ascontiguousarray(a["c"].reshape(8, 128).T)
    o["wada"] = cols(a["w_ada"], 256)
    o["bada"] = a["b_ada"]
    par = np.concatenate([a["norm1_g"], a["norm2_g"], a["pool_scale"], a["q_norm_g"], a["k_norm_g"], a["attn_sinks"],
                          a["mix_norm_g"]], axis=1)
    o["par1"] = par
    o["win1"] = cols(a["w_in"], 256)
    o["poolw"] = np.ascontiguousarray(a["pool_w"].transpose(0, 2, 1, 3)).reshape(L, 128, 512)
    o["wout1"] = cols(a["w_out"], 256)
    o["wq"] = cols(a["peer_wq"], 256)
    o["skT"] = np.ascontiguousarray(a["peer_subkeys"].transpose(0, 3, 1, 2)).reshape(L, 128, 256)
    for l in range(L):
        o[f"uv{l}"] = np.concatenate([a["peer_u"][l], a["peer_v"][l]], axis=1)
    o["par2"] = np.concatenate([a["norm1_g_2"], a["norm2_g_2"], a["mla_q_norm_g_2"], a["mla_kv_norm_g_2"],
                                a["diff_lambda_q1_2"], a["diff_lambda_k1_2"], a["diff_lambda_q2_2"], a["diff_lambda_k2_2"],
                                a["diff_subln_g_2"], a["swa_sinks_2"], a["out_g_mla_2"], a["out_g_swa_2"],
                                a["out_g_na_2"]], axis=1)
    o["fing"] = a["final_norm_g_2"]
    o["win2"] = cols(a["w_in_2"], 240)
    wuq = np.zeros((L, 256, 384), f)
    wuq[:, 0:192] = a["mla_w_uq_2"]
    o["wuq"] = np.ascontiguousarray(wuq.reshape(L, 2, 128, 384).transpose(0, 2, 1, 3)).reshape(L, 128, 768)
    o["wukv"] = np.concatenate([a["mla_w_uk_2"], a["mla_w_uv_2"]], axis=2)
    pos = np.arange(256)
    r, c = pos // 64, pos % 64
    start = np.clip(c - 8, 0, 48)
    inside = (c[None, :] >= start[:, None]) & (c[None, :] < start[:, None] + 16)
    ri = r[None, :] - r[:, None] + 7
    ci = np.clip(c[None, :] - c[:, None] + 15, 0, 30)
    nab = np.where(inside[None, None], a["na_rpb_2"][:, :, ri, ci], f(-1e30)).astype(f)
    o["nab"] = np.ascontiguousarray(nab.reshape(L, 4, 2, 128, 256).transpose(0, 2, 3, 1, 4)).reshape(L * 2, 128, 1024)
    o["wout2"] = cols(a["w_out_2"], 256)
    o["wup"] = cols(a["w_up_2"], 256)
    wd = a["w_down_2"].reshape(L, 16, 2, 128, 1024).transpose(0, 1, 3, 2, 4)
    o["wdn"] = np.ascontiguousarray(wd).reshape(L * 16, 128, 2048)
    return {k: np.ascontiguousarray(x) for k, x in o.items()}


def declare(nc, arrays):
    I = {k: nc.dram_tensor("in_" + k, a.shape, mybir.dt.from_np(a.dtype), kind="ExternalInput").ap()
         for k, a in arrays.items()}
    I["modd"] = nc.dram_tensor("modd", (1, 6144), F32).ap()
    out = nc.dram_tensor("out_x", (256, 1024), F32, kind="ExternalOutput").ap()
    build(nc, I, out)


def kernel(**inputs):
    import concourse.bacc as _bacc
    from concourse.bass_utils import run_bass_kernel_spmd as _run

    arrays = layout(inputs)
    nc = _bacc.Bacc("TRN2", target_bir_lowering=False, num_devices=1)
    declare(nc, arrays)
    r = _run(nc, [{"in_" + k: a for k, a in arrays.items()}], core_ids=[0])
    return r.results[0]["out_x"].reshape(1, 256, 1024)
```
